# Optimizing a Trainium2 kernel written in Bass

```python
import numpy as np
import jax
import jax.numpy as jnp
from jax import lax

D_MODEL = 1024
BATCH = 1
SEQ = 1024
DEPTH = 1

HEAD_DIM = 64
BLK = 128
CONV_CH = D_MODEL // 4
CONV_K = 31
SWA_HEADS = 4
SWA_KV_HEADS = 2
SWA_WINDOW = 128
RET_HEADS = 4
RET_QK = 64
RET_V = 128
NSA_HEADS = 4
NSA_CMP_LEN = 32
NSA_CMP_STRIDE = 16
NSA_CMP_HIDDEN = 256
NSA_SLC_LEN = 64
NSA_TOPN = 8
NSA_WINDOW = 512
NSA_FORCE = 1e4
N_EXPERTS = 64
TOP_K = 6
N_GROUPS = 8
TOPK_GROUPS = 4
D_EXPERT = D_MODEL // 4
ROUTE_SCALE = 2.5
MOE_BLK = 128
N_BRANCH = 4
ALPHA = (2 * DEPTH) ** 0.25
BETA = (8 * DEPTH) ** -0.25
LN_EPS = 1e-5
NEG_INF = -1e30

IN_WIDTHS = (
    2 * CONV_CH,
    SWA_HEADS * HEAD_DIM, SWA_KV_HEADS * HEAD_DIM, SWA_KV_HEADS * HEAD_DIM,
    RET_HEADS * RET_QK, RET_HEADS * RET_QK, RET_HEADS * RET_V, RET_HEADS * RET_V,
    NSA_HEADS * HEAD_DIM,
    HEAD_DIM, HEAD_DIM, HEAD_DIM, HEAD_DIM, HEAD_DIM, HEAD_DIM,
    3 * NSA_HEADS,
    N_BRANCH * D_MODEL,
)

kernel_name = 'hybrid_conv_swa_retention_nsa_moe_deepnorm'

def layer_norm(x, g, b):
    xf = x.astype(jnp.float32)
    mu = jnp.mean(xf, -1, keepdims=True)
    var = jnp.mean(jnp.square(xf - mu), -1, keepdims=True)
    return ((xf - mu) * lax.rsqrt(var + LN_EPS) * g + b).astype(x.dtype)

def alibi_slopes(n):
    return jnp.asarray([2.0 ** (-8.0 * (i + 1) / n) for i in range(n)], jnp.float32)

def masked_softmax(s, mask, sink=None):
    s = jnp.where(mask, s, NEG_INF)
    m = jnp.max(s, axis=-1, keepdims=True)
    if sink is not None:
        m = jnp.maximum(m, sink)
    e = jnp.where(mask, jnp.exp(s - m), 0.0)
    den = jnp.sum(e, -1, keepdims=True)
    if sink is not None:
        den = den + jnp.exp(sink - m)
    return e / jnp.maximum(den, 1e-30)

def banded_attention(q, k, v, slopes, window, sink=None):
    b, hq, s, dh = q.shape
    hkv = k.shape[1]
    rep = hq // hkv
    nb = s // BLK
    nprev = window // BLK

    def spans(t):
        tb = jnp.pad(t.reshape(b, hkv, nb, BLK, dh), ((0, 0), (0, 0), (nprev, 0), (0, 0), (0, 0)))
        return jnp.concatenate([tb[:, :, w:w + nb] for w in range(nprev + 1)], axis=3)

    ks, vs = spans(k), spans(v)
    qb = q.reshape(b, hkv, rep, nb, BLK, dh)
    sc = jnp.einsum('bgrnqd,bgnkd->bgrnqk', qb, ks, preferred_element_type=jnp.float32) * (dh ** -0.5)
    qpos = jnp.arange(nb)[:, None] * BLK + jnp.arange(BLK)[None, :]
    kpos = (jnp.arange(nb)[:, None] - nprev) * BLK + jnp.arange((nprev + 1) * BLK)[None, :]
    dist = qpos[:, :, None] - kpos[:, None, :]
    mask = (dist >= 0) & (dist < window) & (kpos[:, None, :] >= 0)
    sc = sc - slopes.reshape(1, hkv, rep, 1, 1, 1) * dist.astype(jnp.float32)
    sink_b = None if sink is None else sink.astype(jnp.float32).reshape(1, hkv, rep, 1, 1, 1)
    p = masked_softmax(sc, mask, sink_b)
    o = jnp.einsum('bgrnqk,bgnkd->bgrnqd', p.astype(v.dtype), vs)
    return o.reshape(b, hq, s, dh)

def conformer_conv(u, dw, db, g, b):
    a, gate = jnp.split(u, 2, axis=-1)
    h = a * jax.nn.sigmoid(gate)
    c = h.shape[-1]
    hp = jnp.pad(h, ((0, 0), (CONV_K - 1, 0), (0, 0)))
    y = lax.conv_general_dilated(hp, dw[:, None, :], window_strides=(1,), padding='VALID',
                                 dimension_numbers=('NWC', 'WIO', 'NWC'), feature_group_count=c) + db
    return jax.nn.silu(layer_norm(y, g, b))

def retention(q, k, v, g, gn_g, gn_b):
    b, s, _ = q.shape
    nc = s // BLK
    f32 = jnp.float32

    def heads(t, d):
        return t.reshape(b, nc, BLK, RET_HEADS, d).transpose(0, 3, 1, 2, 4).astype(f32)

    qh = heads(q, RET_QK)
    kh = heads(k, RET_QK) * (RET_QK ** -0.5)
    vh = heads(v, RET_V)
    log_gamma = jnp.log1p(-(2.0 ** (-5.0 - jnp.arange(RET_HEADS, dtype=f32))))
    idx = jnp.arange(BLK, dtype=f32)
    diff = idx[:, None] - idx[None, :]
    dmat = jnp.where(diff >= 0, jnp.exp(log_gamma[:, None, None] * jnp.maximum(diff, 0.0)), 0.0)
    inner = jnp.einsum('bhnqd,bhnkd->bhnqk', qh, kh) * dmat[None, :, None]
    o_inner = jnp.einsum('bhnqk,bhnkd->bhnqd', inner, vh)
    zeta = jnp.exp(log_gamma[:, None] * (BLK - 1 - idx)[None, :])
    xi = jnp.exp(log_gamma[:, None] * (idx + 1.0)[None, :])
    chunk_decay = jnp.exp(log_gamma * BLK)
    kv = jnp.einsum('bhnsd,bhnse->bhnde', kh * zeta[None, :, None, :, None], vh)

    def step(state, kv_c):
        return chunk_decay[None, :, None, None] * state + kv_c, state

    init = jnp.zeros((b, RET_HEADS, RET_QK, RET_V), f32)
    _, prev = lax.scan(step, init, jnp.moveaxis(kv, 2, 0))
    prev = jnp.moveaxis(prev, 0, 2)
    o_cross = jnp.einsum('bhnqd,bhnde->bhnqe', qh, prev) * xi[None, :, None, :, None]
    o = o_inner + o_cross
    mu = jnp.mean(o, -1, keepdims=True)
    var = jnp.mean(jnp.square(o - mu), -1, keepdims=True)
    o = (o - mu) * lax.rsqrt(var + LN_EPS)
    o = o.transpose(0, 2, 3, 1, 4).reshape(b, s, RET_HEADS * RET_V) * gn_g + gn_b
    return (jax.nn.silu(g.astype(f32)) * o).astype(g.dtype)

def native_sparse_attention(q, kc, vc, ks, vs, kw, vw, gates, slopes,
                            pe_k, w1_k, w2_k, pe_v, w1_v, w2_v):
    b, s, _ = q.shape
    dh = HEAD_DIM
    f32 = jnp.float32
    qh = q.reshape(b, s, NSA_HEADS, dh).transpose(0, 2, 1, 3)
    tpos = jnp.arange(s)

    def compress(t, pe, w1, w2):
        tc = t.reshape(b, s // NSA_CMP_STRIDE, NSA_CMP_STRIDE, dh)
        blocks = jnp.concatenate([tc[:, :-1], tc[:, 1:]], axis=2) + pe
        flat = blocks.reshape(b, blocks.shape[1], NSA_CMP_LEN * dh)
        return jax.nn.gelu(flat @ w1, approximate=False) @ w2

    kcmp = compress(kc, pe_k, w1_k, w2_k)
    vcmp = compress(vc, pe_v, w1_v, w2_v)
    ncmp = kcmp.shape[1]
    cstart = jnp.arange(ncmp) * NSA_CMP_STRIDE
    cdist = tpos[:, None] - (cstart + NSA_CMP_LEN - 1)[None, :]
    sc = jnp.einsum('bhtd,bcd->bhtc', qh, kcmp, preferred_element_type=f32) * (dh ** -0.5)
    sc = sc - slopes[:, None, None] * cdist.astype(f32)
    p_cmp = masked_softmax(sc, cdist >= 0)
    o_cmp = jnp.einsum('bhtc,bcd->bhtd', p_cmp.astype(vcmp.dtype), vcmp)

    nslc = s // NSA_SLC_LEN
    sstart = jnp.arange(nslc) * NSA_SLC_LEN
    overlap = ((cstart[:, None] < sstart[None, :] + NSA_SLC_LEN)
               & (cstart[:, None] + NSA_CMP_LEN > sstart[None, :])).astype(f32)
    imp = jnp.einsum('bhtc,cj->btj', p_cmp, overlap)
    cur = tpos // NSA_SLC_LEN
    jj = jnp.arange(nslc)
    forced = (jj[None, :] == 0) | (jj[None, :] == cur[:, None]) | (jj[None, :] == cur[:, None] - 1)
    future = jj[None, :] > cur[:, None]
    imp = jnp.where(forced, NSA_FORCE, jnp.where(future, -1.0, imp))
    _, sel = lax.top_k(imp, min(NSA_TOPN, nslc))

    kb = ks.reshape(b, nslc, NSA_SLC_LEN, dh)
    vb = vs.reshape(b, nslc, NSA_SLC_LEN, dh)
    nq = s // BLK
    take = jax.vmap(lambda t, i: t[i])

    def sel_block(args):
        q_blk, idx_blk, t_blk = args
        k_sel = take(kb, idx_blk)
        v_sel = take(vb, idx_blk)
        kpos = idx_blk[..., None] * NSA_SLC_LEN + jnp.arange(NSA_SLC_LEN)
        dist = t_blk[None, :, None, None] - kpos
        sc_s = jnp.einsum('bhqd,bqnld->bhqnl', q_blk, k_sel, preferred_element_type=f32) * (dh ** -0.5)
        sc_s = sc_s - slopes[None, :, None, None, None] * dist[:, None].astype(f32)
        p = masked_softmax(sc_s.reshape(b, NSA_HEADS, BLK, -1), (dist >= 0).reshape(b, 1, BLK, -1))
        return jnp.einsum('bhqm,bqmd->bhqd', p.astype(v_sel.dtype), v_sel.reshape(b, BLK, -1, dh))

    xs = (jnp.moveaxis(qh.reshape(b, NSA_HEADS, nq, BLK, dh), 2, 0),
          jnp.moveaxis(sel.reshape(b, nq, BLK, -1), 1, 0),
          tpos.reshape(nq, BLK))
    o_slc = jnp.moveaxis(lax.map(sel_block, xs), 0, 2).reshape(b, NSA_HEADS, s, dh)

    o_win = banded_attention(qh, kw[:, None], vw[:, None], slopes, NSA_WINDOW)

    gt = jax.nn.sigmoid(gates.astype(f32)).reshape(b, s, 3, NSA_HEADS).transpose(2, 0, 3, 1)[..., None]
    o = gt[0] * o_cmp + gt[1] * o_slc + gt[2] * o_win
    return o.transpose(0, 2, 1, 3).reshape(b, s, NSA_HEADS * dh).astype(q.dtype)

def token_mixer(x, w_in, conv_dw, conv_db, conv_ln_g, conv_ln_b, swa_sink, ret_gn_g, ret_gn_b,
                nsa_pe_k, nsa_w1_k, nsa_w2_k, nsa_pe_v, nsa_w1_v, nsa_w2_v,
                p_conv, p_swa, p_ret, p_nsa, w_out, slopes_swa, slopes_nsa):
    b, s, d = x.shape
    u = x @ w_in
    (conv_in, swa_q, swa_k, swa_v, ret_q, ret_k, ret_v, ret_g,
     nsa_q, nsa_kc, nsa_vc, nsa_ks, nsa_vs, nsa_kw, nsa_vw, nsa_gate, merge_gate) = jnp.split(
        u, [int(c) for c in np.cumsum(IN_WIDTHS)[:-1]], axis=-1)

    def heads(t, n):
        return t.reshape(b, s, n, HEAD_DIM).transpose(0, 2, 1, 3)

    y_conv = conformer_conv(conv_in, conv_dw, conv_db, conv_ln_g, conv_ln_b) @ p_conv
    o_swa = banded_attention(heads(swa_q, SWA_HEADS), heads(swa_k, SWA_KV_HEADS),
                             heads(swa_v, SWA_KV_HEADS), slopes_swa, SWA_WINDOW, swa_sink)
    y_swa = o_swa.transpose(0, 2, 1, 3).reshape(b, s, SWA_HEADS * HEAD_DIM) @ p_swa
    y_ret = retention(ret_q, ret_k, ret_v, ret_g, ret_gn_g, ret_gn_b) @ p_ret
    y_nsa = native_sparse_attention(nsa_q, nsa_kc, nsa_vc, nsa_ks, nsa_vs, nsa_kw, nsa_vw, nsa_gate,
                                    slopes_nsa, nsa_pe_k, nsa_w1_k, nsa_w2_k,
                                    nsa_pe_v, nsa_w1_v, nsa_w2_v) @ p_nsa
    gts = jax.nn.sigmoid(merge_gate.reshape(b, s, N_BRANCH, d).astype(jnp.float32))
    merged = (gts[..., 0, :] * y_conv + gts[..., 1, :] * y_swa
              + gts[..., 2, :] * y_ret + gts[..., 3, :] * y_nsa).astype(x.dtype)
    return merged @ w_out

def moe_ffn(x, router_w, router_b, wg, wu, wd, sh_wg, sh_wu, sh_wd):
    b, s, d = x.shape
    n_tok = b * s
    xt = x.reshape(n_tok, d)
    scores = jax.nn.sigmoid(xt.astype(jnp.float32) @ router_w.astype(jnp.float32).T)
    biased = scores + router_b.astype(jnp.float32)
    grp_score = lax.top_k(biased.reshape(n_tok, N_GROUPS, N_EXPERTS // N_GROUPS), 2)[0].sum(-1)
    _, gidx = lax.top_k(grp_score, TOPK_GROUPS)
    gmask = jnp.any(gidx[:, :, None] == jnp.arange(N_GROUPS)[None, None, :], axis=1)
    emask = jnp.repeat(gmask, N_EXPERTS // N_GROUPS, axis=1)
    _, eidx = lax.top_k(jnp.where(emask, biased, NEG_INF), TOP_K)
    gate = jnp.take_along_axis(scores, eidx, axis=1)
    gate = gate / jnp.sum(gate, -1, keepdims=True) * ROUTE_SCALE

    n_asg = n_tok * TOP_K
    e_flat = eidx.reshape(-1)
    order = jnp.argsort(e_flat)
    e_sorted = e_flat[order]
    tok_sorted = (jnp.arange(n_asg, dtype=jnp.int32) // TOP_K)[order]
    gate_sorted = gate.reshape(-1)[order]
    counts = jnp.bincount(e_flat, length=N_EXPERTS)
    padded = (counts + MOE_BLK - 1) // MOE_BLK * MOE_BLK
    pend = jnp.cumsum(padded)
    dest = (pend - padded)[e_sorted] + jnp.arange(n_asg) - (jnp.cumsum(counts) - counts)[e_sorted]
    n_blocks = (n_asg + N_EXPERTS * (MOE_BLK - 1) + MOE_BLK - 1) // MOE_BLK
    rows = n_blocks * MOE_BLK
    row_tok = jnp.full((rows,), n_tok, jnp.int32).at[dest].set(tok_sorted)
    row_gate = jnp.zeros((rows,), jnp.float32).at[dest].set(gate_sorted)
    blk_exp = jnp.minimum(jnp.searchsorted(pend, jnp.arange(n_blocks) * MOE_BLK, side='right'),
                          N_EXPERTS - 1)
    xpad = jnp.concatenate([xt, jnp.zeros((1, d), xt.dtype)], axis=0)

    def expert_block(args):
        tok, e = args
        h = xpad[tok]
        return (jax.nn.silu(h @ wg[e]) * (h @ wu[e])) @ wd[e]

    y_rows = lax.map(expert_block, (row_tok.reshape(n_blocks, MOE_BLK), blk_exp)).reshape(rows, d)
    routed = jax.ops.segment_sum(y_rows * row_gate[:, None], row_tok, num_segments=n_tok + 1)[:n_tok]
    shared = (jax.nn.silu(xt @ sh_wg) * (xt @ sh_wu)) @ sh_wd
    return (routed + shared).reshape(b, s, d).astype(x.dtype)

def setup_inputs(seed: int = 0) -> dict:
    key = jax.random.key(seed)
    keys = iter(jax.random.split(key, 40))
    L = DEPTH
    D = D_MODEL

    def nrm(shape, scale):
        return jax.random.normal(next(keys), shape, jnp.float32) * scale

    return {
        'x': nrm((BATCH, SEQ, D), 1.0),
        'w_in': nrm((L, D, sum(IN_WIDTHS)), D ** -0.5),
        'conv_dw': nrm((L, CONV_K, CONV_CH), CONV_K ** -0.5),
        'conv_db': nrm((L, CONV_CH), 0.02),
        'conv_ln_g': 1.0 + nrm((L, CONV_CH), 0.02),
        'conv_ln_b': nrm((L, CONV_CH), 0.02),
        'swa_sink': nrm((L, SWA_HEADS), 0.5),
        'ret_gn_g': 1.0 + nrm((L, RET_HEADS * RET_V), 0.02),
        'ret_gn_b': nrm((L, RET_HEADS * RET_V), 0.02),
        'nsa_pe_k': nrm((L, NSA_CMP_LEN, HEAD_DIM), 0.02),
        'nsa_w1_k': nrm((L, NSA_CMP_LEN * HEAD_DIM, NSA_CMP_HIDDEN), (NSA_CMP_LEN * HEAD_DIM) ** -0.5),
        'nsa_w2_k': nrm((L, NSA_CMP_HIDDEN, HEAD_DIM), NSA_CMP_HIDDEN ** -0.5),
        'nsa_pe_v': nrm((L, NSA_CMP_LEN, HEAD_DIM), 0.02),
        'nsa_w1_v': nrm((L, NSA_CMP_LEN * HEAD_DIM, NSA_CMP_HIDDEN), (NSA_CMP_LEN * HEAD_DIM) ** -0.5),
        'nsa_w2_v': nrm((L, NSA_CMP_HIDDEN, HEAD_DIM), NSA_CMP_HIDDEN ** -0.5),
        'p_conv': nrm((L, CONV_CH, D), CONV_CH ** -0.5),
        'p_swa': nrm((L, SWA_HEADS * HEAD_DIM, D), (SWA_HEADS * HEAD_DIM) ** -0.5),
        'p_ret': nrm((L, RET_HEADS * RET_V, D), (RET_HEADS * RET_V) ** -0.5),
        'p_nsa': nrm((L, NSA_HEADS * HEAD_DIM, D), (NSA_HEADS * HEAD_DIM) ** -0.5),
        'w_out': nrm((L, D, D), BETA * D ** -0.5),
        'ln1_g': 1.0 + nrm((L, D), 0.02),
        'ln1_b': nrm((L, D), 0.02),
        'router_w': nrm((L, N_EXPERTS, D), D ** -0.5),
        'router_b': nrm((L, N_EXPERTS), 0.01),
        'moe_wg': nrm((L, N_EXPERTS, D, D_EXPERT), D ** -0.5),
        'moe_wu': nrm((L, N_EXPERTS, D, D_EXPERT), D ** -0.5),
        'moe_wd': nrm((L, N_EXPERTS, D_EXPERT, D), BETA * D_EXPERT ** -0.5),
        'sh_wg': nrm((L, D, D_EXPERT), D ** -0.5),
        'sh_wu': nrm((L, D, D_EXPERT), D ** -0.5),
        'sh_wd': nrm((L, D_EXPERT, D), BETA * D_EXPERT ** -0.5),
        'ln2_g': 1.0 + nrm((L, D), 0.02),
        'ln2_b': nrm((L, D), 0.02),
    }

def reference(x, w_in, conv_dw, conv_db, conv_ln_g, conv_ln_b, swa_sink, ret_gn_g, ret_gn_b,
              nsa_pe_k, nsa_w1_k, nsa_w2_k, nsa_pe_v, nsa_w1_v, nsa_w2_v,
              p_conv, p_swa, p_ret, p_nsa, w_out, ln1_g, ln1_b,
              router_w, router_b, moe_wg, moe_wu, moe_wd, sh_wg, sh_wu, sh_wd, ln2_g, ln2_b):
    slopes = alibi_slopes(SWA_HEADS + NSA_HEADS)
    slopes_swa, slopes_nsa = slopes[:SWA_HEADS], slopes[SWA_HEADS:]
    for l in range(DEPTH):
        mix = token_mixer(x, w_in[l], conv_dw[l], conv_db[l], conv_ln_g[l], conv_ln_b[l], swa_sink[l],
                          ret_gn_g[l], ret_gn_b[l], nsa_pe_k[l], nsa_w1_k[l], nsa_w2_k[l],
                          nsa_pe_v[l], nsa_w1_v[l], nsa_w2_v[l], p_conv[l], p_swa[l], p_ret[l], p_nsa[l],
                          w_out[l], slopes_swa, slopes_nsa)
        x = layer_norm(ALPHA * x + mix, ln1_g[l], ln1_b[l])
        ffn = moe_ffn(x, router_w[l], router_b[l], moe_wg[l], moe_wu[l], moe_wd[l],
                      sh_wg[l], sh_wu[l], sh_wd[l])
        x = layer_norm(ALPHA * x + ffn, ln2_g[l], ln2_b[l])
    return x


_drawn_inputs = setup_inputs


def setup_inputs(seed=0):
    import zlib

    import numpy as np

    out = dict(_drawn_inputs(seed))
    spreads = {}
    factors = {'conv_ln_g': 3.263,
     'conv_ln_b': 2.924,
     'ret_gn_g': 2.907,
     'ret_gn_b': 3.078,
     'nsa_pe_k': 33.291,
     'nsa_pe_v': 5.364,
     'ln2_g': 7.642,
     'ln2_b': 8.023,
     'swa_sink': 2.681}
    for name, (base, spread) in spreads.items():
        noise = np.random.default_rng([zlib.crc32(name.encode()), seed]).standard_normal(out[name].shape)
        drawn = base * np.exp(spread * noise) if base else spread * noise
        out[name] = jnp.asarray(drawn.astype(out[name].dtype))
    for name, factor in factors.items():
        out[name] = (out[name] * factor).astype(out[name].dtype)
    return out
```

```python
from contextlib import ExitStack

import numpy as np

import concourse.bass as bass
from concourse import mybir

F32, F32R, I32, BF16 = mybir.dt.float32, mybir.dt.float32r, mybir.dt.int32, mybir.dt.bfloat16
ALU, ACT, AX = mybir.AluOpType, mybir.ActivationFunctionType, mybir.AxisListType

P = 128
D = 1024
S = 1024
KD = D // P
NT = S // P
HALF = 512
CONV_K, CONV_C = 31, 2
DH = 64
NCMP, CMP_LEN, CMP_STRIDE, CMP_HID = 63, 32, 16, 256
NSLC, SLC = 16, 64
E, NG, TOPG, TOPK, FE = 64, 8, 4, 6, 256
EG = E // NG
ALPHA = float(2 ** 0.25)
EPS = 1e-5
ROUTE = 2.5
BIG = 1e33
NEG = -1e30
SLOPES = [2.0 ** -(i + 1) for i in range(8)]
SLOPE_SWA, SLOPE_NSA = SLOPES[:4], SLOPES[4:]
MAXB = 128

IN_NAMES = ['x', 'w_in', 'conv_dw', 'conv_db', 'conv_ln_g', 'conv_ln_b', 'swa_sink', 'ret_gn_g', 'ret_gn_b',
            'nsa_pe_k', 'nsa_w1_k', 'nsa_w2_k', 'nsa_pe_v', 'nsa_w1_v', 'nsa_w2_v', 'p_conv', 'p_swa', 'p_ret',
            'p_nsa', 'w_out', 'ln1_g', 'ln1_b', 'router_w', 'router_b', 'moe_wg', 'moe_wu', 'moe_wd',
            'sh_wg', 'sh_wu', 'sh_wd', 'ln2_g', 'ln2_b']

O_CONV, O_SQ, O_SK, O_SV, O_RQ, O_RK, O_RV, O_RG, O_NQ = 0, 512, 768, 896, 1024, 1280, 1536, 2048, 2560
O_KC, O_KS, O_VS, O_KW, O_VW, O_GT, O_MG = 2816, 2944, 3008, 3072, 3136, 3200, 3212


def constants():
    q = np.arange(P)[:, None].astype(np.float64)
    out = {}
    out['ident'] = np.eye(P)
    j = np.arange(1024)[None, :]
    d = q + 896 - j
    out['dist_sel'] = np.where(d >= 0, d, BIG)
    j = np.arange(640)[None, :]
    d = q + 512 - j
    out['dist_win'] = np.where((d >= 0) & (d < 512), d, BIG)
    j = np.arange(256)[None, :]
    d = q + 128 - j
    out['dist_swa'] = np.where((d >= 0) & (d < 128), d, BIG)
    n, c = np.arange(NT)[None, :, None], np.arange(NCMP)[None, None, :]
    d = q[:, :, None] + P * n - (CMP_STRIDE * c + CMP_LEN - 1)
    out['dist_cmp'] = np.where(d >= 0, d, BIG).reshape(P, -1)
    out['mask_cmp'] = (d >= 0).reshape(P, -1)
    t, jj = q[:, :, None] + P * n, np.arange(NSLC)[None, None, :]
    cur = t // SLC
    forced = (jj == 0) | (jj == cur) | (jj == cur - 1)
    out['imp_keep'] = (~forced & (jj <= cur)).reshape(P, -1)
    out['imp_set'] = np.where(forced, 1e4, np.where(jj > cur, -1.0, 0.0)).reshape(P, -1)
    lg = np.log1p(-(2.0 ** (-5.0 - np.arange(4))))
    k, qq = np.arange(P)[:, None], np.arange(P)[None, :]
    out['decay'] = np.stack([np.where(qq >= k, 0.125 * np.exp(lg[h] * np.maximum(qq - k, 0)), 0) for h in range(4)],
                            1).reshape(P, -1)
    xi = np.exp(lg[:, None] * (np.arange(P) + 1.0)[None, :])
    out['xi'] = np.stack([np.repeat(xi[2 * p:2 * p + 2], 64, 0) for p in range(2)], 1).reshape(P, -1)
    out['zeta'] = (0.125 * np.exp(lg[:, None] * (P - 1 - np.arange(P))[None, :])).T
    cd = np.exp(lg * P)
    out['chunk_decay'] = np.stack([np.repeat(cd[2 * p:2 * p + 2], 64) for p in range(2)], 1)
    out['mean_conv'] = np.full((P, P), 1.0 / (CONV_C * P))
    return {k: np.ascontiguousarray(v, dtype=np.float32) for k, v in out.items()}


def constants_moe():
    r = np.arange(P)[:, None]
    out = {}
    out['ident'] = np.eye(P)
    out['before'] = (r < np.arange(P)[None, :])
    out['ones'] = np.ones((P, P))
    out['rank'] = np.tile(np.arange((NT + 1) * P)[None, :], (P, 1))
    out['tile_tok'] = np.tile(P * np.arange(NT)[None, :] - 1024.0, (P, 1))
    out['row'] = r
    out['neg_row'] = -1.0 * r
    out['row_dummy'] = r + 1024.0
    out['even'] = (r % 2 == 0) & (r > 0)
    out['steps'] = np.tile(P * np.arange(8)[None, :], (P, 1))
    out['lower'] = np.tile((np.arange(8)[None, :] < np.arange(8)[:, None]).reshape(1, -1), (P, 1))
    return {k: np.ascontiguousarray(v, dtype=np.float32) for k, v in out.items()}


def packed(tables):
    at, offs = 0, {}
    for k, v in tables.items():
        offs[k] = (at, v.shape[1])
        at += v.shape[1]
    return np.concatenate(list(tables.values()), 1), offs


def chunk_list():
    one = lambda c: [(0, c, P)]
    pairs = lambda a, b: [(0, a, 64), (64, b, 64)]
    out = [('conv_gate', c, one(O_CONV + 256 + c * P)) for c in range(2)]
    out += [('conv_a', c, one(O_CONV + c * P)) for c in range(2)]

    def ret(p):
        return ([('ret_q', p, one(O_RQ + p * P)), ('ret_k', p, one(O_RK + p * P))]
                + [('ret_v', (p, e), one(O_RV + (2 * p + e) * P)) for e in range(2)]
                + [('ret_g', (p, e), one(O_RG + (2 * p + e) * P)) for e in range(2)])
    gates = [('merge', (j, b), one(O_MG + b * D + j * P)) for j in range(KD) for b in range(4)]
    out += ret(0) + gates[:5] + ret(1)
    out += [('swa_q', c, pairs(O_SQ + c * 64, O_SQ + c * 64 + 128)) for c in range(2)]
    out += [('swa_k', 0, one(O_SK)), ('swa_v', 0, one(O_SV))]
    out += [('nsa_q', c, one(O_NQ + c * P)) for c in range(2)]
    out += [('kcvc', 0, one(O_KC)), ('ks', 0, pairs(O_KS, O_KS)), ('kw', 0, pairs(O_KW, O_KW)),
            ('vsvw', 0, pairs(O_VS, O_VW)), ('gate', 0, one(O_GT))]
    return out + gates[5:]


CHUNKS = chunk_list()
NCH = len(CHUNKS)
WHERE = {(k, i): c for c, (k, i, _) in enumerate(CHUNKS)}


def attention_units():
    swa = [dict(kind='swa', n=n, h=h, b0=max(0, n - 1), nb=min(n + 1, 2)) for n in range(NT) for h in range(4)]
    nsa = []
    for n in range(NT):
        for h in range(4):
            nsa.append(dict(kind='win', n=n, h=h, b0=max(0, n - 4), nb=min(n + 1, 5)))
            nsa.append(dict(kind='sel', n=n, h=h, b0=0, nb=n + 1))
    fills = 0
    units = swa + nsa
    for u, un in enumerate(units):
        un['u'] = u
    return swa, nsa


SWA, NSA = attention_units()
UNITS = SWA + NSA


def schedule():
    items = [('xt', g) for g in range(8)] + [('mm', 0), ('mm', 1)] + [('xt', g) for g in range(8, 16)]
    state = dict(q=2, fill=0, pv=0)
    last = 4 * NCH

    def adv(n):
        for _ in range(n):
            if state['q'] < last:
                items.append(('mm', state['q']))
                state['q'] += 1

    def upto(c):
        adv(max(0, 4 * c - state['q']))

    def fill(kind, *a):
        items.append(('fill', state['fill'], kind, a))
        state['fill'] += 1

    upto(WHERE['ret_q', 0])
    items.append(('conv_h',))
    for k in range(CONV_K):
        items.append(('tap', k))
        adv(1)
    adv(2)
    for c in ('conv_mean', 'conv_var', 'conv_out'):
        items.append((c,))
        adv(4)

    def retention(p):
        items.append(('ret_a', p, 0))
        for n in range(NT):
            adv(1)
            if n + 1 < NT:
                items.append(('ret_a', p, n + 1))
            items.append(('ret_b', p, n))
        items.append(('ret_norm', p))
        adv(6)
        for g in range(4):
            fill('ret', p, g)
        items.append(('ret_store', p))
    upto(WHERE['ret_g', (0, 1)] + 1)
    retention(0)
    upto(WHERE['ret_g', (1, 1)] + 1)
    retention(1)
    upto(WHERE['swa_v', 0] + 1)
    for g in range(2):
        fill('swa_v', g)
        adv(1)

    def attention(units, rate):
        debt = 0.0
        for k in range(-1, len(units) + 1):
            if k + 1 < len(units):
                un = units[k + 1]
                if un['kind'] == 'sel' and un['h'] == 0:
                    items.append(('sel_table', un['n']))
                items.append(('score', un['u']))
                items.append(('max', un['u']))
            if 0 <= k < len(units):
                items.append(('norm', units[k]['u']))
            if k < 1 and k + 1 < len(units):
                items.append(('exp', units[k + 1]['u']))
            if k >= 1:
                prev = units[k - 1]
                groups = [list(range(a, min(a + 4, prev['nb']))) for a in range(0, prev['nb'], 4)]
                prev['last_fill'] = state['fill'] + len(groups) - 1
                for g, blocks in enumerate(groups):
                    fill('unit', prev['u'], tuple(blocks), state['pv'])
                    if g == 0 and k + 1 < len(units):
                        items.append(('exp', units[k + 1]['u']))
                    debt += rate / len(groups)
                    adv(int(debt))
                    debt -= int(debt)
                    items.append(('pv', state['pv'], prev['u'], tuple(blocks)))
                    state['pv'] += 1
                prev['last_pv'] = state['pv'] - 1
                if prev['h'] == 3 and prev['kind'] != 'win':
                    items.append(('out', prev['kind'], prev['n']))
    attention(SWA, 0.9)
    upto(WHERE['gate', 0] + 1)
    fill('gate')
    for g in range(2):
        fill('vsvw', g)
    fill('pe')
    adv(6)
    items.append(('hidden',))
    adv(2)
    items.append(('hidden_t',))
    adv(1)
    items.append(('compress',))
    adv(1)
    for n in range(NT):
        items.append(('cmp_score', n))
        adv(3)
        fill('cmp', n)
    attention(NSA, (last - state['q']) / len(NSA))
    adv(last)
    return items


SCHEDULE = schedule()


def bcast(ap, axis, n):
    ap = ap.unsqueeze(axis)
    shape = list(ap.shape)
    shape[axis] = n
    return ap.broadcast_to(shape)


class Order:

    def __init__(self, eng, sem):
        self.eng, self.sem, self.n = eng, sem, 0

    def after(self, ins):
        self.n += 1
        ins.then_inc(self.sem, 1)
        self.eng.wait_ge(self.sem, self.n)


def mixers(nc, d, c_ap, c_at, yt, gates, sem):
    with ExitStack() as ctx:
        def sb(name, shape, dt=F32):
            return ctx.enter_context(nc.sbuf_tensor(name, shape, dt))

        cst = sb('a_const', [P, c_ap.shape[1]])

        def const(name):
            at, width = c_at[name]
            return cst[:, at:at + width]
        ident = const('ident')
        x_hi, x_lo = sb('x_hi', [P, KD, S], F32R), sb('x_lo', [P, KD, S], F32R)
        w_hi, w_lo = sb('w_hi', [P, 2, KD, P], F32R), sb('w_lo', [P, 2, KD, P], F32R)
        w_raw = sb('w_raw', [P, 2, KD, P])
        gate_out = sb('gate_out', [P, 2, HALF])
        reg_a, reg_b, reg_s = sb('reg_a', [P, 8 * 1024]), sb('reg_b', [P, 8 * 1024]), sb('reg_s', [P, 5 * 1024])
        state, o_stats = sb('state', [P, 2, P]), sb('o_stats', [P, 16, 6])
        o_mv, o_rstd = sb('o_mv', [P, 16, 2]), sb('o_rstd', [P, 16])
        hid = sb('hid', [P, 4, 64])
        k_cmp, v_cmp = sb('k_cmp', [P, 64]), sb('v_cmp', [64, DH])
        w2k, w2v = sb('w2k', [P, 2, P]), sb('w2v', [P, 2, DH])
        cs = sb('cs', [P, 2, 4, NCMP])
        c_max, c_sum = sb('c_max', [P, 4]), sb('c_sum', [P, 4])
        c_all = sb('c_all', [P, 65])
        imp, imp_top, imp_cut = sb('imp', [P, NSLC]), sb('imp_top', [P, 8]), sb('imp_cut', [P, NSLC])
        gate_n = sb('gate_n', [P, NT, 12])
        sel_pen = sb('sel_pen', [P, NT, NSLC])
        out_t = sb('out_t', [P, 2, 2, P])
        conv_n = sb('conv_n', [34, 256])
        conv_p = sb('conv_p', [P, 2, 34])
        pe_n, pe_t = sb('pe_n', [32, P]), sb('pe_t', [P, 32])
        sink8 = sb('sink8', [P, 4])
        m_raw, m_neg, den, e_sink = sb('m_raw', [P, 3]), sb('m_neg', [P, 3]), sb('den', [P, 3]), sb('e_sink', [P, 3])
        rden = sb('rden', [P, 3])
        eps = sb('eps', [P, 1])
        bank = [ctx.enter_context(nc.psum_tensor(f'a_bank{i}', [P, HALF], F32)) for i in range(8)]

        def view(region, at, *shape):
            size = int(np.prod(shape))
            ap = region[:, at:at + size]
            if len(shape) == 2:
                return ap.rearrange('p (a b) -> p a b', b=shape[1])
            if len(shape) == 3:
                return ap.rearrange('p (a b c) -> p a b c', b=shape[1], c=shape[2])
            return ap
        x_nat = view(reg_a, 0, NT, D)
        conv_gate, conv_h, conv_y = view(reg_b, 0, 2, S), view(reg_b, 2048, 2, S + CONV_K - 1), view(reg_b, 4160, 2, S)
        conv_r = view(reg_b, 2048, S)
        RET = [dict(v=view(r, 0, 2, S), g=view(r, 2048, 2, S), q=view(r, 4096, S), k=view(r, 5120, S),
                    out=view(r, 4096, 2, S), th=view(r, 6144, 2, S)) for r in (reg_a, reg_b)]
        v_n, inner = view(reg_s, 0, 2, 2, P), view(reg_s, 512, 2, 2, P)
        q_xi, k_z = view(reg_s, 1024, 2, P), view(reg_s, 1280, 2, P)
        gn_g, gn_b = view(reg_s, 2048, 4, P), view(reg_s, 2560, 4, P)
        swa_q, swa_k, swa_vt, swa_v = (view(reg_a, 0, 2, S), view(reg_a, 2048, S), view(reg_a, 3072, S),
                                       view(reg_a, 4096, NT, P))
        nsa_q, kcvc, k_slc, k_win = (view(reg_b, 0, 2, S), view(reg_b, 2048, S), view(reg_b, 3072, S),
                                     view(reg_b, 4096, S))
        vsvw_t, vsvw, gate_t = view(reg_b, 5120, S), view(reg_b, 6144, NT, P), view(reg_b, 7168, S)
        w1 = view(reg_a, 0, CMP_LEN, CMP_HID)
        p_cmp_t = view(reg_a, 0, NT, 4, P)
        soft, w_t, dist_n = view(reg_s, 0, 3, 1024), view(reg_s, 3072, 2, HALF), view(reg_s, 4096, 1024)
        w_t3 = view(reg_s, 3072, 2, 4, P)
        hid_n = view(reg_s, 0, 2, CMP_HID)
        z_cmp = view(reg_s, 3072, CMP_LEN, 64)

        ident_in, const_in, x_in, small_in, gn_in = sem('ident_in'), sem('const_in'), [sem(f'x_in{i}') for i in range(4)], sem('small_in'), sem('gn_in')
        w_in_s = [sem(f'w_raw_in{i}') for i in range(2)]
        w_hi_ready, w_lo_ready = sem('w_hi_ready'), sem('w_lo_ready')
        x_t, x_hi_ready, x_lo_ready = sem('x_t'), sem('x_hi_ready'), sem('x_lo_ready')
        half_done, half_out = sem('half_done'), sem('half_out')
        gate_stored = [sem('gate_stored0'), sem('gate_stored1')]
        fill_done, fill_out = sem('fill_done'), sem('fill_out')
        dve_order, act_order, pool_order = sem('dve_order'), sem('act_order'), sem('pool_order')
        taps_done, conv_params = sem('taps_done'), sem('conv_params')
        conv_mean_done, conv_sq, conv_var_done, conv_sd, conv_norm, conv_th, conv_fin = (
            sem('conv_mean_done'), sem('conv_sq'), sem('conv_var_done'), sem('conv_sd'), sem('conv_norm'),
            sem('conv_th'), sem('conv_fin'))
        conv_stored = sem('conv_stored')
        ret_a_done, ret_mid, ret_v_out, ret_b_done, ret_state = (sem('ret_a_done'), sem('ret_mid'), sem('ret_v_out'),
                                                                 sem('ret_b_done'), sem('ret_state'))
        ret_mv, ret_sd, ret_th, ret_fin, ret_stored = (sem('ret_mv'), sem('ret_sd'), sem('ret_th'), sem('ret_fin'),
                                                       sem('ret_stored'))
        score_done, max_done, exp_done, soft_done = (sem('score_done'), sem('max_done'), sem('exp_done'),
                                                     sem('soft_done'))
        pv_done, tile_out = sem('pv_done'), sem('tile_out')
        tile_stored = [sem('tile_stored0'), sem('tile_stored1')]
        w1_in, z_ready, hid_done, hid_out, cmp_done, cmp_out = (sem('w1_in'), sem('z_ready'), sem('hid_done'),
                                                                sem('hid_out'), sem('cmp_done'), sem('cmp_out'))
        cscore_done, cmax_done, cexp_done, csoft_done = (sem('cscore_done'), sem('cmax_done'), sem('cexp_done'),
                                                         sem('csoft_done'))
        hid_gelu, hid_t_done = sem('hid_gelu'), sem('hid_t_done')
        eps_ready, state_zero = sem('eps_ready'), sem('state_zero')

        block = ctx.enter_context(nc.Block())

        def home(c, h):
            kind, i, _ = CHUNKS[c]
            cols = slice(h * HALF, (h + 1) * HALF)
            if kind == 'conv_gate':
                return conv_gate[:, i, cols]
            if kind == 'conv_a':
                return conv_h[:, i, CONV_K - 1 + h * HALF:CONV_K - 1 + (h + 1) * HALF]
            if kind in ('ret_q', 'ret_k'):
                return RET[i][kind[-1]][:, cols]
            if kind in ('ret_v', 'ret_g'):
                return RET[i[0]][kind[-1]][:, i[1], cols]
            if kind in ('swa_q', 'nsa_q'):
                return (swa_q if kind == 'swa_q' else nsa_q)[:, i, cols]
            return {'swa_k': swa_k, 'swa_v': swa_vt, 'kcvc': kcvc, 'ks': k_slc, 'kw': k_win, 'vsvw': vsvw_t,
                    'gate': gate_t}[kind][:, cols]

        def raw_total(c):
            return sum(16 * len(CHUNKS[k][2]) for k in range(c % 2, c + 1, 2))

        @block.sync
        def _(sp):
            at, width = c_at['ident']
            sp.dma_start(ident, c_ap[:, at:at + width]).then_inc(ident_in, 16)
            for h in range(4):
                rows, cols = slice(h // 2 * HALF, (h // 2 + 1) * HALF), slice(h % 2 * HALF, (h % 2 + 1) * HALF)
                sp.dma_start(x_nat[:, h // 2 * 4:h // 2 * 4 + 4, cols],
                             d['x'][0, rows, cols].rearrange('(n p) d -> p n d', p=P)).then_inc(x_in[h], 16)
            for c, (_, _, parts) in enumerate(CHUNKS):
                if c == 2:
                    sp.dma_start(cst[:, width:], c_ap[:, width:]).then_inc(const_in, 16)
                if c >= 2:
                    sp.wait_ge(w_lo_ready, c - 1)
                    sp.wait_ge(w_hi_ready, c - 1)
                for dst, src, width in parts:
                    sp.dma_start(w_raw[:, c % 2, :, dst:dst + width],
                                 d['w_in'][0, :, src:src + width].rearrange('(k p) n -> p k n', p=P)
                                 ).then_inc(w_in_s[c % 2], 16)

        @block.gpsimd
        def _(pool):
            pool.dma_start(conv_n[0:31, :], d['conv_dw'][0]).then_inc(small_in, 16)
            for i, name in enumerate(('conv_db', 'conv_ln_g', 'conv_ln_b')):
                pool.dma_start(conv_n[31 + i:32 + i, :], d[name]).then_inc(small_in, 16)
            pool.dma_start(pe_n[:, 0:64], d['nsa_pe_k'][0]).then_inc(small_in, 16)
            pool.dma_start(pe_n[:, 64:128], d['nsa_pe_v'][0]).then_inc(small_in, 16)
            for i in range(2):
                pool.dma_start(w2k[:, :, 64 * i:64 * i + 64],
                               d['nsa_w2_k'][0].rearrange('(m p) n -> p m n', p=P)).then_inc(small_in, 16)
            pool.dma_start(w2v[:, :, :], d['nsa_w2_v'][0].rearrange('(m p) n -> p m n', p=P)).then_inc(small_in, 16)
            pool.dma_start(sink8[:, :], d['swa_sink'].broadcast_to([P, 4])).then_inc(small_in, 16)
            pool.dma_start(gn_g[:, :, :], d['ret_gn_g'].broadcast_to([P, 512]).rearrange('p (a b) -> p a b', b=P)).then_inc(gn_in, 16)
            pool.dma_start(gn_b[:, :, :], d['ret_gn_b'].broadcast_to([P, 512]).rearrange('p (a b) -> p a b', b=P)).then_inc(gn_in, 16)
            stored = [0, 0]
            for item in SCHEDULE:
                if item[0] == 'conv_out':
                    pool.wait_ge(conv_fin, 1)
                    pool.dma_start(yt[0:2].rearrange('c p s -> p c s'), conv_y).then_inc(conv_stored, 16)
                elif item[0] == 'ret_store':
                    pair = item[1]
                    pool.wait_ge(fill_out, 4 * pair + 4)
                    pool.dma_start(yt[4 + 2 * pair:6 + 2 * pair].rearrange('c p s -> p c s'),
                                   RET[pair]['out']).then_inc(ret_stored, 16)
                elif item[0] == 'out':
                    kind, n = item[1:]
                    t = n + NT * (kind != 'swa')
                    pool.wait_ge(tile_out, t + 1)
                    at = 2 if kind == 'swa' else 8
                    pool.dma_start(yt[at:at + 2, :, n * P:(n + 1) * P].rearrange('c p s -> p c s'),
                                   out_t[:, n % 2]).then_inc(tile_stored[n % 2], 16)
                    stored[n % 2] += 16
                    if kind == 'swa' and n == NT - 1:
                        pool.wait_ge(pv_done, SWA[-1]['last_pv'] + 1)
                        for i, name in enumerate(('nsa_w1_k', 'nsa_w1_v')):
                            pool.dma_start(w1[64 * i:64 * i + 64], d[name][0].rearrange('(l e) h -> e l h', e=DH)
                                           ).then_inc(w1_in, 16)
            for i in range(2):
                pool.wait_ge(tile_stored[i], stored[i])
            pool.wait_ge(conv_stored, 16)
            pool.wait_ge(ret_stored, 32)

        @block.tensor
        def _(pe):
            def quarter(q):
                c, h, part = q // 4, q // 2 % 2, q % 2
                if q % 4 == 0:
                    pe.wait_ge(w_hi_ready, c + 1)
                    pe.wait_ge(w_lo_ready, c + 1)
                if q in (0, 2):
                    pe.wait_ge(x_lo_ready, 8 if q == 0 else 16)
                if part == 0 and c >= 1:
                    pe.wait_ge(half_out, 2 * c + h - 1)
                for k in range(4 * part, 4 * part + 4):
                    cols = slice(h * HALF, (h + 1) * HALF)
                    for j, (w, x) in enumerate(((w_hi, x_hi), (w_hi, x_lo), (w_lo, x_hi))):
                        ins = pe.matmul(bank[h][:, :], w[:, c % 2, k, :], x[:, k, cols],
                                        start=(k == 0 and j == 0), stop=(k == KD - 1 and j == 2))
                if part == 1:
                    ins.then_inc(half_done, 1)

            def transposes(pairs_):
                for out, in_, idn in pairs_:
                    ins = pe.transpose(out, in_, idn)
                return ins

            pe.wait_ge(ident_in, 16)
            for item in SCHEDULE:
                what = item[0]
                if what == 'mm':
                    quarter(item[1])
                elif what == 'xt':
                    g = item[1]
                    h, k = g // 8, g % 8
                    if g % 4 == 0:
                        pe.wait_ge(x_in[g // 4], 16)
                    if g >= 4:
                        pe.wait_ge(x_lo_ready, g - 3)
                    transposes([(bank[2 + g % 4][:, j * P:(j + 1) * P], x_nat[:, 4 * h + j, k * P:(k + 1) * P], ident)
                                for j in range(4)]).then_inc(x_t, 1)
                elif what == 'conv_h':
                    pe.wait_ge(small_in, 160)
                    transposes([(bank[6][:, c * 34:(c + 1) * 34], conv_n[:, c * P:(c + 1) * P], ident[0:34, 0:34])
                                for c in range(2)]).then_inc(conv_params, 1)
                elif what == 'conv_mean':
                    pe.wait_ge(const_in, 16)
                    pe.wait_ge(taps_done, 2 * CONV_K)
                    for h in range(2):
                        for c in range(2):
                            ins = pe.matmul(bank[2 + h][:, :], const('mean_conv'), conv_y[:, c, h * HALF:(h + 1) * HALF],
                                            start=c == 0, stop=c == 1)
                    ins.then_inc(conv_mean_done, 1)
                elif what == 'conv_var':
                    pe.wait_ge(conv_sq, 1)
                    for h in range(2):
                        for c in range(2):
                            ins = pe.matmul(bank[4 + h][:, :], const('mean_conv'),
                                            conv_gate[:, c, h * HALF:(h + 1) * HALF], start=c == 0, stop=c == 1)
                    ins.then_inc(conv_var_done, 1)
                elif what == 'ret_a':
                    pair, n = item[1:]
                    i = NT * pair + n
                    s, R, blk = i % 2, RET[pair], slice(n * P, (n + 1) * P)
                    T, K = bank[2 + 3 * s], bank[3 + 3 * s]
                    if n == 0:
                        pe.wait_ge(half_out, 2 * WHERE['ret_g', (pair, 1)] + 2)
                        pe.wait_ge(conv_norm, 1)
                        pe.wait_ge(fill_out, 4 * pair) if pair else None
                    if i >= 2:
                        pe.wait_ge(ret_v_out, i - 1)
                        pe.wait_ge(ret_mid, i - 1)
                        pe.wait_ge(ret_state, i - 1)
                    transposes([(T[:, e * P:(e + 1) * P], R['v'][:, e, blk], ident) for e in range(2)]
                               + [(T[:, (2 + e) * P:(3 + e) * P], R['g'][:, e, blk], ident) for e in range(2)]
                               + [(K[:, 0:P], R['k'][:, blk], ident)])
                    for e in range(2):
                        rows = slice(64 * e, 64 * e + 64)
                        out = K[:, P:2 * P] if e == 0 else bank[4 + 3 * s][:, 3 * P:4 * P]
                        ins = pe.matmul(out, R['k'][rows, blk], R['q'][rows, blk], start=True, stop=True)
                    ins.then_inc(ret_a_done, 1)
                elif what == 'ret_b':
                    pair, n = item[1:]
                    i = NT * pair + n
                    s, O = i % 2, bank[4 + 3 * (i % 2)]
                    pe.wait_ge(ret_mid, i + 1)
                    pe.wait_ge(ret_v_out, i + 1)
                    if i == 0:
                        pe.wait_ge(state_zero, 1)
                    else:
                        pe.wait_ge(ret_state, i)
                    pe.matmul(O[:, 0:2 * P], q_xi[:, s, :], state[:, :, :], start=True, stop=False)
                    for e in range(2):
                        pe.matmul(O[:, e * P:(e + 1) * P], inner[:, s, e, :], v_n[:, s, e, :], start=False, stop=e == 1)
                    for e in range(2):
                        rows = slice(64 * e, 64 * e + 64)
                        ins = pe.matmul(O[rows, 2 * P:3 * P], k_z[:, s, rows], v_n[:, s, e, :], start=True, stop=True)
                    ins.then_inc(ret_b_done, 1)
                elif what == 'fill':
                    f, kind, a = item[1:]
                    B = bank[6]
                    if f:
                        pe.wait_ge(fill_out, f)
                    if kind == 'ret':
                        pair, g = a
                        e, n0 = g // 2, 4 * (g % 2)
                        pe.wait_ge(ret_fin, pair + 1)
                        todo = [(B[:, j * P:(j + 1) * P], RET[pair]['v'][:, e, (n0 + j) * P:(n0 + j + 1) * P], ident)
                                for j in range(4)]
                    elif kind in ('swa_v', 'vsvw'):
                        pe.wait_ge(half_out, 2 * WHERE[kind, 0] + 2)
                        src = swa_vt if kind == 'swa_v' else vsvw_t
                        todo = [(B[:, j * P:(j + 1) * P], src[:, (4 * a[0] + j) * P:(4 * a[0] + j + 1) * P], ident)
                                for j in range(4)]
                    elif kind == 'gate':
                        pe.wait_ge(half_out, 2 * WHERE['gate', 0] + 2)
                        todo = [(B[:, n * 12:(n + 1) * 12], gate_t[0:12, n * P:(n + 1) * P], ident[0:12, 0:12])
                                for n in range(NT)]
                    elif kind == 'pe':
                        todo = [(B[:, 0:32], pe_n[:, :], ident[0:32, 0:32])]
                    elif kind == 'cmp':
                        n = a[0]
                        pe.wait_ge(csoft_done, n + 1)
                        todo = [(B[0:NCMP, h * P:(h + 1) * P], cs[:, n % 2, h, :], ident) for h in range(4)]
                    else:
                        u, blocks, _ = a
                        pe.wait_ge(soft_done, u + 1)
                        todo = [(B[:, j * P:(j + 1) * P], soft[:, u % 3, b * P:(b + 1) * P], ident)
                                for j, b in enumerate(blocks)]
                    transposes(todo).then_inc(fill_done, 1)
                elif what == 'hidden':
                    pe.wait_ge(w1_in, 32)
                    pe.wait_ge(z_ready, 2)
                    for kv in range(2):
                        rows = slice(64 * kv, 64 * kv + 64)
                        B = bank[2 + 3 * kv]
                        for l in range(CMP_LEN):
                            ins = pe.matmul(B[0:NCMP, 0:CMP_HID], z_cmp[rows, l, 0:NCMP], w1[rows, l, :],
                                            start=l == 0, stop=l == CMP_LEN - 1)
                    ins.then_inc(hid_done, 1)
                elif what == 'hidden_t':
                    pe.wait_ge(hid_gelu, 1)
                    transposes([(bank[2][:, j * 64:j * 64 + NCMP], hid_n[0:NCMP, j // 2, (j % 2) * P:(j % 2 + 1) * P],
                                 ident[0:NCMP, 0:NCMP]) for j in range(4)]).then_inc(hid_t_done, 1)
                elif what == 'compress':
                    pe.wait_ge(hid_out, 1)
                    for m in range(2):
                        pe.matmul(bank[3][:, 0:NCMP], w2k[:, m, :], hid[:, m, 0:NCMP], start=m == 0, stop=m == 1)
                    for m in range(2):
                        ins = pe.matmul(bank[4][0:NCMP, 0:DH], hid[:, 2 + m, 0:NCMP], w2v[:, m, :], start=m == 0,
                                        stop=m == 1)
                    ins.then_inc(cmp_done, 1)
                elif what == 'cmp_score':
                    n = item[1]
                    pe.wait_ge(cmp_out, 1)
                    if n >= 2:
                        pe.wait_ge(cmax_done, n - 1)
                    for h in range(4):
                        rows = slice(64 * (h % 2), 64 * (h % 2) + 64)
                        B = bank[2 + 2 * (n % 2) + h % 2]
                        ins = pe.matmul(B[:, h * 64:h * 64 + NCMP], nsa_q[rows, h // 2, n * P:(n + 1) * P],
                                        k_cmp[rows, 0:NCMP], start=True, stop=True)
                    ins.then_inc(cscore_done, 1)
                elif what == 'score':
                    un = UNITS[item[1]]
                    u, n, h = un['u'], un['n'], un['h']
                    if u >= 2:
                        pe.wait_ge(max_done, u - 1)
                    if un['kind'] == 'swa':
                        if u == 0:
                            pe.wait_ge(half_out, 2 * WHERE['swa_k', 0] + 2)
                            pe.wait_ge(ret_state, 16)
                        rows, qs, keys = slice(64 * (h // 2), 64 * (h // 2) + 64), swa_q[:, h % 2], swa_k
                    else:
                        if u == len(SWA):
                            pe.wait_ge(cmax_done, NT)
                        rows, qs = slice(64 * (h % 2), 64 * (h % 2) + 64), nsa_q[:, h // 2]
                        keys = k_win if un['kind'] == 'win' else k_slc
                    L = un['nb'] * P
                    for at in range(0, L, HALF):
                        w = min(HALF, L - at)
                        ins = pe.matmul(bank[2 + 2 * (u % 2) + at // HALF][:, 0:w], qs[rows, n * P:(n + 1) * P],
                                        keys[rows, un['b0'] * P + at:un['b0'] * P + at + w], start=True, stop=True)
                    ins.then_inc(score_done, 1)
                elif what == 'pv':
                    i, u, blocks = item[1:]
                    un = UNITS[u]
                    kind, n, h = un['kind'], un['n'], un['h']
                    pe.wait_ge(fill_out, un['last_fill'] - (un['nb'] - 1) // 4 + blocks[0] // 4 + 1)
                    rows = slice(64 * (h % 2), 64 * (h % 2) + 64)
                    at = 256 * (n % 2) + P * (h // 2)
                    out = bank[7][rows, at:at + P]
                    t = n + NT * (kind != 'swa')
                    first = blocks[0] == 0 and kind != 'sel'
                    if first and h == 0 and t:
                        pe.wait_ge(tile_out, t)
                    if first and kind == 'win':
                        pe.matmul(out, v_cmp[0:NCMP, :], p_cmp_t[0:NCMP, n, h, :], start=True, stop=False)
                    cols = {'swa': slice(64 * (h // 2), 64 * (h // 2) + 64), 'sel': slice(0, 64),
                            'win': slice(64, 128)}[kind]
                    vals = swa_v if kind == 'swa' else vsvw
                    for b in blocks:
                        ins = pe.matmul(out, vals[:, un['b0'] + b, cols], w_t3[:, i % 2, b % 4, :],
                                        start=(b == 0 and kind == 'swa'), stop=(b == un['nb'] - 1 and kind != 'win'))
                    ins.then_inc(pv_done, 1)

        @block.scalar
        def _(act):
            order = Order(act, act_order)
            stored = [0, 0]

            def split(c):
                act.wait_ge(w_in_s[c % 2], raw_total(c))
                if c >= 2:
                    act.wait_ge(half_done, 2 * (c - 2) + 2)
                act.activation(w_hi[:, c % 2, :, :], w_raw[:, c % 2, :, :], ACT.Copy).then_inc(w_hi_ready, 1)

            def half(c, h):
                kind, i, _ = CHUNKS[c]
                act.wait_ge(half_done, 2 * c + h + 1)
                if kind == 'merge':
                    m = gate_index[c] * 2 + h
                    if m >= 2:
                        act.wait_ge(gate_stored[m % 2], 16 * (m // 2))
                    order.after(act.activation(gate_out[:, m % 2, :], bank[h][:, :], ACT.Tanh, scale=0.5))
                    act.nop().then_inc(half_out, 1)
                    act.dma_start(gates[i[0], i[1], :, h * HALF:(h + 1) * HALF], gate_out[:, m % 2, :]
                                  ).then_inc(gate_stored[m % 2], 16)
                    return
                if h == 0:
                    if (kind, i) == ('ret_q', 0):
                        act.wait_ge(x_t, 16)
                    if (kind, i) == ('ret_q', 1):
                        act.wait_ge(conv_stored, 16)
                    if (kind, i) == ('swa_q', 0):
                        act.wait_ge(ret_stored, 16)
                    if (kind, i) == ('nsa_q', 0):
                        act.wait_ge(ret_stored, 32)
                f, kw = (ACT.Tanh, dict(scale=0.5)) if kind in ('conv_gate', 'gate') else (ACT.Copy, {})
                act.activation(home(c, h), bank[h][:, :], f, **kw).then_inc(half_out, 1)

            gate_index = {c: g for g, c in enumerate(c for c in range(NCH) if CHUNKS[c][0] == 'merge')}
            for item in SCHEDULE:
                what = item[0]
                if what == 'xt' and item[1] in (4, 6):
                    split(item[1] // 2 - 2)
                if what == 'mm':
                    q = item[1]
                    c, h = q // 4, q // 2 % 2
                    if q % 2 == 1:
                        half(c, h)
                        if h == 1 and c + 2 < NCH:
                            split(c + 2)
                elif what == 'xt':
                    g = item[1]
                    h, k = g // 8, g % 8
                    act.wait_ge(x_t, g + 1)
                    act.activation(x_hi[:, k, h * HALF:(h + 1) * HALF], bank[2 + g % 4][:, :], ACT.Copy
                                   ).then_inc(x_hi_ready, 1)
                elif what == 'conv_var':
                    act.wait_ge(eps_ready, 1)
                    act.wait_ge(conv_var_done, 1)
                    for h in range(2):
                        ins = act.activation(conv_r[:, h * HALF:(h + 1) * HALF], bank[4 + h][:, :], ACT.Sqrt,
                                             bias=eps[:, 0:1])
                    ins.then_inc(conv_sd, 1)
                elif what == 'conv_out':
                    act.wait_ge(conv_norm, 1)
                    act.activation(conv_gate, conv_y, ACT.Tanh).then_inc(conv_th, 1)
                elif what == 'ret_a':
                    pair, n = item[1:]
                    i = NT * pair + n
                    s, T = i % 2, bank[2 + 3 * (i % 2)]
                    act.wait_ge(ret_a_done, i + 1)
                    if i >= 2:
                        act.wait_ge(ret_b_done, i - 1)
                    act.activation(v_n[:, s, :, :], T[:, 0:2 * P], ACT.Copy)
                    act.activation(RET[pair]['g'][:, :, n * P:(n + 1) * P],
                                   T[:, 2 * P:4 * P].rearrange('p (e c) -> p e c', e=2), ACT.Copy).then_inc(ret_v_out, 1)
                elif what == 'ret_norm':
                    pair = item[1]
                    act.wait_ge(ret_v_out, NT * (pair + 1))
                    act.activation(RET[pair]['th'], RET[pair]['g'], ACT.Tanh, scale=0.5).then_inc(ret_th, 1)
                    act.wait_ge(ret_mv, pair + 1)
                    act.activation(o_rstd[:, :], o_mv[:, :, 1], ACT.Sqrt, bias=eps[:, 0:1]).then_inc(ret_sd, 1)
                elif what == 'fill':
                    f, kind, a = item[1:]
                    B = bank[6]
                    act.wait_ge(fill_done, f + 1)
                    if kind == 'ret':
                        pair, g = a
                        out, src = RET[pair]['out'][:, g // 2, HALF * (g % 2):HALF * (g % 2) + HALF], B[:, :]
                    elif kind in ('swa_v', 'vsvw'):
                        out, src = (swa_v if kind == 'swa_v' else vsvw)[:, 4 * a[0]:4 * a[0] + 4, :], B[:, :]
                    elif kind == 'gate':
                        act.activation(gate_n[:, :, :], B[:, 0:96].rearrange('p (n g) -> p n g', n=NT), ACT.Copy, scale=0.5,
                                       bias=0.5).then_inc(fill_out, 1)
                        continue
                    elif kind == 'pe':
                        out, src = pe_t[:, :], B[:, 0:32]
                    elif kind == 'cmp':
                        if a[0] == 0:
                            act.wait_ge(hid_done, 1)
                        out, src = p_cmp_t[0:NCMP, a[0], :, :], B[0:NCMP, :]
                    else:
                        _, blocks, i = a
                        if i >= 2:
                            act.wait_ge(pv_done, i - 1)
                        out, src = w_t[:, i % 2, 0:len(blocks) * P], B[:, 0:len(blocks) * P]
                    act.activation(out, src, ACT.Copy).then_inc(fill_out, 1)
                elif what == 'out':
                    kind, n = item[1:]
                    t = n + NT * (kind != 'swa')
                    last = (SWA[4 * n + 3] if kind == 'swa' else NSA[8 * n + 7])['last_pv']
                    act.wait_ge(pv_done, last + 1)
                    if t >= 2:
                        act.wait_ge(tile_stored[n % 2], 16 * (t // 2))
                    act.activation(out_t[:, n % 2], bank[7][:, 256 * (n % 2):256 * (n % 2) + 256], ACT.Copy
                                   ).then_inc(tile_out, 1)
                elif what == 'exp':
                    un = UNITS[item[1]]
                    u, s, L = un['u'], un['u'] % 3, un['nb'] * P
                    act.wait_ge(max_done, u + 1)
                    if u >= 3:
                        act.wait_ge(soft_done, u - 2)
                    if un['kind'] == 'swa':
                        act.activation(e_sink[:, s:s + 1], sink8[:, un['h']:un['h'] + 1], ACT.Exp, scale=0.125,
                                       bias=m_neg[:, s:s + 1])
                    act.activation(soft[:, s, 0:L], soft[:, s, 0:L], ACT.Exp, scale=0.125, bias=m_neg[:, s:s + 1],
                                   accum_out=den[:, s:s + 1]).then_inc(exp_done, 1)
                elif what == 'hidden':
                    act.wait_ge(hid_done, 1)
                    for kv in range(2):
                        ins = act.activation(hid_n[0:NCMP, kv, :], bank[2 + 3 * kv][0:NCMP, 0:CMP_HID], ACT.Gelu)
                    ins.then_inc(hid_gelu, 1)
                elif what == 'hidden_t':
                    act.wait_ge(hid_t_done, 1)
                    act.activation(hid[:, :, 0:NCMP],
                                   bank[2][:, 0:256].rearrange('p (j c) -> p j c', j=4)[:, :, 0:NCMP], ACT.Copy
                                   ).then_inc(hid_out, 1)
                elif what == 'compress':
                    act.wait_ge(cmp_done, 1)
                    act.activation(k_cmp[:, 0:NCMP], bank[3][:, 0:NCMP], ACT.Copy)
                    act.activation(v_cmp[0:NCMP, :], bank[4][0:NCMP, 0:DH], ACT.Copy).then_inc(cmp_out, 1)
                elif what == 'cmp_score':
                    n = item[1]
                    act.wait_ge(cmax_done, n + 1)
                    act.activation(cs[:, n % 2, :, :], cs[:, n % 2, :, :], ACT.Exp, scale=0.125).then_inc(cexp_done, 1)
            for i in range(2):
                act.wait_ge(gate_stored[i], 16 * len(gate_index))

        @block.vector
        def _(dve):
            order = Order(dve, dve_order)

            def split(c):
                dve.wait_ge(w_hi_ready, c + 1)
                dve.tensor_tensor(w_lo[:, c % 2, :, :], w_raw[:, c % 2, :, :], w_hi[:, c % 2, :, :].bitcast(F32),
                                  ALU.subtract).then_inc(w_lo_ready, 1)

            dve.memset(eps[:, :], EPS).then_inc(eps_ready, 1)
            dve.memset(state[:, :, :], 0.0).then_inc(state_zero, 1)
            order.after(dve.memset(conv_h[:, :, 0:CONV_K - 1], 0.0))
            for item in SCHEDULE:
                what = item[0]
                if what == 'xt' and item[1] in (4, 6):
                    split(item[1] // 2 - 2)
                if what == 'mm':
                    q = item[1]
                    if q % 4 == 3 and q // 4 + 2 < NCH:
                        split(q // 4 + 2)
                elif what == 'xt':
                    g = item[1]
                    h, k = g // 8, g % 8
                    cols = slice(h * HALF, (h + 1) * HALF)
                    dve.wait_ge(x_hi_ready, g + 1)
                    dve.tensor_tensor(x_lo[:, k, cols], bank[2 + g % 4][:, :], x_hi[:, k, cols].bitcast(F32),
                                      ALU.subtract).then_inc(x_lo_ready, 1)
                elif what == 'conv_h':
                    dve.wait_ge(conv_params, 1)
                    order.after(dve.tensor_copy(conv_p[:, :, :], bank[6][:, 0:68].rearrange('p (c k) -> p c k', c=2)))
                    order.after(dve.tensor_scalar(conv_p[:, :, 0:31], conv_p[:, :, 0:31], 0.5, None, ALU.mult))
                    order.after(dve.tensor_scalar(conv_p[:, :, 32:34], conv_p[:, :, 32:34], 0.5, None, ALU.mult))
                    dve.wait_ge(half_out, 2 * WHERE['conv_a', 1] + 2)
                    for c in range(2):
                        body = conv_h[:, c, CONV_K - 1:]
                        order.after(dve.scalar_tensor_tensor(body, conv_gate[:, c, :], 1.0, body, ALU.add, ALU.mult))
                elif what == 'tap':
                    k = item[1]
                    for c in range(2):
                        if k == 0:
                            ins = dve.tensor_scalar(conv_y[:, c, :], conv_h[:, c, 0:S], conv_p[:, c, 0:1],
                                                    conv_p[:, c, 31:32], ALU.mult, ALU.add)
                        else:
                            dve.wait_ge(taps_done, 2 * k - 1 + c)
                            ins = dve.scalar_tensor_tensor(conv_y[:, c, :], conv_h[:, c, k:k + S], conv_p[:, c, k:k + 1],
                                                           conv_y[:, c, :], ALU.mult, ALU.add)
                        ins.then_inc(taps_done, 1)
                elif what == 'conv_mean':
                    dve.wait_ge(conv_mean_done, 1)
                    for h in range(2):
                        cols = slice(h * HALF, (h + 1) * HALF)
                        order.after(dve.tensor_tensor(conv_y[:, :, cols], conv_y[:, :, cols],
                                                      bcast(bank[2 + h][:, :], 1, 2), ALU.subtract))
                    dve.tensor_tensor(conv_gate, conv_y, conv_y, ALU.mult).then_inc(conv_sq, 1)
                elif what == 'conv_var':
                    dve.wait_ge(conv_sd, 1)
                    order.after(dve.reciprocal(conv_r, conv_r))
                    order.after(dve.tensor_tensor(conv_y, conv_y, bcast(conv_r, 1, 2), ALU.mult))
                    for c in range(2):
                        ins = dve.tensor_scalar(conv_y[:, c, :], conv_y[:, c, :], conv_p[:, c, 32:33],
                                                conv_p[:, c, 33:34], ALU.mult, ALU.add)
                    ins.then_inc(conv_norm, 1)
                elif what == 'conv_out':
                    dve.wait_ge(conv_th, 1)
                    dve.wait_ge(conv_norm, 1)
                    dve.scalar_tensor_tensor(conv_y, conv_gate, 1.0, conv_y, ALU.add, ALU.mult).then_inc(conv_fin, 1)
                elif what == 'ret_a':
                    pair, n = item[1:]
                    i = NT * pair + n
                    s, R, K = i % 2, RET[pair], bank[3 + 3 * (i % 2)]
                    dve.wait_ge(ret_a_done, i + 1)
                    if i >= 2:
                        dve.wait_ge(ret_b_done, i - 1)
                    for e, src in enumerate((K[:, P:2 * P], bank[4 + 3 * s][:, 3 * P:4 * P])):
                        dve.tensor_tensor(inner[:, s, e, :], src,
                                          const('decay')[:, (2 * pair + e) * P:(2 * pair + e + 1) * P], ALU.mult)
                    dve.tensor_tensor(k_z[:, s, :].rearrange('p (e c) -> p e c', e=2),
                                      K[:, 0:P].rearrange('p (e c) -> p e c', e=2),
                                      bcast(const('zeta')[:, 2 * pair:2 * pair + 2], 2, 64), ALU.mult)
                    dve.tensor_tensor(q_xi[:, s, :], R['q'][:, n * P:(n + 1) * P],
                                      const('xi')[:, pair * P:(pair + 1) * P], ALU.mult).then_inc(ret_mid, 1)
                elif what == 'ret_b':
                    pair, n = item[1:]
                    i = NT * pair + n
                    R, O = RET[pair], bank[4 + 3 * (i % 2)]
                    dve.wait_ge(ret_b_done, i + 1)
                    kv = O[:, 2 * P:3 * P]
                    if n == NT - 1:
                        dve.memset(state[:, :, :], 0.0)
                    else:
                        for e in range(2):
                            rows = slice(64 * e, 64 * e + 64)
                            dve.scalar_tensor_tensor(state[rows, e, :], state[rows, e, :],
                                                     const('chunk_decay')[rows, pair:pair + 1], kv[rows, :],
                                                     ALU.mult, ALU.add)
                    for e in range(2):
                        dve.bn_stats(o_stats[:, e * NT + n, :], O[:, e * P:(e + 1) * P])
                    dve.tensor_copy(R['v'][:, :, n * P:(n + 1) * P],
                                    O[:, 0:2 * P].rearrange('p (e c) -> p e c', e=2)).then_inc(ret_state, 1)
                elif what == 'ret_norm':
                    pair = item[1]
                    R = RET[pair]
                    dve.wait_ge(ret_state, NT * (pair + 1))
                    for j in range(16):
                        ins = dve.bn_aggr(o_mv[:, j, :], o_stats[:, j, :])
                    ins.then_inc(ret_mv, 1)
                    if pair == 0:
                        dve.wait_ge(gn_in, 32)
                        order.after(dve.tensor_scalar(reg_s[:, 2048:3072], reg_s[:, 2048:3072], 0.5, None, ALU.mult))
                    dve.wait_ge(ret_sd, pair + 1)
                    order.after(dve.reciprocal(o_rstd[:, :], o_rstd[:, :]))
                    for e in range(2):
                        for n in range(NT):
                            j, blk = e * NT + n, R['v'][:, e, n * P:(n + 1) * P]
                            ins = dve.tensor_scalar(blk, blk, o_mv[:, j, 0:1], o_rstd[:, j:j + 1], ALU.subtract,
                                                    ALU.mult)
                    order.after(ins)
                    per = lambda ap: ap.rearrange('p (n c) -> p n c', c=P)
                    for table, op in ((gn_g, ALU.mult), (gn_b, ALU.add)):
                        for e in range(2):
                            o = per(R['v'][:, e, :])
                            ins = dve.tensor_tensor(o, o, bcast(table[:, 2 * pair + e, :], 1, NT), op)
                        order.after(ins)
                    dve.wait_ge(ret_th, pair + 1)
                    order.after(dve.scalar_tensor_tensor(R['g'], R['th'], 1.0, R['g'], ALU.add, ALU.mult))
                    dve.tensor_tensor(R['v'], R['v'], R['g'], ALU.mult).then_inc(ret_fin, 1)
                elif what == 'sel_table':
                    n = item[1]
                    order.after(dve.tensor_tensor(
                        dist_n[:, 0:(n + 1) * P].rearrange('p (b l) -> p b l', l=SLC),
                        const('dist_sel')[:, 896 - P * n:1024].rearrange('p (b l) -> p b l', l=SLC),
                        bcast(sel_pen[:, n, 0:2 * n + 2], 2, SLC), ALU.add))
                elif what == 'max':
                    un = UNITS[item[1]]
                    kind, u, n, h, s, L = un['kind'], un['u'], un['n'], un['h'], un['u'] % 3, un['nb'] * P
                    if u == 0:
                        order.after(dve.tensor_scalar(sink8[:, :], sink8[:, :], 8.0, None, ALU.mult))
                    table = {'swa': const('dist_swa'), 'win': const('dist_win'), 'sel': dist_n[:, 0:L]}[kind]
                    table = table[:, table.shape[1] - L:]
                    slope = (SLOPE_SWA if kind == 'swa' else SLOPE_NSA)[h]
                    dve.wait_ge(score_done, u + 1)
                    if u >= 3:
                        dve.wait_ge(fill_done, UNITS[u - 3]['last_fill'] + 1)
                    for at in range(0, L, HALF):
                        w = min(HALF, L - at)
                        ins = dve.scalar_tensor_tensor(soft[:, s, at:at + w], table[:, at:at + w], -8.0 * slope,
                                                       bank[2 + 2 * (u % 2) + at // HALF][:, 0:w], ALU.mult, ALU.add)
                    order.after(ins)
                    order.after(dve.reduce_max(m_raw[:, s:s + 1], soft[:, s, 0:L], AX.X))
                    if kind == 'swa':
                        dve.tensor_scalar(m_neg[:, s:s + 1], m_raw[:, s:s + 1], sink8[:, h:h + 1], -0.125, ALU.max,
                                          ALU.mult).then_inc(max_done, 1)
                    else:
                        dve.tensor_scalar(m_neg[:, s:s + 1], m_raw[:, s:s + 1], -0.125, None, ALU.mult
                                          ).then_inc(max_done, 1)
                elif what == 'norm':
                    un = UNITS[item[1]]
                    kind, u, n, h, s, L = un['kind'], un['u'], un['n'], un['h'], un['u'] % 3, un['nb'] * P
                    dve.wait_ge(exp_done, u + 1)
                    if kind == 'swa':
                        order.after(dve.tensor_scalar(den[:, s:s + 1], den[:, s:s + 1], e_sink[:, s:s + 1], 1e-30,
                                                      ALU.add, ALU.max))
                    else:
                        order.after(dve.tensor_scalar(den[:, s:s + 1], den[:, s:s + 1], 1e-30, None, ALU.max))
                    order.after(dve.reciprocal(rden[:, s:s + 1], den[:, s:s + 1]))
                    if kind == 'swa':
                        dve.tensor_scalar(soft[:, s, 0:L], soft[:, s, 0:L], rden[:, s:s + 1], None, ALU.mult
                                          ).then_inc(soft_done, 1)
                    else:
                        col = 4 * (2 if kind == 'win' else 1) + h
                        dve.tensor_scalar(soft[:, s, 0:L], soft[:, s, 0:L], rden[:, s:s + 1], gate_n[:, n, col:col + 1],
                                          ALU.mult, ALU.mult).then_inc(soft_done, 1)
                elif what == 'fill' and item[2] == 'pe':
                    dve.wait_ge(fill_out, item[1] + 1)
                    src = kcvc.rearrange('p (i l) -> p l i', l=CMP_STRIDE)
                    for part in range(2):
                        rows = slice(CMP_STRIDE * part, CMP_STRIDE * (part + 1))
                        dve.tensor_tensor(z_cmp[:, rows, 0:NCMP], src[:, :, part:part + NCMP],
                                          bcast(pe_t[:, rows], 2, NCMP), ALU.add).then_inc(z_ready, 1)
                elif what == 'cmp_score':
                    n = item[1]
                    t = cs[:, n % 2, :, :]
                    if n == 0:
                        order.after(dve.memset(c_all[:, :], 0.0))
                    dve.wait_ge(cscore_done, n + 1)
                    if n >= 2:
                        dve.wait_ge(fill_done, CMP_FILL + n - 1)
                    for h in range(4):
                        B = bank[2 + 2 * (n % 2) + h % 2]
                        ins = dve.scalar_tensor_tensor(cs[:, n % 2, h, :], const('dist_cmp')[:, n * NCMP:(n + 1) * NCMP],
                                                       -8.0 * SLOPE_NSA[h], B[:, h * 64:h * 64 + NCMP], ALU.mult, ALU.add)
                    order.after(ins)
                    order.after(dve.reduce_max(c_max[:, :], t, AX.X))
                    dve.tensor_tensor(t, t, bcast(c_max[:, :], 2, NCMP), ALU.subtract).then_inc(cmax_done, 1)
                    dve.wait_ge(cexp_done, n + 1)
                    order.after(dve.tensor_tensor(t, t, bcast(const('mask_cmp')[:, n * NCMP:(n + 1) * NCMP], 1, 4), ALU.mult))
                    order.after(dve.reduce_sum(c_sum[:, :], t, AX.X))
                    order.after(dve.tensor_scalar(c_sum[:, :], c_sum[:, :], 1e-30, None, ALU.max))
                    order.after(dve.reciprocal(c_sum[:, :], c_sum[:, :]))
                    order.after(dve.tensor_tensor(t, t, bcast(c_sum[:, :], 2, NCMP), ALU.mult))
                    order.after(dve.reduce_sum(c_all[:, 1:64], t.rearrange('p h c -> p c h'), AX.X))
                    order.after(dve.reduce_sum(imp[:, :], c_all[:, 1:65].rearrange('p (j c) -> p j c', c=4), AX.X))
                    order.after(dve.tensor_tensor(imp[:, :], imp[:, :],
                                                  c_all[:, 0:64].rearrange('p (j c) -> p j c', c=4)[:, :, 0], ALU.add))
                    order.after(dve.tensor_tensor(imp[:, :], imp[:, :], const('imp_keep')[:, n * NSLC:(n + 1) * NSLC],
                                                  ALU.mult))
                    order.after(dve.tensor_tensor(imp[:, :], imp[:, :], const('imp_set')[:, n * NSLC:(n + 1) * NSLC],
                                                  ALU.add))
                    order.after(dve.max(imp_top[:, :], imp[:, :]))
                    order.after(dve.match_replace(imp_cut[:, :], imp_top[:, :], imp[:, :], NEG))
                    order.after(dve.tensor_scalar(sel_pen[:, n, :], imp_cut[:, :], NEG, BIG, ALU.not_equal, ALU.mult))
                    dve.tensor_tensor(t, t, bcast(gate_n[:, n, 0:4], 2, NCMP), ALU.mult).then_inc(csoft_done, 1)


CMP_FILL = next(item[1] for item in SCHEDULE if item[0] == 'fill' and item[2] == 'cmp')


def merge_and_project(nc, d, yt, gates, x1d, x1_n, x1_t, logits, scratch, sem):
    SPLIT = [(0, 2), (2, 4), (4, 8), (8, 10)]
    with ExitStack() as ctx:
        def sb(name, shape, dt=F32):
            return ctx.enter_context(nc.sbuf_tensor(name, shape, dt))
        merged, w_out = sb('merged', [P, KD, S]), sb('w_out_sb', [P, KD, D])
        y_sb = scratch[:, 0:10240].rearrange('p (c s) -> p c s', s=S)
        g_sb = scratch[:, 10240:18432].rearrange('p (r b s) -> p r b s', r=2, b=4)
        p_sb = sb('p_sb', [P, 2, 10, P])
        term = sb('term', [P, 2, HALF])
        x_row, g1, b1 = sb('x_row', [P, 2, D]), sb('g1', [P, D]), sb('b1', [P, D])
        r_nat, r_t = sb('r_nat', [E, D]), sb('r_t', [P, KD, E])
        stats, mv, sd = sb('ln_stats', [P, 2, 2, 6]), sb('ln_mv', [P, 2, 2]), sb('ln_sd', [P, 2])
        ident, eps = sb('b_ident', [P, P]), sb('b_eps', [P, 1])
        bank = [ctx.enter_context(nc.psum_tensor(f'b_bank{i}', [P, HALF], F32)) for i in range(8)]

        y_in, wo_in, ln_in, id_in = sem('y_in'), sem('wo_in'), sem('ln_in'), sem('id_in')
        p_in, g_in, x_in = ([sem(f'{n}{i}') for i in range(2)] for n in ('p_in', 'g_in', 'xr_in'))
        y_done, half_merged = sem('y_done'), sem('half_merged')
        r_tr, r_ready, b_order, eps_set = sem('r_tr'), sem('r_ready'), sem('b_order'), sem('b_eps_set')
        mix_done, xa_ready, mv_done, sd_done, pre_read, x1_done = (sem('mix_done'), sem('xa_ready'), sem('mv_done'),
                                                                   sem('sd_done'), sem('pre_read'), sem('x1_done'))
        x1_tr, x1_t_out, router_done, x1_stored = sem('x1_tr'), sem('x1_t_out'), sem('router_done'), sem('x1_stored')
        block = ctx.enter_context(nc.Block())

        @block.sync
        def _(sp):
            sp.dma_start(ident[:, :], d['ident']).then_inc(id_in, 16)
            sp.dma_start(r_nat[:, :], d['router_w'][0]).then_inc(id_in, 16)
            for j in range(KD):
                cols = slice(j * P, (j + 1) * P)
                if j >= 2:
                    sp.wait_ge(y_done, 8 * (j - 1))
                for (a, b), name in zip(SPLIT, ('p_conv', 'p_swa', 'p_ret', 'p_nsa')):
                    sp.dma_start(p_sb[:, j % 2, a:b, :], d[name][0, :, cols].rearrange('(c p) n -> p c n', p=P)
                                 ).then_inc(p_in[j % 2], 16)
                if j == 0:
                    for a, b in SPLIT:
                        sp.dma_start(y_sb[:, a:b, :], yt[a:b].rearrange('c p s -> p c s')).then_inc(y_in, 16)
                if j >= 2:
                    sp.wait_ge(half_merged, 2 * (j - 1))
                sp.dma_start(g_sb[:, j % 2, :, :], gates[j].rearrange('b p s -> p b s')).then_inc(g_in[j % 2], 16)
                if j == 1:
                    sp.dma_start(w_out[:, :, :], d['w_out'][0].rearrange('(k p) n -> p k n', p=P)).then_inc(wo_in, 16)
                    sp.dma_start(g1[:, :], d['ln1_g'].broadcast_to([P, D])).then_inc(ln_in, 16)
                    sp.dma_start(b1[:, :], d['ln1_b'].broadcast_to([P, D])).then_inc(ln_in, 16)
            for t in range(NT):
                if t >= 2:
                    sp.wait_ge(pre_read, t - 1)
                sp.dma_start(x_row[:, t % 2, :], d['x'][0, t * P:(t + 1) * P, :]).then_inc(x_in[t % 2], 16)
                if t >= 2:
                    sp.wait_ge(x1_done, t - 1)
                    sp.dma_start(x1d[(t - 2) * P:(t - 1) * P, :], x1_n[:, t - 2, :]).then_inc(x1_stored, 16)
            for t in (NT - 2, NT - 1):
                sp.wait_ge(x1_done, t + 1)
                sp.dma_start(x1d[t * P:(t + 1) * P, :], x1_n[:, t, :]).then_inc(x1_stored, 16)
            sp.wait_ge(x1_stored, 16 * NT)

        @block.tensor
        def _(pe):
            pe.wait_ge(id_in, 32)
            for k in range(KD):
                ins = pe.transpose(bank[7][:, k * E:(k + 1) * E], r_nat[:, k * P:(k + 1) * P], ident[0:E, 0:E])
            ins.then_inc(r_tr, 1)
            pe.wait_ge(r_ready, 1)
            pe.wait_ge(y_in, 64)
            for j in range(KD):
                pe.wait_ge(p_in[j % 2], 64 * (j // 2 + 1))
                for h in range(2):
                    if j:
                        pe.wait_ge(half_merged, 2 * j + h - 1)
                    for b, (lo, hi) in enumerate(SPLIT):
                        for c in range(lo, hi):
                            ins = pe.matmul(bank[4 * h + b][:, :], p_sb[:, j % 2, c, :],
                                            y_sb[:, c, h * HALF:(h + 1) * HALF], start=c == lo, stop=c == hi - 1)
                        ins.then_inc(y_done, 1)

            def rows_out(t):
                if t >= 2:
                    pe.wait_ge(pre_read, t - 1)
                for h in range(2):
                    for k in range(KD):
                        ins = pe.matmul(bank[2 * (t % 2) + h][:, :], merged[:, k, t * P:(t + 1) * P],
                                        w_out[:, k, h * HALF:(h + 1) * HALF], start=k == 0, stop=k == KD - 1)
                ins.then_inc(mix_done, 1)
            pe.wait_ge(half_merged, 2 * KD)
            pe.wait_ge(wo_in, 16)
            rows_out(0)
            for t in range(NT):
                if t + 1 < NT:
                    rows_out(t + 1)
                pe.wait_ge(x1_done, t + 1)
                if t:
                    pe.wait_ge(x1_t_out, t)
                for k in range(KD):
                    ins = pe.transpose(bank[4 + k // 4][:, (k % 4) * P:(k % 4 + 1) * P], x1_n[:, t, k * P:(k + 1) * P],
                                       ident[:, :])
                ins.then_inc(x1_tr, 1)
                pe.wait_ge(x1_t_out, t + 1)
                for k in range(KD):
                    ins = pe.matmul(bank[6][:, t * E:(t + 1) * E], x1_t[:, k, t * P:(t + 1) * P], r_t[:, k, :],
                                    start=k == 0, stop=k == KD - 1)
            ins.then_inc(router_done, 1)

        @block.scalar
        def _(act):
            act.wait_ge(r_tr, 1)
            act.activation(r_t[:, :, :], bank[7][:, :].rearrange('p (k e) -> p k e', e=E), ACT.Copy).then_inc(r_ready, 1)
            act.wait_ge(eps_set, 1)

            def scaled(t):
                act.wait_ge(x_in[t % 2], 16 * (t // 2 + 1))
                act.activation(x_row[:, t % 2, :], x_row[:, t % 2, :], ACT.Copy, scale=ALPHA).then_inc(xa_ready, 1)
            scaled(0)
            for t in range(NT):
                if t + 1 < NT:
                    scaled(t + 1)
                act.wait_ge(mv_done, t + 1)
                act.activation(sd[:, t % 2:t % 2 + 1], mv[:, t % 2, 1:2], ACT.Sqrt, bias=eps[:, 0:1]).then_inc(sd_done, 1)
                act.wait_ge(x1_tr, t + 1)
                for h in range(2):
                    ins = act.activation(x1_t[:, 4 * h:4 * h + 4, t * P:(t + 1) * P],
                                         bank[4 + h][:, :].rearrange('p (k c) -> p k c', k=4), ACT.Copy)
                ins.then_inc(x1_t_out, 1)
            act.wait_ge(router_done, 1)
            act.activation(logits[:, :, :], bank[6][:, :].rearrange('p (n e) -> p n e', e=E), ACT.Sigmoid
                           ).then_inc(r_ready, 1)
            act.wait_ge(r_ready, 2)

        @block.vector
        def _(dve):
            order = Order(dve, b_order)
            dve.memset(eps[:, :], EPS).then_inc(eps_set, 1)
            for j in range(KD):
                dve.wait_ge(g_in[j % 2], 16 * (j // 2 + 1))
                for h in range(2):
                    cols = slice(h * HALF, (h + 1) * HALF)
                    total = merged[:, j, cols]
                    for b in range(4):
                        dve.wait_ge(y_done, 8 * j + 4 * h + b + 1)
                        out = total if b == 0 else term[:, b % 2, :]
                        order.after(dve.scalar_tensor_tensor(out, g_sb[:, j % 2, b, cols], 1.0, bank[4 * h + b][:, :],
                                                             ALU.add, ALU.mult))
                        if b:
                            ins = dve.tensor_tensor(total, total, out, ALU.add)
                            if b < 3:
                                order.after(ins)
                    ins.then_inc(half_merged, 1)
            dve.wait_ge(half_merged, 2 * KD)
            dve.wait_ge(ln_in, 32)
            for t in range(NT):
                s, row = t % 2, x1_n[:, t, :]
                dve.wait_ge(mix_done, t + 1)
                dve.wait_ge(xa_ready, t + 1)
                for h in range(2):
                    cols = slice(h * HALF, (h + 1) * HALF)
                    ins = dve.scalar_tensor_tensor(x1_n[:, t, cols], bank[2 * s + h][:, :], 0.5, x_row[:, s, cols],
                                                   ALU.mult, ALU.add)
                ins.then_inc(pre_read, 1)
                dve.wait_ge(pre_read, t + 1)
                for h in range(2):
                    ins = dve.bn_stats(stats[:, s, h, :], x1_n[:, t, h * HALF:(h + 1) * HALF])
                order.after(ins)
                dve.bn_aggr(mv[:, s, :], stats[:, s, :, :]).then_inc(mv_done, 1)
                dve.wait_ge(sd_done, t + 1)
                order.after(dve.reciprocal(sd[:, s:s + 1], sd[:, s:s + 1]))
                order.after(dve.tensor_scalar(row, row, mv[:, s, 0:1], sd[:, s:s + 1], ALU.subtract, ALU.mult))
                order.after(dve.tensor_tensor(row, row, g1[:, :], ALU.mult))
                dve.tensor_tensor(row, row, b1[:, :], ALU.add).then_inc(x1_done, 1)


def experts(nc, d, c_ap, c_at, x1d, acc, x1_n, x1_t, scores, scratch, out, sem):
    with ExitStack() as ctx:
        def sb(name, shape, dt=F32):
            return ctx.enter_context(nc.sbuf_tensor(name, shape, dt))
        cst = sb('e_const', [P, c_ap.shape[1]])

        def const(name):
            at, width = c_at[name]
            return cst[:, at:at + width]
        ident = const('ident')
        w_gu, w_d = sb('w_gu', [P, 2, 2, KD, FE]), sb('w_d', [P, 2, 2, D])
        s_gu, s_d = sb('s_gu', [P, KD, 2 * FE]), sb('s_d', [P, 2, D])
        area = sb('area', [P, 8192])
        w4 = lambda i: area[:, 2048 * i:2048 * (i + 1)].rearrange('p (s c) -> p s c', s=2)
        x_g, y_out = w4(0), w4(2)
        x_gt = area[:, 2048:4096].rearrange('p (s k c) -> p s k c', s=2, c=P)
        one_hot = sb('one_hot', [P, 2, NT, P], BF16)
        r3 = lambda i, w=E: area[:, 512 * i:512 * i + NT * w].rearrange('p (n e) -> p n e', n=NT)
        r4 = lambda i: area[:, 512 * i:512 * (i + 1)].rearrange('p (n g h) -> p n g h', n=NT, g=NG)
        biased, t8, t_gt, t_ge = r3(0), r4(1), r4(2), r4(3)
        cand, cut = r3(4, E + 2), r3(6, E + 2)
        mask, run = r3(8), r3(9)
        gate_w, cmp8 = r3(10), r4(11)
        gs, keep = sb('gs', [P, NT, NG]), sb('keep', [P, NT, NG])
        top = sb('top', [P, NT, 8])
        g_sum = sb('g_sum', [P, NT])
        rb = sb('rb', [P, E])
        pos = sb('pos', [P, NT, E])
        info = sb('info', [P, NT, E, 6], BF16)
        n_blk, end_blk, le = sb('n_blk', [P, E]), sb('end_blk', [P, E]), sb('le', [P, E])
        ek = sb('ek', [P, 4])
        table = sb('table', [1, 2 * MAXB + 1], I32)
        hidden, silu, u_sb, hid_t = sb('hidden', [P, 2, FE]), sb('silu', [P, 2, FE]), sb('u_sb', [P, 2, FE]), sb('hid_t', [P, 2, P])
        found, idx_f = sb('found', [P, 2, 6]), sb('idx_f', [P, 1])
        row_gate = sb('row_gate', [P, 4])
        idx_kept, idx, idx_out = sb('idx_kept', [P, 2], I32), sb('idx', [P, 2], I32), sb('idx_out', [P, 2], I32)
        s_row, s_acc = area[:, 6144:8192].rearrange('p (s d) -> p s d', s=2), scratch[:, 2 * NT * D:2 * NT * D + 2 * D].rearrange('p (s d) -> p s d', s=2)
        zero = s_row[:, 0, :]
        g2, b2 = s_gu[:, 0:2, :].rearrange('p a b -> p (a b)'), s_gu[:, 2:4, :].rearrange('p a b -> p (a b)')
        stats, mv, sd, eps = sb('ln2_stats', [P, 2, 2, 6]), sb('ln2_mv', [P, 2, 2]), sb('ln2_sd', [P, 2]), sb('e_eps', [P, 1])
        rows2 = x1_t[:, :, :]
        bank = [ctx.enter_context(nc.psum_tensor(f'e_bank{i}', [P, HALF], F32)) for i in range(8)]

        in_const, sh_in, rb_in, zero_set = sem('e_const_in'), sem('sh_in'), sem('rb_in'), sem('zero_set')
        d_order, mask_done, pos_done, ek_done, tab_done, tab_ready, route_ready = (
            sem('d_order'), sem('mask_done'), sem('pos_done'), sem('ek_done'), sem('tab_done'), sem('tab_ready'),
            sem('route_ready'))
        s_gu_done, s_silu, s_h, s_ht, s_ht_out, s_down, s_y, s_acc_ready, s_a_order, s_p_order = (
            sem(n) for n in ('s_gu_done', 's_silu', 's_h', 's_ht', 's_ht_out', 's_down', 's_y', 's_acc_ready',
                             's_a_order', 's_p_order'))
        acc_in = [sem('acc_in0'), sem('acc_in1')]
        w_gu_in, w_d_in, gathered = ([sem(f'{n}{i}') for i in range(2)] for n in ('w_gu_in', 'w_d_in', 'gathered'))
        oh_ready, idx_done, idx_ready, xt_done, xgt_ready, gu_done, sg_ready, h_ready, ht_done, ht_ready, down_done, \
            y_act, y_dve, scattered, gathers, so_ready = (
                sem(n) for n in ('oh_ready', 'idx_done', 'idx_ready', 'xt_done', 'xgt_ready', 'gu_done', 'sg_ready',
                                 'h_ready', 'ht_done', 'ht_ready', 'down_done', 'y_act', 'y_dve', 'scattered', 'gathers', 'so_ready'))
        acc_row_in = [sem(f'acc_row_in{i}') for i in range(NT)]
        ln_in2, eps_set2, mv_done2, sd_done2, row_done, out_stored, f_order = (
            sem(n) for n in ('ln_in2', 'eps_set2', 'mv_done2', 'sd_done2', 'row_done', 'out_stored', 'f_order'))
        block = ctx.enter_context(nc.Block())
        CREDIT = ((gu_done, 2), (h_ready, 2), (ht_done, 2), (down_done, 2), (y_act, 1), (y_dve, 1), (xt_done, 1),
                  (ht_ready, 1))

        def trips(eng):
            eng.wait_ge(tab_ready, 1)
            return eng.value_load(table[0:1, 2 * MAXB:2 * MAXB + 1], min_val=1, max_val=MAXB // 2 - 4)

        def expert_of(eng, b):
            return eng.value_load(table[0:1, bass.ds(b, 1)], min_val=0, max_val=E - 1)

        @block.sync
        def _(sp):
            sp.dma_start(cst[:, :], c_ap).then_inc(in_const, 16)
            sp.dma_start(rb[:, :], d['router_b'].broadcast_to([P, E])).then_inc(rb_in, 16)
            for i, name in enumerate(('sh_wg', 'sh_wu')):
                sp.dma_start(s_gu[:, :, i * FE:(i + 1) * FE], d[name][0].rearrange('(k p) f -> p k f', p=P)).then_inc(sh_in, 16)
            sp.dma_start(s_d[:, :, :], d['sh_wd'][0].rearrange('(k p) n -> p k n', p=P)).then_inc(sh_in, 16)
            n = trips(sp)

            def load_up(blk, s):
                e = expert_of(sp, blk)
                sp.wait_ge(gu_done, blk + 1)
                for m, name in enumerate(('moe_wg', 'moe_wu')):
                    sp.dma_start(w_gu[:, s, m, :, :].rearrange('p k f -> p (k f)'),
                                 d[name][0, bass.ds(e, 1)].rearrange('a (p k) f -> p (a k f)', k=KD)
                                 ).then_inc(w_gu_in[s], 16)

            def load_down(blk, s):
                e = expert_of(sp, blk)
                sp.wait_ge(down_done, blk + 1)
                sp.dma_start(w_d[:, s, :, :].rearrange('p k f -> p (k f)'),
                             d['moe_wd'][0, bass.ds(e, 1)].rearrange('a (p k) f -> p (a k f)', k=2)
                             ).then_inc(w_d_in[s], 16)
            load_up(0, 0)
            with sp.Fori(0, n) as i:
                for s in range(2):
                    load_up(2 * i + s + 1, 1 - s)
                    load_down(2 * i + s, s)
            load_up(2 * n + 1, 1)
            for s in range(2):
                load_down(2 * n + s, s)
            sp.dma_start(g2, d['ln2_g'].broadcast_to([P, D])).then_inc(ln_in2, 16)
            sp.dma_start(b2, d['ln2_b'].broadcast_to([P, D])).then_inc(ln_in2, 16)
            sp.wait_ge(scattered, 32 * n + 64)
            for t in range(NT):
                sp.dma_start(rows2[:, t, :], acc[t * P:(t + 1) * P, :]).then_inc(acc_row_in[t], 16)
            for t in range(NT):
                sp.wait_ge(row_done, t + 1)
                sp.dma_start(out[0, t * P:(t + 1) * P, :], rows2[:, t, :]).then_inc(out_stored, 16)
            sp.wait_ge(out_stored, 16 * NT)

        @block.gpsimd
        def _(pool):
            pool.memset(zero, 0.0).then_inc(zero_set, 1)
            pool.wait_ge(zero_set, 1)
            pool.dma_start(acc[S:S + P, :], zero).then_inc(scattered, 16)
            pool.dma_start(x1d[S:S + P, :], zero).then_inc(scattered, 16)
            for t in range(NT):
                s = t % 2
                pool.wait_ge(s_silu, t + 1)
                if t >= 2:
                    pool.wait_ge(s_ht, t - 1)
                pool.tensor_tensor(hidden[:, s, :], silu[:, s, :], u_sb[:, s, :], ALU.mult).then_inc(s_h, 1)
                pool.wait_ge(s_y, t + 1)
                pool.tensor_tensor(s_acc[:, s, :], s_acc[:, s, :], s_row[:, s, :], ALU.add).then_inc(s_acc_ready, 1)
                pool.wait_ge(s_acc_ready, t + 1)
                pool.dma_start(acc[t * P:(t + 1) * P, :], s_acc[:, s, :]).then_inc(acc_in[s], 16)
            for s in range(2):
                pool.wait_ge(acc_in[s], 16 * NT // 2)
            pool.wait_ge(scattered, 32)
            n = trips(pool)

            def gather(s, blk):
                pool.wait_ge(idx_ready, blk + 1)
                if not isinstance(blk, int) or blk >= 2:
                    pool.wait_ge(xt_done, blk)
                pool.sem_inc(gathers, 1)
                pool.indirect_dma_start(out=x_g[:, s, :], out_offset=None, in_=x1d[:, :],
                                        in_offset=bass.IndirectOffsetOnAxis(ap=idx[:, s:s + 1], axis=0)
                                        ).then_inc(gathered[s], 16)

            def body(b, s, ahead=True):
                if ahead:
                    gather(1 - s, b + 3)
                pool.wait_ge(y_act, b + 2)
                pool.wait_ge(y_dve, b + 2)
                pool.wait_ge(so_ready, b + 1)
                pool.wait_ge(scattered, 16 * b + 32)
                pool.sem_inc(gathers, 1)
                pool.indirect_dma_start(out=acc[:, :], out_offset=bass.IndirectOffsetOnAxis(ap=idx_out[:, s:s + 1], axis=0),
                                        in_=y_out[:, s, :], in_offset=None, compute_op=ALU.add
                                        ).then_inc(scattered, 16)
            gather(0, 0)
            gather(1, 1)
            gather(0, 2)
            with pool.Fori(0, n) as i:
                for s in range(2):
                    body(2 * i + s, s)
            for s in range(2):
                body(2 * n + s, s, ahead=False)
            pool.wait_ge(gathered[0], 16 * n + 32)
            pool.wait_ge(gathered[1], 16 * n + 16)
            pool.wait_ge(scattered, 32 * n + 64)

        @block.tensor
        def _(pe):
            pe.wait_ge(in_const, 16)
            pe.wait_ge(sh_in, 48)

            def shared_up(t):
                s = t % 2
                if t >= 2:
                    pe.wait_ge(s_silu, t - 1)
                for k in range(KD):
                    ins = pe.matmul(bank[s][:, :], x1_t[:, k, t * P:(t + 1) * P], s_gu[:, k, :], start=k == 0, stop=k == KD - 1)
                ins.then_inc(s_gu_done, 1)

            def shared_down(t):
                s = t % 2
                pe.wait_ge(s_h, t + 1)
                if t:
                    pe.wait_ge(s_ht_out, t)
                for j in range(2):
                    ins = pe.transpose(bank[4][:, j * P:(j + 1) * P], hidden[:, s, j * P:(j + 1) * P], ident)
                ins.then_inc(s_ht, 1)
                if t:
                    pe.wait_ge(s_y, t)
                pe.wait_ge(s_ht_out, t + 1)
                for h in range(2):
                    for j in range(2):
                        ins = pe.matmul(bank[2 + h][:, :], hid_t[:, j, :], s_d[:, j, h * HALF:(h + 1) * HALF],
                                        start=j == 0, stop=j == 1)
                ins.then_inc(s_down, 1)

            shared_up(0)
            for t in range(NT):
                if t + 1 < NT:
                    shared_up(t + 1)
                shared_down(t)
                if t == 4:
                    pe.wait_ge(mask_done, 1)
                    for n in range(NT):
                        o = bank[6][:, n * E:(n + 1) * E]
                        pe.matmul(o, const('before'), mask[:, n, :], start=True, stop=n == 0)
                        if n:
                            pe.matmul(o, const('ones'), run[:, n - 1, :], start=False, stop=True)
                    pe.matmul(bank[7][:, 0:E], const('ones'), run[:, NT - 1, :], start=True, stop=True).then_inc(pos_done, 1)
                if t == 5:
                    pe.wait_ge(ek_done, 1)
                    for i in range(2):
                        pe.matmul(bank[5][0:1, i * MAXB:(i + 1) * MAXB], ek[:, i:i + 1], ident, start=True, stop=True)
                    pe.matmul(bank[5][0:1, 2 * MAXB:2 * MAXB + 1], ek[:, 2:3], const('ones')[:, 0:1], start=True,
                              stop=True).then_inc(tab_done, 1)
            n = trips(pe)
            pe.wait_ge(route_ready, 1)
            pe.wait_ge(s_y, NT)

            def find(blk, s):
                e = expert_of(pe, blk)
                pe.wait_ge(oh_ready, blk + 1)
                if not isinstance(blk, int) or blk >= 1:
                    pe.wait_ge(idx_ready, blk)
                for t in range(NT):
                    ins = pe.matmul(bank[7][:, 8 * s:8 * s + 6], one_hot[:, s, t, :],
                                    info[:, t, bass.ds(e, 1), :].rearrange('p a b -> p (a b)'), start=t == 0, stop=t == NT - 1)
                ins.then_inc(idx_done, 1)

            def turn(blk, s, count):
                pe.wait_ge(gathered[s], count)
                if not isinstance(blk, int) or blk >= 1:
                    pe.wait_ge(xgt_ready, blk)
                for k in range(KD):
                    ins = pe.transpose(bank[4 + k // 4][:, (k % 4) * P:(k % 4 + 1) * P],
                                       x_g[:, s, :].rearrange('p (c k) -> p k c', k=KD)[:, k, :], ident)
                ins.then_inc(xt_done, 1)

            def up(blk, s, count):
                pe.wait_ge(w_gu_in[s], count)
                pe.wait_ge(xgt_ready, blk + 1)
                pe.wait_ge(h_ready, blk + 1)
                for k in range(KD):
                    ins = pe.matmul(bank[s][:, :].rearrange('p (m f) -> p m f', m=2), x_gt[:, s, k, :],
                                    w_gu[:, s, :, k, :], start=k == 0, stop=k == KD - 1)
                ins.then_inc(gu_done, 1)

            def body(b, s, i, ahead1=True, ahead=True):
                pe.wait_ge(h_ready, b + 3)
                pe.wait_ge(ht_ready, b + 1)
                for j in range(2):
                    ins = pe.transpose(bank[6][:, j * P:(j + 1) * P],
                                       hidden[:, s, :].rearrange('p (c k) -> p k c', k=2)[:, j, :], ident)
                ins.then_inc(ht_done, 1)
                if ahead:
                    find(b + 3, 1 - s)
                if ahead1:
                    up(b + 1, 1 - s, 32 * i + 32 * (s + 1))
                if ahead:
                    turn(b + 2, s, 16 * i + 32)
                pe.wait_ge(w_d_in[s], 16 * i + 16)
                pe.wait_ge(ht_ready, b + 2)
                pe.wait_ge(y_act, b + 1)
                pe.wait_ge(y_dve, b + 1)
                for h in range(2):
                    for j in range(2):
                        ins = pe.matmul(bank[2 + h][:, :], hid_t[:, j, :], w_d[:, s, j, h * HALF:(h + 1) * HALF],
                                        start=j == 0, stop=j == 1)
                ins.then_inc(down_done, 1)
            for sm, v in CREDIT:
                pe.sem_inc(sm, v)
            find(0, 0)
            find(1, 1)
            find(2, 0)
            turn(0, 0, 16)
            up(0, 0, 32)
            turn(1, 1, 16)
            with pe.Fori(0, n) as i:
                for s in range(2):
                    body(2 * i + s, s, i)
            for s in range(2):
                body(2 * n + s, s, n, ahead1=s == 0, ahead=False)

        @block.scalar
        def _(act):
            for t in range(NT):
                s = t % 2
                act.wait_ge(s_gu_done, t + 1)
                if t >= 2:
                    act.wait_ge(s_h, t - 1)
                act.activation(silu[:, s, :], bank[s][:, 0:FE], ACT.Silu)
                act.activation(u_sb[:, s, :], bank[s][:, FE:2 * FE], ACT.Copy).then_inc(s_silu, 1)
                act.wait_ge(s_ht, t + 1)
                if t:
                    act.wait_ge(s_down, t)
                act.activation(hid_t[:, :, :], bank[4][:, 0:2 * P].rearrange('p (j c) -> p j c', j=2), ACT.Copy
                               ).then_inc(s_ht_out, 1)
                if t == 0:
                    act.wait_ge(scattered, 32)
                if t >= 2:
                    act.wait_ge(acc_in[s], 16 * (t // 2))
                act.activation(s_row[:, s, :], x1_n[:, t, :], ACT.Copy, scale=ALPHA)
                act.wait_ge(s_down, t + 1)
                for h in range(2):
                    ins = act.activation(s_acc[:, s, h * HALF:(h + 1) * HALF], bank[2 + h][:, :], ACT.Copy)
                ins.then_inc(s_y, 1)
            n = trips(act)

            def turned(blk, s):
                act.wait_ge(xt_done, blk + 2)
                act.wait_ge(gu_done, blk + 1)
                for h in range(2):
                    ins = act.activation(x_gt[:, s, 4 * h:4 * h + 4, :],
                                         bank[4 + h][:, :].rearrange('p (k c) -> p k c', k=4), ACT.Copy)
                ins.then_inc(xgt_ready, 1)

            def gated(blk, s):
                act.wait_ge(gu_done, blk + 3)
                act.wait_ge(h_ready, blk + 1)
                act.activation(silu[:, s, :], bank[s][:, 0:FE], ACT.Silu).then_inc(sg_ready, 1)

            def body(b, s, ahead1=True, ahead=True):
                act.wait_ge(ht_done, b + 3)
                act.wait_ge(down_done, b + 2)
                act.activation(hid_t[:, :, :], bank[6][:, 0:2 * P].rearrange('p (j c) -> p j c', j=2), ACT.Copy
                               ).then_inc(ht_ready, 1)
                if ahead1:
                    gated(b + 1, 1 - s)
                if ahead:
                    turned(b + 2, s)
                act.wait_ge(down_done, b + 3)
                act.wait_ge(scattered, 16 * b + 16)
                act.activation(y_out[:, s, 0:HALF], bank[2][:, :], ACT.Copy).then_inc(y_act, 1)
            turned(0, 0)
            gated(0, 0)
            turned(1, 1)
            with act.Fori(0, n) as i:
                for s in range(2):
                    body(2 * i + s, s)
            for s in range(2):
                body(2 * n + s, s, ahead1=s == 0, ahead=False)
            act.wait_ge(eps_set2, 1)
            for t in range(NT):
                act.wait_ge(mv_done2, t + 1)
                act.activation(sd[:, t % 2:t % 2 + 1], mv[:, t % 2, 1:2], ACT.Sqrt, bias=eps[:, 0:1]).then_inc(sd_done2, 1)

        @block.vector
        def _(dve):
            order = Order(dve, d_order)
            X = order.after
            dve.memset(eps[:, :], EPS).then_inc(eps_set2, 1)
            dve.wait_ge(in_const, 16)
            dve.wait_ge(rb_in, 16)
            X(dve.tensor_tensor(biased, scores[:, :, :], bcast(rb[:, :], 1, NT), ALU.add))
            for n in range(NT):
                for g in range(NG):
                    ins = dve.max(t8[:, n, g, :], biased[:, n, g * EG:(g + 1) * EG])
            X(ins)
            X(dve.tensor_tensor(gs[:, :, :], t8[:, :, :, 0], t8[:, :, :, 1], ALU.add))
            other, own = bcast(gs[:, :, :], 2, NG), bcast(gs[:, :, :], 3, NG)
            X(dve.tensor_tensor(t_gt, other, own, ALU.is_gt))
            X(dve.tensor_tensor(t_ge, other, own, ALU.is_ge))
            X(dve.tensor_tensor(t_ge, t_ge, t_gt, ALU.subtract))
            X(dve.tensor_tensor(t_ge.rearrange('p n g h -> p n (g h)'), t_ge.rearrange('p n g h -> p n (g h)'),
                                bcast(const('lower'), 1, NT), ALU.mult))
            X(dve.tensor_tensor(t_gt, t_gt, t_ge, ALU.add))
            X(dve.reduce_sum(keep[:, :, :], t_gt, AX.X))
            X(dve.tensor_scalar(keep[:, :, :], keep[:, :, :], float(TOPG), None, ALU.is_lt))
            split = lambda ap: ap.rearrange('p n (g h) -> p n g h', g=NG)
            for n in range(NT):
                ins = dve.tensor_tensor(cand[:, n, 0:E].rearrange('p (g h) -> p g h', g=NG),
                                        biased[:, n, :].rearrange('p (g h) -> p g h', g=NG), bcast(keep[:, n, :], 2, EG),
                                        ALU.mult)
            dve.memset(cand[:, :, E:E + 2], 1e30)
            X(dve.tensor_scalar(gs[:, :, :], keep[:, :, :], 1e30, -1e30, ALU.mult, ALU.add))
            for n in range(NT):
                ins = dve.tensor_tensor(cand[:, n, 0:E].rearrange('p (g h) -> p g h', g=NG),
                                        cand[:, n, 0:E].rearrange('p (g h) -> p g h', g=NG), bcast(gs[:, n, :], 2, EG),
                                        ALU.add)
            X(ins)
            for n in range(NT):
                ins = dve.max(top[:, n, :], cand[:, n, 0:E])
            X(ins)
            X(dve.memset(top[:, :, TOPK:8], 1e30))
            for n in range(NT):
                ins = dve.match_replace(cut[:, n, :], top[:, n, :], cand[:, n, :], -3e38)
            X(ins)
            X(dve.tensor_scalar(mask, cut[:, :, 0:E], -3e38, None, ALU.is_equal))
            X(dve.tensor_copy(run[:, 0, :], mask[:, 0, :]))
            for n in range(1, NT):
                ins = dve.tensor_tensor(run[:, n, :], run[:, n - 1, :], mask[:, n, :], ALU.add)
                if n < NT - 1:
                    X(ins)
            ins.then_inc(mask_done, 1)
            X(dve.tensor_tensor(gate_w, scores[:, :, :], mask, ALU.mult))
            X(dve.reduce_sum(g_sum[:, :], gate_w, AX.X))
            X(dve.reciprocal(g_sum[:, :], g_sum[:, :]))
            X(dve.tensor_tensor(gate_w, gate_w, bcast(g_sum[:, :], 2, E), ALU.mult))
            X(dve.tensor_scalar(gate_w, gate_w, ROUTE, None, ALU.mult))
            for part in (3, 4, 5):
                X(dve.tensor_copy(info[:, :, :, part], gate_w))
                if part < 5:
                    X(dve.tensor_tensor(gate_w, gate_w, info[:, :, :, part], ALU.subtract))
            dve.tensor_copy(info[:, :, :, 0], bcast(const('tile_tok'), 2, E))
            dve.tensor_copy(info[:, :, :, 1], bcast(const('row').broadcast_to([P, NT]), 2, E))
            dve.memset(info[:, :, :, 2], 1.0)
            dve.wait_ge(pos_done, 1)
            X(dve.tensor_scalar(pos[:, :, :], bank[6][:, :].rearrange('p (n e) -> p n e', n=NT), 4096.0, None, ALU.add))
            X(dve.tensor_tensor(pos[:, :, :], pos[:, :, :], mask, ALU.mult))
            dve.tensor_scalar(pos[:, :, :], pos[:, :, :], -4096.0, None, ALU.add)
            c8 = cmp8.rearrange('p n g h -> p (n g) h')
            X(dve.tensor_copy(le[:, :], bank[7][:, 0:E]))
            X(dve.tensor_tensor(c8, bcast(le[:, :], 2, 8), bcast(const('steps'), 1, E), ALU.is_gt))
            X(dve.reduce_sum(n_blk[:, :], c8, AX.X))
            X(dve.memset(end_blk[:, :], 1.0))
            X(dve.tensor_tensor_scan(le[:, :], end_blk[:, :], n_blk[:, :], 0.0, ALU.mult, ALU.add))
            X(dve.tensor_scalar(end_blk[:, :], le[:, :], const('row'), None, ALU.is_le))
            X(dve.reduce_sum(ek[:, 0:1], end_blk[:, :], AX.X))
            X(dve.tensor_tensor(end_blk[:, :], end_blk[:, :], n_blk[:, :], ALU.mult))
            X(dve.reduce_sum(ek[:, 1:2], end_blk[:, :], AX.X))
            X(dve.tensor_scalar(ek[:, 3:4], ek[:, 0:1], float(E), 8.0, ALU.is_ge, ALU.mult))
            X(dve.tensor_tensor(ek[:, 1:2], const('row'), ek[:, 1:2], ALU.subtract))
            X(dve.tensor_scalar(ek[:, 1:2], ek[:, 1:2], ek[:, 3:4], 8.0, ALU.max, ALU.min))
            X(dve.tensor_scalar(ek[:, 1:2], ek[:, 1:2], float(P), None, ALU.mult))
            X(dve.tensor_scalar(ek[:, 2:3], ek[:, 3:4], 8.0, const('even'), ALU.is_lt, ALU.mult))
            dve.tensor_scalar(ek[:, 0:1], ek[:, 0:1], float(E - 1), None, ALU.min).then_inc(ek_done, 1)
            dve.wait_ge(tab_done, 1)
            dve.tensor_copy(table[:, :], bank[5][0:1, 0:2 * MAXB + 1]).then_inc(tab_ready, 1)
            n = trips(dve)
            dve.nop().then_inc(route_ready, 1)

            def one_hots(blk, s):
                e = expert_of(dve, blk)
                first = dve.value_load(table[0:1, bass.ds(blk + MAXB, 1)], min_val=0, max_val=NT * P)
                ranks = const('rank')[:, bass.ds(first, P)]
                if not isinstance(blk, int) or blk >= 2:
                    dve.wait_ge(idx_done, blk - 1)
                dve.tensor_tensor(one_hot[:, s, :, :], bcast(ranks, 1, NT),
                                  pos[:, :, bass.ds(e, 1)].broadcast_to([P, NT, P]), ALU.is_equal).then_inc(oh_ready, 1)

            def keep_rows(s):
                dve.tensor_copy(row_gate[:, 2 + s:3 + s], row_gate[:, s:s + 1])
                return dve.tensor_copy(idx_kept[:, s:s + 1], idx[:, s:s + 1])

            def rows(blk, s):
                dve.wait_ge(idx_done, blk + 1)
                if not isinstance(blk, int) or blk >= 2:
                    dve.wait_ge(xt_done, blk)
                    keep_rows(s)
                wait_f(dve.tensor_copy(found[:, s, :], bank[7][:, 8 * s:8 * s + 6]), blk, 1)
                wait_f(dve.scalar_tensor_tensor(idx_f[:, :], found[:, s, 2:3], const('neg_row'), found[:, s, 0:1],
                                                ALU.mult, ALU.add), blk, 2)
                dve.reduce_sum(row_gate[:, s:s + 1], found[:, s, 3:6], AX.X)
                dve.tensor_scalar(idx[:, s:s + 1], idx_f[:, :], found[:, s, 1:2], const('row_dummy'), ALU.add, ALU.add
                                  ).then_inc(idx_ready, 1)

            def wait_f(ins, blk, k):
                ins.then_inc(f_order, 1)
                dve.wait_ge(f_order, 2 * blk + k)

            def hide(blk, s):
                dve.wait_ge(sg_ready, blk + 1)
                dve.wait_ge(ht_done, blk + 1)
                dve.wait_ge(idx_ready, blk + 3)
                dve.scalar_tensor_tensor(hidden[:, s, :], bank[s][:, FE:2 * FE], row_gate[:, 2 + s:3 + s], silu[:, s, :],
                                         ALU.mult, ALU.mult).then_inc(h_ready, 1)
                dve.wait_ge(scattered, 16 * blk + 16)
                dve.tensor_copy(idx_out[:, s:s + 1], idx_kept[:, s:s + 1]).then_inc(so_ready, 1)

            def body(b, s, ahead1=True, ahead=True):
                if ahead:
                    rows(b + 3, 1 - s)
                elif ahead1:
                    keep_rows(1 - s).then_inc(idx_ready, 1)
                if ahead1:
                    hide(b + 1, 1 - s)
                if ahead:
                    one_hots(b + 4, s)
                dve.wait_ge(down_done, b + 3)
                dve.wait_ge(scattered, 16 * b + 16)
                dve.tensor_copy(y_out[:, s, HALF:D], bank[3][:, :]).then_inc(y_dve, 1)
            one_hots(0, 0)
            one_hots(1, 1)
            rows(0, 0)
            rows(1, 1)
            one_hots(2, 0)
            rows(2, 0)
            hide(0, 0)
            one_hots(3, 1)
            with dve.Fori(0, n) as i:
                for s in range(2):
                    body(2 * i + s, s)
            for s in range(2):
                body(2 * n + s, s, ahead1=s == 0, ahead=False)
            dve.wait_ge(ln_in2, 32)
            for t in range(NT):
                s, row = t % 2, rows2[:, t, :]
                dve.wait_ge(acc_row_in[t], 16)
                for h in range(2):
                    ins = dve.bn_stats(stats[:, s, h, :], rows2[:, t, h * HALF:(h + 1) * HALF])
                X(ins)
                dve.bn_aggr(mv[:, s, :], stats[:, s, :, :]).then_inc(mv_done2, 1)
                dve.wait_ge(sd_done2, t + 1)
                X(dve.reciprocal(sd[:, s:s + 1], sd[:, s:s + 1]))
                X(dve.tensor_scalar(row, row, mv[:, s, 0:1], sd[:, s:s + 1], ALU.subtract, ALU.mult))
                X(dve.tensor_tensor(row, row, g2, ALU.mult))
                dve.tensor_tensor(row, row, b2, ALU.add).then_inc(row_done, 1)


def program(nc, d, consts, c_at, consts_moe, e_at, out):
    yt = nc.dram_tensor('yt', (10, P, S), F32, kind='Internal').ap()
    gates = nc.dram_tensor('gates', (KD, 4, P, S), F32, kind='Internal').ap()
    x1d = nc.dram_tensor('x1d', (S + P, D), F32, kind='Internal').ap()
    acc = nc.dram_tensor('acc', (S + P, D), F32, kind='Internal').ap()
    with ExitStack() as ctx:
        def sem(name):
            return ctx.enter_context(nc.semaphore(name))
        d = dict(d, ident=consts_moe[:, e_at['ident'][0]:e_at['ident'][0] + P])
        mixers(nc, d, consts, c_at, yt, gates, sem)
        x1 = ctx.enter_context(nc.sbuf_tensor('x1', [P, 2 * KD * S + 2048], F32))
        x1_n = x1[:, 0:NT * D].rearrange('p (n d) -> p n d', d=D)
        x1_t = x1[:, NT * D:2 * NT * D].rearrange('p (k s) -> p k s', s=S)
        scores = ctx.enter_context(nc.sbuf_tensor('scores', [P, NT, E], F32))
        merge_and_project(nc, d, yt, gates, x1d, x1_n, x1_t, scores, x1, sem)
        experts(nc, d, consts_moe, e_at, x1d, acc, x1_n, x1_t, scores, x1, out, sem)


def kernel(**inputs):
    import concourse.bacc as bacc
    from concourse.bass_utils import run_bass_kernel_spmd

    nc = bacc.Bacc('TRN2', target_bir_lowering=False, num_devices=1)
    (c_tab, c_at), (e_tab, e_at) = packed(constants()), packed(constants_moe())
    arrays = {f'in_{k}': np.ascontiguousarray(inputs[k]) for k in IN_NAMES}
    arrays['in_tables'], arrays['in_tables_moe'] = c_tab, e_tab
    aps = {k: nc.dram_tensor(k, v.shape, mybir.dt.from_np(v.dtype), kind='ExternalInput').ap() for k, v in arrays.items()}
    out = nc.dram_tensor('out_0', (1, S, D), F32, kind='ExternalOutput').ap()
    program(nc, {k: aps[f'in_{k}'] for k in IN_NAMES}, aps['in_tables'], c_at, aps['in_tables_moe'], e_at, out)
    got = run_bass_kernel_spmd(nc, [arrays], core_ids=[0])
    return got.results[0]['out_0']
```

```python
from contextlib import ExitStack

import numpy as np

import concourse.bass as bass
from concourse import mybir

F32, F32R, I32, BF16 = mybir.dt.float32, mybir.dt.float32r, mybir.dt.int32, mybir.dt.bfloat16
ALU, ACT, AX = mybir.AluOpType, mybir.ActivationFunctionType, mybir.AxisListType

P = 128
D = 1024
S = 1024
KD = D // P
NT = S // P
HALF = 512
CONV_K, CONV_C = 31, 2
DH = 64
NCMP, CMP_LEN, CMP_STRIDE, CMP_HID = 63, 32, 16, 256
NSLC, SLC = 16, 64
E, NG, TOPG, TOPK, FE = 64, 8, 4, 6, 256
EG = E // NG
ALPHA = float(2 ** 0.25)
EPS = 1e-5
ROUTE = 2.5
BIG = 1e33
NEG = -1e30
SLOPES = [2.0 ** -(i + 1) for i in range(8)]
SLOPE_SWA, SLOPE_NSA = SLOPES[:4], SLOPES[4:]
MAXB = 128

IN_NAMES = ['x', 'w_in', 'conv_dw', 'conv_db', 'conv_ln_g', 'conv_ln_b', 'swa_sink', 'ret_gn_g', 'ret_gn_b',
            'nsa_pe_k', 'nsa_w1_k', 'nsa_w2_k', 'nsa_pe_v', 'nsa_w1_v', 'nsa_w2_v', 'p_conv', 'p_swa', 'p_ret',
            'p_nsa', 'w_out', 'ln1_g', 'ln1_b', 'router_w', 'router_b', 'moe_wg', 'moe_wu', 'moe_wd',
            'sh_wg', 'sh_wu', 'sh_wd', 'ln2_g', 'ln2_b']

O_CONV, O_SQ, O_SK, O_SV, O_RQ, O_RK, O_RV, O_RG, O_NQ = 0, 512, 768, 896, 1024, 1280, 1536, 2048, 2560
O_KC, O_KS, O_VS, O_KW, O_VW, O_GT, O_MG = 2816, 2944, 3008, 3072, 3136, 3200, 3212


def constants():
    q = np.arange(P)[:, None].astype(np.float64)
    out = {}
    out['ident'] = np.eye(P)
    j = np.arange(1024)[None, :]
    d = q + 896 - j
    out['dist_sel'] = np.where(d >= 0, d, BIG)
    j = np.arange(640)[None, :]
    d = q + 512 - j
    out['dist_win'] = np.where((d >= 0) & (d < 512), d, BIG)
    j = np.arange(256)[None, :]
    d = q + 128 - j
    out['dist_swa'] = np.where((d >= 0) & (d < 128), d, BIG)
    n, c = np.arange(NT)[None, :, None], np.arange(NCMP)[None, None, :]
    d = q[:, :, None] + P * n - (CMP_STRIDE * c + CMP_LEN - 1)
    out['dist_cmp'] = np.where(d >= 0, d, BIG).reshape(P, -1)
    out['mask_cmp'] = (d >= 0).reshape(P, -1)
    t, jj = q[:, :, None] + P * n, np.arange(NSLC)[None, None, :]
    cur = t // SLC
    forced = (jj == 0) | (jj == cur) | (jj == cur - 1)
    out['imp_keep'] = (~forced & (jj <= cur)).reshape(P, -1)
    out['imp_set'] = np.where(forced, 1e4, np.where(jj > cur, -1.0, 0.0)).reshape(P, -1)
    lg = np.log1p(-(2.0 ** (-5.0 - np.arange(4))))
    k, qq = np.arange(P)[:, None], np.arange(P)[None, :]
    out['decay'] = np.stack([np.where(qq >= k, 0.125 * np.exp(lg[h] * np.maximum(qq - k, 0)), 0) for h in range(4)],
                            1).reshape(P, -1)
    xi = np.exp(lg[:, None] * (np.arange(P) + 1.0)[None, :])
    out['xi'] = np.stack([np.repeat(xi[2 * p:2 * p + 2], 64, 0) for p in range(2)], 1).reshape(P, -1)
    out['zeta'] = (0.125 * np.exp(lg[:, None] * (P - 1 - np.arange(P))[None, :])).T
    cd = np.exp(lg * P)
    out['chunk_decay'] = np.stack([np.repeat(cd[2 * p:2 * p + 2], 64) for p in range(2)], 1)
    out['mean_conv'] = np.full((P, P), 1.0 / (CONV_C * P))
    return {k: np.ascontiguousarray(v, dtype=np.float32) for k, v in out.items()}


def constants_moe():
    r = np.arange(P)[:, None]
    out = {}
    out['ident'] = np.eye(P)
    out['before'] = (r < np.arange(P)[None, :])
    out['ones'] = np.ones((P, P))
    out['rank'] = np.tile(np.arange((NT + 1) * P)[None, :], (P, 1))
    out['tile_tok'] = np.tile(P * np.arange(NT)[None, :] - 1024.0, (P, 1))
    out['row'] = r
    out['neg_row'] = -1.0 * r
    out['row_dummy'] = r + 1024.0
    out['even'] = (r % 2 == 0) & (r > 0)
    out['steps'] = np.tile(P * np.arange(8)[None, :], (P, 1))
    out['lower'] = np.tile((np.arange(8)[None, :] < np.arange(8)[:, None]).reshape(1, -1), (P, 1))
    return {k: np.ascontiguousarray(v, dtype=np.float32) for k, v in out.items()}


def packed(tables):
    at, offs = 0, {}
    for k, v in tables.items():
        offs[k] = (at, v.shape[1])
        at += v.shape[1]
    return np.concatenate(list(tables.values()), 1), offs


def chunk_list():
    one = lambda c: [(0, c, P)]
    pairs = lambda a, b: [(0, a, 64), (64, b, 64)]
    out = [('conv_gate', c, one(O_CONV + 256 + c * P)) for c in range(2)]
    out += [('conv_a', c, one(O_CONV + c * P)) for c in range(2)]

    def ret(p):
        return ([('ret_q', p, one(O_RQ + p * P)), ('ret_k', p, one(O_RK + p * P))]
                + [('ret_v', (p, e), one(O_RV + (2 * p + e) * P)) for e in range(2)]
                + [('ret_g', (p, e), one(O_RG + (2 * p + e) * P)) for e in range(2)])
    gates = [('merge', (j, b), one(O_MG + b * D + j * P)) for j in range(KD) for b in range(4)]
    out += ret(0) + gates[:5] + ret(1)
    out += [('swa_q', c, pairs(O_SQ + c * 64, O_SQ + c * 64 + 128)) for c in range(2)]
    out += [('swa_k', 0, one(O_SK)), ('swa_v', 0, one(O_SV))]
    out += [('nsa_q', c, one(O_NQ + c * P)) for c in range(2)]
    out += [('kcvc', 0, one(O_KC)), ('kskw', 0, pairs(O_KS, O_KW)),
            ('vsvw', 0, pairs(O_VS, O_VW)), ('gate', 0, one(O_GT))]
    return out + gates[5:]


CHUNKS = chunk_list()
NCH = len(CHUNKS)
WHERE = {(k, i): c for c, (k, i, _) in enumerate(CHUNKS)}


def attention_units():
    swa = [dict(kind='swa', n=n, h=h, b0=max(0, n - 1), nb=min(n + 1, 2)) for n in range(NT) for h in range(4)]
    nsa = []
    for n in range(NT):
        for h in range(4):
            nsa.append(dict(kind='win', n=n, h=h, b0=max(0, n - 4), nb=min(n + 1, 5)))
            nsa.append(dict(kind='sel', n=n, h=h, b0=0, nb=n + 1))
    units = swa + nsa
    for u, un in enumerate(units):
        un['u'] = u
    return swa, nsa


SWA, NSA = attention_units()
UNITS = SWA + NSA


def schedule():
    items = [('xt', g) for g in range(8)] + [('mm', 0), ('mm', 1)] + [('xt', g) for g in range(8, 16)]
    state = dict(q=2, fill=0, pv=0)
    last = 4 * NCH

    def adv(n):
        for _ in range(n):
            if state['q'] < last:
                items.append(('mm', state['q']))
                state['q'] += 1

    def upto(c):
        adv(max(0, 4 * c - state['q']))

    def fill(kind, *a):
        items.append(('fill', state['fill'], kind, a))
        state['fill'] += 1

    upto(WHERE['ret_q', 0])
    items.append(('conv_h',))
    for k in range(CONV_K):
        items.append(('tap', k))
        adv(1)
    adv(2)
    for c in ('conv_mean', 'conv_var', 'conv_out'):
        items.append((c,))
        adv(4)

    def retention(p):
        items.append(('ret_a', p, 0))
        for n in range(NT):
            adv(1)
            if n + 1 < NT:
                items.append(('ret_a', p, n + 1))
            items.append(('ret_b', p, n))
        items.append(('ret_norm', p))
        adv(6)
        for g in range(4):
            fill('ret', p, g)
        items.append(('ret_store', p))
    upto(WHERE['ret_g', (0, 1)] + 1)
    retention(0)
    upto(WHERE['ret_g', (1, 1)] + 1)
    retention(1)
    upto(WHERE['swa_v', 0] + 1)
    for g in range(2):
        fill('swa_v', g)
        adv(1)

    def attention(units, rate):
        debt = 0.0
        waiting = []

        def product():
            un, blocks = waiting.pop()
            items.append(('pv', state['pv'], un['u'], blocks))
            un['last_pv'] = state['pv']
            state['pv'] += 1
            if un['h'] == 3 and un['kind'] != 'win' and blocks[-1] == un['nb'] - 1:
                items.append(('out', un['kind'], un['n']))
        for k in range(-1, len(units) + 1):
            if k + 1 < len(units):
                un = units[k + 1]
                if un['kind'] == 'sel' and un['h'] == 0:
                    items.append(('sel_table', un['n']))
                items.append(('score', un['u']))
                items.append(('max', un['u']))
            if 0 <= k < len(units):
                items.append(('norm', units[k]['u']))
            if k < 1 and k + 1 < len(units):
                items.append(('exp', units[k + 1]['u']))
            if k >= 1:
                prev = units[k - 1]
                groups = [tuple(range(a, min(a + 4, prev['nb']))) for a in range(0, prev['nb'], 4)]
                prev['last_fill'] = state['fill'] + len(groups) - 1
                for g, blocks in enumerate(groups):
                    fill('unit', prev['u'], blocks, state['pv'] + len(waiting))
                    if g == 0 and k + 1 < len(units):
                        items.append(('exp', units[k + 1]['u']))
                    debt += rate / len(groups)
                    adv(int(debt))
                    debt -= int(debt)
                    if waiting:
                        product()
                    waiting.append((prev, blocks))
        product()
    attention(SWA, 1.0)
    upto(WHERE['gate', 0] + 1)
    fill('gate')
    for g in range(2):
        fill('vsvw', g)
    fill('pe')
    adv(6)
    items.append(('hidden',))
    adv(1)
    items.append(('hidden_t',))
    adv(1)
    items.append(('compress',))
    adv(1)
    for n in range(NT):
        items.append(('cmp_score', n))
        adv(3)
        fill('cmp', n)
    attention(NSA, (last - state['q']) / len(NSA))
    adv(last)
    return items


SCHEDULE = schedule()


def bcast(ap, axis, n):
    ap = ap.unsqueeze(axis)
    shape = list(ap.shape)
    shape[axis] = n
    return ap.broadcast_to(shape)


class Order:

    def __init__(self, eng, sem):
        self.eng, self.sem, self.n = eng, sem, 0

    def after(self, ins):
        self.n += 1
        ins.then_inc(self.sem, 1)
        self.eng.wait_ge(self.sem, self.n)


def mixers(nc, d, c_ap, c_at, yt, gates, sem):
    with ExitStack() as ctx:
        def sb(name, shape, dt=F32):
            return ctx.enter_context(nc.sbuf_tensor(name, shape, dt))

        cst = sb('a_const', [P, c_ap.shape[1]])

        def const(name):
            at, width = c_at[name]
            return cst[:, at:at + width]
        ident = const('ident')
        x_hi, x_lo = sb('x_hi', [P, KD, S], F32R), sb('x_lo', [P, KD, S], F32R)
        w_hi, w_lo = sb('w_hi', [P, 2, KD, P], F32R), sb('w_lo', [P, 2, KD, P], F32R)
        w_raw = sb('w_raw', [P, 2, KD, P])
        gate_out = sb('gate_out', [P, 2, HALF])
        reg_a, reg_b, reg_s = sb('reg_a', [P, 8 * 1024]), sb('reg_b', [P, 8 * 1024]), sb('reg_s', [P, 5 * 1024])
        state, o_stats = sb('state', [P, 2, P]), sb('o_stats', [P, 16, 6])
        o_mv, o_rstd = sb('o_mv', [P, 16, 2]), sb('o_rstd', [P, 16])
        hid = sb('hid', [P, 4, 64])
        k_cmp, v_cmp = sb('k_cmp', [P, 64]), sb('v_cmp', [64, DH])
        w2k, w2v = sb('w2k', [P, 2, P]), sb('w2v', [P, 2, DH])
        cs = sb('cs', [P, 2, 4, NCMP])
        c_max, c_sum = sb('c_max', [P, 4]), sb('c_sum', [P, 4])
        c_all = sb('c_all', [P, 65])
        imp, imp_top, imp_cut = sb('imp', [P, NSLC]), sb('imp_top', [P, 8]), sb('imp_cut', [P, NSLC])
        gate_n = sb('gate_n', [P, NT, 12])
        sel_pen = sb('sel_pen', [P, NT, NSLC])
        out_t = sb('out_t', [P, 2, 2, P])
        conv_n = sb('conv_n', [34, 256])
        conv_p = sb('conv_p', [P, 2, 34])
        pe_n, pe_t = sb('pe_n', [32, P]), sb('pe_t', [P, 32])
        sink8 = sb('sink8', [P, 4])
        m_raw, m_neg, den, e_sink = sb('m_raw', [P, 3]), sb('m_neg', [P, 3]), sb('den', [P, 3]), sb('e_sink', [P, 3])
        rden = sb('rden', [P, 3])
        eps = sb('eps', [P, 1])
        bank = [ctx.enter_context(nc.psum_tensor(f'a_bank{i}', [P, HALF], F32)) for i in range(8)]

        def view(region, at, *shape):
            size = int(np.prod(shape))
            ap = region[:, at:at + size]
            if len(shape) == 2:
                return ap.rearrange('p (a b) -> p a b', b=shape[1])
            if len(shape) == 3:
                return ap.rearrange('p (a b c) -> p a b c', b=shape[1], c=shape[2])
            return ap
        x_nat = view(reg_a, 0, NT, D)
        conv_gate, conv_h, conv_y = view(reg_b, 0, 2, S), view(reg_b, 2048, 2, S + CONV_K - 1), view(reg_b, 4160, 2, S)
        conv_r = view(reg_b, 2048, S)
        RET = [dict(v=view(r, 0, 2, S), g=view(r, 2048, 2, S), q=view(r, 4096, S), k=view(r, 5120, S),
                    out=view(r, 4096, 2, S), th=view(r, 6144, 2, S)) for r in (reg_a, reg_b)]
        v_n, inner = view(reg_s, 0, 2, 2, P), view(reg_s, 512, 2, 2, P)
        q_xi, k_z = view(reg_s, 1024, 2, P), view(reg_s, 1280, 2, P)
        gn_g, gn_b = view(reg_s, 2048, 4, P), view(reg_s, 2560, 4, P)
        swa_q, swa_k, swa_vt, swa_v = (view(reg_a, 0, 2, S), view(reg_a, 2048, S), view(reg_a, 3072, S),
                                       view(reg_a, 4096, NT, P))
        nsa_q, kcvc, k_slc, k_win = (view(reg_b, 0, 2, S), view(reg_b, 2048, S), view(reg_b, 3072, S),
                                     view(reg_b, 4096, S))
        vsvw_t, vsvw, gate_t = view(reg_b, 5120, S), view(reg_b, 6144, NT, P), view(reg_b, 7168, S)
        w1 = view(reg_a, 0, CMP_LEN, CMP_HID)
        p_cmp_t = view(reg_a, 0, NT, 4, P)
        soft, w_t, dist_n = view(reg_s, 0, 3, 1024), view(reg_s, 3072, 2, HALF), view(reg_s, 4096, 1024)
        w_t3 = view(reg_s, 3072, 2, 4, P)
        hid_n = view(reg_s, 0, 2, CMP_HID)
        z_cmp = view(reg_s, 3072, CMP_LEN, 64)

        ident_in, const_in, x_in, small_in, gn_in = sem('ident_in'), sem('const_in'), [sem(f'x_in{i}') for i in range(6)], sem('small_in'), sem('gn_in')
        w_in_s = [sem(f'w_raw_in{i}') for i in range(2)]
        w_hi_ready, w_lo_ready = sem('w_hi_ready'), sem('w_lo_ready')
        x_t, x_hi_ready, x_lo_ready = sem('x_t'), sem('x_hi_ready'), sem('x_lo_ready')
        half_done, half_out = sem('half_done'), sem('half_out')
        gate_stored = [sem('gate_stored0'), sem('gate_stored1')]
        fill_done, fill_out = sem('fill_done'), sem('fill_out')
        dve_order, act_order = sem('dve_order'), sem('act_order')
        taps_done, conv_params = sem('taps_done'), sem('conv_params')
        conv_mean_done, conv_sq, conv_var_done, conv_sd, conv_norm, conv_th, conv_fin = (
            sem('conv_mean_done'), sem('conv_sq'), sem('conv_var_done'), sem('conv_sd'), sem('conv_norm'),
            sem('conv_th'), sem('conv_fin'))
        conv_stored = sem('conv_stored')
        ret_a_done, ret_mid, ret_v_out, ret_b_done, ret_state = (sem('ret_a_done'), sem('ret_mid'), sem('ret_v_out'),
                                                                 sem('ret_b_done'), sem('ret_state'))
        ret_mv, ret_sd, ret_th, ret_fin, ret_stored = (sem('ret_mv'), sem('ret_sd'), sem('ret_th'), sem('ret_fin'),
                                                       sem('ret_stored'))
        score_done, max_done, exp_done, soft_done = (sem('score_done'), sem('max_done'), sem('exp_done'),
                                                     sem('soft_done'))
        pv_done, tile_out = sem('pv_done'), sem('tile_out')
        tile_stored = [sem('tile_stored0'), sem('tile_stored1')]
        w1_in, z_ready, hid_done, hid_out, cmp_done, cmp_out = (sem('w1_in'), sem('z_ready'), sem('hid_done'),
                                                                sem('hid_out'), sem('cmp_done'), sem('cmp_out'))
        cscore_done, cmax_done, cexp_done, csoft_done = (sem('cscore_done'), sem('cmax_done'), sem('cexp_done'),
                                                         sem('csoft_done'))
        keys_copied = sem('keys_copied')
        hid_gelu, hid_t_done = sem('hid_gelu'), sem('hid_t_done')
        eps_ready, state_zero = sem('eps_ready'), sem('state_zero')

        block = ctx.enter_context(nc.Block())

        def home(c, h):
            kind, i, _ = CHUNKS[c]
            cols = slice(h * HALF, (h + 1) * HALF)
            if kind == 'conv_gate':
                return conv_gate[:, i, cols]
            if kind == 'conv_a':
                return conv_h[:, i, CONV_K - 1 + h * HALF:CONV_K - 1 + (h + 1) * HALF]
            if kind in ('ret_q', 'ret_k'):
                return RET[i][kind[-1]][:, cols]
            if kind in ('ret_v', 'ret_g'):
                return RET[i[0]][kind[-1]][:, i[1], cols]
            if kind in ('swa_q', 'nsa_q'):
                return (swa_q if kind == 'swa_q' else nsa_q)[:, i, cols]
            return {'swa_k': swa_k, 'swa_v': swa_vt, 'kcvc': kcvc, 'vsvw': vsvw_t,
                    'gate': gate_t}[kind][:, cols]

        X_PIECES = [(0, 0, 2), (0, 2, 4), (0, 4, 6), (0, 6, 8), (1, 0, 4), (1, 4, 8)]

        def raw_total(c):
            return sum(16 * len(CHUNKS[k][2]) for k in range(c % 2, c + 1, 2))

        @block.sync
        def _(sp):
            at, width = c_at['ident']
            sp.dma_start(ident, c_ap[:, at:at + width]).then_inc(ident_in, 16)
            def load(c):
                for dst, src, width in CHUNKS[c][2]:
                    sp.dma_start(w_raw[:, c % 2, :, dst:dst + width],
                                 d['w_in'][0, :, src:src + width].rearrange('(k p) n -> p k n', p=P)
                                 ).then_inc(w_in_s[c % 2], 16)
            for i, (h, a, b) in enumerate(X_PIECES):
                sp.dma_start(x_nat[:, 4 * h:4 * h + 4, a * P:b * P],
                             d['x'][0, h * HALF:(h + 1) * HALF, a * P:b * P].rearrange('(n p) d -> p n d', p=P)
                             ).then_inc(x_in[i], 16)
                if i in (3, 4):
                    load(i - 3)
            for c in range(2, NCH):
                if c == 2:
                    sp.dma_start(cst[:, width:], c_ap[:, width:]).then_inc(const_in, 16)
                sp.wait_ge(w_lo_ready, c - 1)
                sp.wait_ge(w_hi_ready, c - 1)
                load(c)

        @block.gpsimd
        def _(pool):
            pool.dma_start(conv_n[0:31, :], d['conv_dw'][0]).then_inc(small_in, 16)
            for i, name in enumerate(('conv_db', 'conv_ln_g', 'conv_ln_b')):
                pool.dma_start(conv_n[31 + i:32 + i, :], d[name]).then_inc(small_in, 16)
            pool.dma_start(pe_n[:, 0:64], d['nsa_pe_k'][0]).then_inc(small_in, 16)
            pool.dma_start(pe_n[:, 64:128], d['nsa_pe_v'][0]).then_inc(small_in, 16)
            for i in range(2):
                pool.dma_start(w2k[:, :, 64 * i:64 * i + 64],
                               d['nsa_w2_k'][0].rearrange('(m p) n -> p m n', p=P)).then_inc(small_in, 16)
            pool.dma_start(w2v[:, :, :], d['nsa_w2_v'][0].rearrange('(m p) n -> p m n', p=P)).then_inc(small_in, 16)
            pool.dma_start(sink8[:, :], d['swa_sink'].broadcast_to([P, 4])).then_inc(small_in, 16)
            pool.dma_start(gn_g[:, :, :], d['ret_gn_g'].broadcast_to([P, 512]).rearrange('p (a b) -> p a b', b=P)).then_inc(gn_in, 16)
            pool.dma_start(gn_b[:, :, :], d['ret_gn_b'].broadcast_to([P, 512]).rearrange('p (a b) -> p a b', b=P)).then_inc(gn_in, 16)
            stored = [0, 0]

            def split(c):
                pool.wait_ge(w_in_s[c % 2], raw_total(c))
                if c >= 2:
                    pool.wait_ge(half_done, 2 * (c - 2) + 2)
                pool.tensor_copy(w_hi[:, c % 2, :, :], w_raw[:, c % 2, :, :]).then_inc(w_hi_ready, 1)
                pool.wait_ge(w_hi_ready, c + 1)
                pool.tensor_tensor(w_lo[:, c % 2, :, :], w_raw[:, c % 2, :, :], w_hi[:, c % 2, :, :].bitcast(F32),
                                   ALU.subtract).then_inc(w_lo_ready, 1)
            for item in SCHEDULE:
                if item[0] == 'mm' and item[1] % 4 == 3 and item[1] // 4 + 2 < NCH:
                    split(item[1] // 4 + 2)
                if item == ('mm', 4 * WHERE['kskw', 0] + 3):
                    pool.wait_ge(half_out, 2 * WHERE['kskw', 0] + 2)
                    pool.dma_start(k_slc[64:128, :], k_slc[0:64, :]).then_inc(keys_copied, 16)
                    pool.dma_start(k_win[0:64, :], k_win[64:128, :]).then_inc(keys_copied, 16)
                if item[0] == 'conv_out':
                    pool.wait_ge(conv_fin, 1)
                    pool.dma_start(yt[0:2].rearrange('c p s -> p c s'), conv_y).then_inc(conv_stored, 16)
                elif item[0] == 'ret_store':
                    pair = item[1]
                    pool.wait_ge(fill_out, 4 * pair + 4)
                    pool.dma_start(yt[4 + 2 * pair:6 + 2 * pair].rearrange('c p s -> p c s'),
                                   RET[pair]['out']).then_inc(ret_stored, 16)
                elif item[0] == 'out':
                    kind, n = item[1:]
                    t = n + NT * (kind != 'swa')
                    pool.wait_ge(tile_out, t + 1)
                    at = 2 if kind == 'swa' else 8
                    pool.dma_start(yt[at:at + 2, :, n * P:(n + 1) * P].rearrange('c p s -> p c s'),
                                   out_t[:, n % 2]).then_inc(tile_stored[n % 2], 16)
                    stored[n % 2] += 16
                    if kind == 'swa' and n == NT - 1:
                        pool.wait_ge(pv_done, SWA[-1]['last_pv'] + 1)
                        for i, name in enumerate(('nsa_w1_k', 'nsa_w1_v')):
                            pool.dma_start(w1[64 * i:64 * i + 64], d[name][0].rearrange('(l e) h -> e l h', e=DH)
                                           ).then_inc(w1_in, 16)
            for i in range(2):
                pool.wait_ge(tile_stored[i], stored[i])
            pool.wait_ge(conv_stored, 16)
            pool.wait_ge(ret_stored, 32)

        @block.tensor
        def _(pe):
            def quarter(q):
                c, h, part = q // 4, q // 2 % 2, q % 2
                if q % 4 == 0:
                    pe.wait_ge(w_hi_ready, c + 1)
                    pe.wait_ge(w_lo_ready, c + 1)
                if q in (0, 2):
                    pe.wait_ge(x_lo_ready, 8 if q == 0 else 16)
                if part == 0 and c >= 1:
                    pe.wait_ge(half_out, 2 * c + h - 1)
                for k in range(4 * part, 4 * part + 4):
                    cols = slice(h * HALF, (h + 1) * HALF)
                    for j, (w, x) in enumerate(((w_hi, x_hi), (w_hi, x_lo), (w_lo, x_hi))):
                        ins = pe.matmul(bank[h][:, :], w[:, c % 2, k, :], x[:, k, cols],
                                        start=(k == 0 and j == 0), stop=(k == KD - 1 and j == 2))
                if part == 1:
                    ins.then_inc(half_done, 1)

            def transposes(pairs_):
                for out, in_, idn in pairs_:
                    ins = pe.transpose(out, in_, idn)
                return ins

            pe.wait_ge(ident_in, 16)
            for item in SCHEDULE:
                what = item[0]
                if what == 'mm':
                    quarter(item[1])
                elif what == 'xt':
                    g = item[1]
                    h, k = g // 8, g % 8
                    for i, piece in enumerate(X_PIECES):
                        if piece[:2] == (h, k):
                            pe.wait_ge(x_in[i], 16)
                    if g >= 4:
                        pe.wait_ge(x_lo_ready, g - 3)
                    transposes([(bank[2 + g % 4][:, j * P:(j + 1) * P], x_nat[:, 4 * h + j, k * P:(k + 1) * P], ident)
                                for j in range(4)]).then_inc(x_t, 1)
                elif what == 'conv_h':
                    pe.wait_ge(small_in, 160)
                    transposes([(bank[6][:, c * 34:(c + 1) * 34], conv_n[:, c * P:(c + 1) * P], ident[0:34, 0:34])
                                for c in range(2)]).then_inc(conv_params, 1)
                elif what == 'conv_mean':
                    pe.wait_ge(const_in, 16)
                    pe.wait_ge(taps_done, 2 * CONV_K)
                    for h in range(2):
                        for c in range(2):
                            ins = pe.matmul(bank[2 + h][:, :], const('mean_conv'), conv_y[:, c, h * HALF:(h + 1) * HALF],
                                            start=c == 0, stop=c == 1)
                    ins.then_inc(conv_mean_done, 1)
                elif what == 'conv_var':
                    pe.wait_ge(conv_sq, 1)
                    for h in range(2):
                        for c in range(2):
                            ins = pe.matmul(bank[4 + h][:, :], const('mean_conv'),
                                            conv_gate[:, c, h * HALF:(h + 1) * HALF], start=c == 0, stop=c == 1)
                    ins.then_inc(conv_var_done, 1)
                elif what == 'ret_a':
                    pair, n = item[1:]
                    i = NT * pair + n
                    s, R, blk = i % 2, RET[pair], slice(n * P, (n + 1) * P)
                    T, K = bank[2 + 3 * s], bank[3 + 3 * s]
                    if n == 0:
                        pe.wait_ge(half_out, 2 * WHERE['ret_g', (pair, 1)] + 2)
                        pe.wait_ge(conv_norm, 1)
                        pe.wait_ge(fill_out, 4 * pair) if pair else None
                    if i >= 2:
                        pe.wait_ge(ret_v_out, i - 1)
                        pe.wait_ge(ret_mid, i - 1)
                        pe.wait_ge(ret_state, i - 1)
                    transposes([(T[:, e * P:(e + 1) * P], R['v'][:, e, blk], ident) for e in range(2)]
                               + [(T[:, (2 + e) * P:(3 + e) * P], R['g'][:, e, blk], ident) for e in range(2)]
                               + [(K[:, 0:P], R['k'][:, blk], ident)])
                    for e in range(2):
                        rows = slice(64 * e, 64 * e + 64)
                        out = K[:, P:2 * P] if e == 0 else bank[4 + 3 * s][:, 3 * P:4 * P]
                        ins = pe.matmul(out, R['k'][rows, blk], R['q'][rows, blk], start=True, stop=True)
                    ins.then_inc(ret_a_done, 1)
                elif what == 'ret_b':
                    pair, n = item[1:]
                    i = NT * pair + n
                    s, O = i % 2, bank[4 + 3 * (i % 2)]
                    pe.wait_ge(ret_mid, i + 1)
                    pe.wait_ge(ret_v_out, i + 1)
                    if i == 0:
                        pe.wait_ge(state_zero, 1)
                    else:
                        pe.wait_ge(ret_state, i)
                    pe.matmul(O[:, 0:2 * P], q_xi[:, s, :], state[:, :, :], start=True, stop=False)
                    for e in range(2):
                        pe.matmul(O[:, e * P:(e + 1) * P], inner[:, s, e, :], v_n[:, s, e, :], start=False, stop=e == 1)
                    for e in range(2):
                        rows = slice(64 * e, 64 * e + 64)
                        ins = pe.matmul(O[rows, 2 * P:3 * P], k_z[:, s, rows], v_n[:, s, e, :], start=True, stop=True)
                    ins.then_inc(ret_b_done, 1)
                elif what == 'fill':
                    f, kind, a = item[1:]
                    B = bank[6]
                    if f:
                        pe.wait_ge(fill_out, f)
                    if kind == 'ret':
                        pair, g = a
                        e, n0 = g // 2, 4 * (g % 2)
                        pe.wait_ge(ret_fin, pair + 1)
                        todo = [(B[:, j * P:(j + 1) * P], RET[pair]['v'][:, e, (n0 + j) * P:(n0 + j + 1) * P], ident)
                                for j in range(4)]
                    elif kind in ('swa_v', 'vsvw'):
                        pe.wait_ge(half_out, 2 * WHERE[kind, 0] + 2)
                        src = swa_vt if kind == 'swa_v' else vsvw_t
                        todo = [(B[:, j * P:(j + 1) * P], src[:, (4 * a[0] + j) * P:(4 * a[0] + j + 1) * P], ident)
                                for j in range(4)]
                    elif kind == 'gate':
                        pe.wait_ge(half_out, 2 * WHERE['gate', 0] + 2)
                        todo = [(B[:, n * 12:(n + 1) * 12], gate_t[0:12, n * P:(n + 1) * P], ident[0:12, 0:12])
                                for n in range(NT)]
                    elif kind == 'pe':
                        todo = [(B[:, 0:32], pe_n[:, :], ident[0:32, 0:32])]
                    elif kind == 'cmp':
                        n = a[0]
                        pe.wait_ge(csoft_done, n + 1)
                        todo = [(B[0:NCMP, h * P:(h + 1) * P], cs[:, n % 2, h, :], ident) for h in range(4)]
                    else:
                        u, blocks, _ = a
                        pe.wait_ge(soft_done, u + 1)
                        todo = [(B[:, j * P:(j + 1) * P], soft[:, u % 3, b * P:(b + 1) * P], ident)
                                for j, b in enumerate(blocks)]
                    transposes(todo).then_inc(fill_done, 1)
                elif what == 'hidden':
                    pe.wait_ge(w1_in, 32)
                    pe.wait_ge(z_ready, 2)
                    for kv in range(2):
                        rows = slice(64 * kv, 64 * kv + 64)
                        B = bank[2 + 3 * kv]
                        for l in range(CMP_LEN):
                            ins = pe.matmul(B[0:NCMP, 0:CMP_HID], z_cmp[rows, l, 0:NCMP], w1[rows, l, :],
                                            start=l == 0, stop=l == CMP_LEN - 1)
                    ins.then_inc(hid_done, 1)
                elif what == 'hidden_t':
                    pe.wait_ge(hid_gelu, 1)
                    transposes([(bank[2][:, j * 64:j * 64 + NCMP], hid_n[0:NCMP, j // 2, (j % 2) * P:(j % 2 + 1) * P],
                                 ident[0:NCMP, 0:NCMP]) for j in range(4)]).then_inc(hid_t_done, 1)
                elif what == 'compress':
                    pe.wait_ge(hid_out, 1)
                    for m in range(2):
                        pe.matmul(bank[3][:, 0:NCMP], w2k[:, m, :], hid[:, m, 0:NCMP], start=m == 0, stop=m == 1)
                    for m in range(2):
                        ins = pe.matmul(bank[4][0:NCMP, 0:DH], hid[:, 2 + m, 0:NCMP], w2v[:, m, :], start=m == 0,
                                        stop=m == 1)
                    ins.then_inc(cmp_done, 1)
                elif what == 'cmp_score':
                    n = item[1]
                    pe.wait_ge(cmp_out, 1)
                    if n >= 2:
                        pe.wait_ge(cmax_done, n - 1)
                    for h in range(4):
                        rows = slice(64 * (h % 2), 64 * (h % 2) + 64)
                        B = bank[2 + 2 * (n % 2) + h % 2]
                        ins = pe.matmul(B[:, h * 64:h * 64 + NCMP], nsa_q[rows, h // 2, n * P:(n + 1) * P],
                                        k_cmp[rows, 0:NCMP], start=True, stop=True)
                    ins.then_inc(cscore_done, 1)
                elif what == 'score':
                    un = UNITS[item[1]]
                    u, n, h = un['u'], un['n'], un['h']
                    if u >= 2:
                        pe.wait_ge(max_done, u - 1)
                    if un['kind'] == 'swa':
                        if u == 0:
                            pe.wait_ge(half_out, 2 * WHERE['swa_k', 0] + 2)
                            pe.wait_ge(ret_state, 16)
                        rows, qs, keys = slice(64 * (h // 2), 64 * (h // 2) + 64), swa_q[:, h % 2], swa_k
                    else:
                        if u == len(SWA):
                            pe.wait_ge(cmax_done, NT)
                            pe.wait_ge(keys_copied, 32)
                        rows, qs = slice(64 * (h % 2), 64 * (h % 2) + 64), nsa_q[:, h // 2]
                        keys = k_win if un['kind'] == 'win' else k_slc
                    L = un['nb'] * P
                    for at in range(0, L, HALF):
                        w = min(HALF, L - at)
                        ins = pe.matmul(bank[2 + 2 * (u % 2) + at // HALF][:, 0:w], qs[rows, n * P:(n + 1) * P],
                                        keys[rows, un['b0'] * P + at:un['b0'] * P + at + w], start=True, stop=True)
                    ins.then_inc(score_done, 1)
                elif what == 'pv':
                    i, u, blocks = item[1:]
                    un = UNITS[u]
                    kind, n, h = un['kind'], un['n'], un['h']
                    pe.wait_ge(fill_out, un['last_fill'] - (un['nb'] - 1) // 4 + blocks[0] // 4 + 1)
                    rows = slice(64 * (h % 2), 64 * (h % 2) + 64)
                    at = 256 * (n % 2) + P * (h // 2)
                    out = bank[7][rows, at:at + P]
                    t = n + NT * (kind != 'swa')
                    first = blocks[0] == 0 and kind != 'sel'
                    if first and h == 0 and t:
                        pe.wait_ge(tile_out, t)
                    if first and kind == 'win':
                        pe.matmul(out, v_cmp[0:NCMP, :], p_cmp_t[0:NCMP, n, h, :], start=True, stop=False)
                    cols = {'swa': slice(64 * (h // 2), 64 * (h // 2) + 64), 'sel': slice(0, 64),
                            'win': slice(64, 128)}[kind]
                    vals = swa_v if kind == 'swa' else vsvw
                    for b in blocks:
                        ins = pe.matmul(out, vals[:, un['b0'] + b, cols], w_t3[:, i % 2, b % 4, :],
                                        start=(b == 0 and kind == 'swa'), stop=(b == un['nb'] - 1 and kind != 'win'))
                    ins.then_inc(pv_done, 1)

        @block.scalar
        def _(act):
            order = Order(act, act_order)

            def half(c, h):
                kind, i, _ = CHUNKS[c]
                act.wait_ge(half_done, 2 * c + h + 1)
                if kind == 'merge':
                    m = gate_index[c] * 2 + h
                    if m >= 2:
                        act.wait_ge(gate_stored[m % 2], 16 * (m // 2))
                    order.after(act.activation(gate_out[:, m % 2, :], bank[h][:, :], ACT.Tanh, scale=0.5))
                    act.nop().then_inc(half_out, 1)
                    act.dma_start(gates[i[0], i[1], :, h * HALF:(h + 1) * HALF], gate_out[:, m % 2, :]
                                  ).then_inc(gate_stored[m % 2], 16)
                    return
                if h == 0:
                    if (kind, i) == ('ret_q', 0):
                        act.wait_ge(x_t, 16)
                    if (kind, i) == ('ret_q', 1):
                        act.wait_ge(conv_stored, 16)
                    if (kind, i) == ('swa_q', 0):
                        act.wait_ge(ret_stored, 16)
                    if (kind, i) == ('nsa_q', 0):
                        act.wait_ge(ret_stored, 32)
                if kind == 'kskw':
                    cols = slice(h * HALF, (h + 1) * HALF)
                    act.activation(k_slc[0:64, cols], bank[h][0:64, :], ACT.Copy)
                    act.activation(k_win[64:128, cols], bank[h][64:128, :], ACT.Copy).then_inc(half_out, 1)
                    return
                f, kw = (ACT.Tanh, dict(scale=0.5)) if kind in ('conv_gate', 'gate') else (ACT.Copy, {})
                act.activation(home(c, h), bank[h][:, :], f, **kw).then_inc(half_out, 1)

            gate_index = {c: g for g, c in enumerate(c for c in range(NCH) if CHUNKS[c][0] == 'merge')}
            for item in SCHEDULE:
                what = item[0]
                if what == 'xt' and item[1] in (5, 11):
                    c = item[1] // 8
                    act.wait_ge(w_in_s[c], raw_total(c))
                    act.activation(w_hi[:, c, :, :], w_raw[:, c, :, :], ACT.Copy).then_inc(w_hi_ready, 1)
                if what == 'mm':
                    q = item[1]
                    c, h = q // 4, q // 2 % 2
                    if q % 2 == 1:
                        half(c, h)
                elif what == 'xt':
                    g = item[1]
                    h, k = g // 8, g % 8
                    act.wait_ge(x_t, g + 1)
                    act.activation(x_hi[:, k, h * HALF:(h + 1) * HALF], bank[2 + g % 4][:, :], ACT.Copy
                                   ).then_inc(x_hi_ready, 1)
                elif what == 'conv_var':
                    act.wait_ge(eps_ready, 1)
                    act.wait_ge(conv_var_done, 1)
                    for h in range(2):
                        ins = act.activation(conv_r[:, h * HALF:(h + 1) * HALF], bank[4 + h][:, :], ACT.Sqrt,
                                             bias=eps[:, 0:1])
                    ins.then_inc(conv_sd, 1)
                elif what == 'conv_out':
                    act.wait_ge(conv_norm, 1)
                    act.activation(conv_gate, conv_y, ACT.Tanh).then_inc(conv_th, 1)
                elif what == 'ret_a':
                    pair, n = item[1:]
                    i = NT * pair + n
                    s, T = i % 2, bank[2 + 3 * (i % 2)]
                    act.wait_ge(ret_a_done, i + 1)
                    if i >= 2:
                        act.wait_ge(ret_b_done, i - 1)
                    act.activation(v_n[:, s, :, :], T[:, 0:2 * P], ACT.Copy)
                    act.activation(RET[pair]['g'][:, :, n * P:(n + 1) * P],
                                   T[:, 2 * P:4 * P].rearrange('p (e c) -> p e c', e=2), ACT.Copy).then_inc(ret_v_out, 1)
                elif what == 'ret_norm':
                    pair = item[1]
                    act.wait_ge(ret_v_out, NT * (pair + 1))
                    act.activation(RET[pair]['th'], RET[pair]['g'], ACT.Tanh, scale=0.5).then_inc(ret_th, 1)
                    act.wait_ge(ret_mv, pair + 1)
                    act.activation(o_rstd[:, :], o_mv[:, :, 1], ACT.Sqrt, bias=eps[:, 0:1]).then_inc(ret_sd, 1)
                elif what == 'fill':
                    f, kind, a = item[1:]
                    B = bank[6]
                    act.wait_ge(fill_done, f + 1)
                    if kind == 'ret':
                        pair, g = a
                        out, src = RET[pair]['out'][:, g // 2, HALF * (g % 2):HALF * (g % 2) + HALF], B[:, :]
                    elif kind in ('swa_v', 'vsvw'):
                        out, src = (swa_v if kind == 'swa_v' else vsvw)[:, 4 * a[0]:4 * a[0] + 4, :], B[:, :]
                    elif kind == 'gate':
                        act.activation(gate_n[:, :, :], B[:, 0:96].rearrange('p (n g) -> p n g', n=NT), ACT.Copy, scale=0.5,
                                       bias=0.5).then_inc(fill_out, 1)
                        continue
                    elif kind == 'pe':
                        out, src = pe_t[:, :], B[:, 0:32]
                    elif kind == 'cmp':
                        if a[0] == 0:
                            act.wait_ge(hid_done, 1)
                        out, src = p_cmp_t[0:NCMP, a[0], :, :], B[0:NCMP, :]
                    else:
                        _, blocks, i = a
                        if i >= 2:
                            act.wait_ge(pv_done, i - 1)
                        out, src = w_t[:, i % 2, 0:len(blocks) * P], B[:, 0:len(blocks) * P]
                    act.activation(out, src, ACT.Copy).then_inc(fill_out, 1)
                elif what == 'out':
                    kind, n = item[1:]
                    t = n + NT * (kind != 'swa')
                    last = (SWA[4 * n + 3] if kind == 'swa' else NSA[8 * n + 7])['last_pv']
                    act.wait_ge(pv_done, last + 1)
                    if t >= 2:
                        act.wait_ge(tile_stored[n % 2], 16 * (t // 2))
                    act.activation(out_t[:, n % 2], bank[7][:, 256 * (n % 2):256 * (n % 2) + 256], ACT.Copy
                                   ).then_inc(tile_out, 1)
                elif what == 'exp':
                    un = UNITS[item[1]]
                    u, s, L = un['u'], un['u'] % 3, un['nb'] * P
                    act.wait_ge(max_done, u + 1)
                    if u >= 3:
                        act.wait_ge(soft_done, u - 2)
                    if un['kind'] == 'swa':
                        act.activation(e_sink[:, s:s + 1], sink8[:, un['h']:un['h'] + 1], ACT.Exp, scale=0.125,
                                       bias=m_neg[:, s:s + 1])
                    act.activation(soft[:, s, 0:L], soft[:, s, 0:L], ACT.Exp, scale=0.125, bias=m_neg[:, s:s + 1],
                                   accum_out=den[:, s:s + 1]).then_inc(exp_done, 1)
                elif what == 'hidden':
                    act.wait_ge(hid_done, 1)
                    for kv in range(2):
                        ins = act.activation(hid_n[0:NCMP, kv, :], bank[2 + 3 * kv][0:NCMP, 0:CMP_HID], ACT.Gelu)
                    ins.then_inc(hid_gelu, 1)
                elif what == 'hidden_t':
                    act.wait_ge(hid_t_done, 1)
                    act.activation(hid[:, :, 0:NCMP],
                                   bank[2][:, 0:256].rearrange('p (j c) -> p j c', j=4)[:, :, 0:NCMP], ACT.Copy
                                   ).then_inc(hid_out, 1)
                elif what == 'compress':
                    act.wait_ge(cmp_done, 1)
                    act.activation(k_cmp[:, 0:NCMP], bank[3][:, 0:NCMP], ACT.Copy)
                    act.activation(v_cmp[0:NCMP, :], bank[4][0:NCMP, 0:DH], ACT.Copy).then_inc(cmp_out, 1)
                elif what == 'cmp_score':
                    n = item[1]
                    act.wait_ge(cmax_done, n + 1)
                    act.activation(cs[:, n % 2, :, :], cs[:, n % 2, :, :], ACT.Exp, scale=0.125).then_inc(cexp_done, 1)
            for i in range(2):
                act.wait_ge(gate_stored[i], 16 * len(gate_index))

        @block.vector
        def _(dve):
            order = Order(dve, dve_order)

            dve.memset(eps[:, :], EPS).then_inc(eps_ready, 1)
            dve.memset(state[:, :, :], 0.0).then_inc(state_zero, 1)
            order.after(dve.memset(conv_h[:, :, 0:CONV_K - 1], 0.0))
            for item in SCHEDULE:
                what = item[0]
                if what == 'xt' and item[1] in (5, 11):
                    c = item[1] // 8
                    dve.wait_ge(w_hi_ready, c + 1)
                    dve.tensor_tensor(w_lo[:, c, :, :], w_raw[:, c, :, :], w_hi[:, c, :, :].bitcast(F32),
                                      ALU.subtract).then_inc(w_lo_ready, 1)
                if what == 'xt':
                    g = item[1]
                    h, k = g // 8, g % 8
                    cols = slice(h * HALF, (h + 1) * HALF)
                    dve.wait_ge(x_hi_ready, g + 1)
                    dve.tensor_tensor(x_lo[:, k, cols], bank[2 + g % 4][:, :], x_hi[:, k, cols].bitcast(F32),
                                      ALU.subtract).then_inc(x_lo_ready, 1)
                elif what == 'conv_h':
                    dve.wait_ge(conv_params, 1)
                    order.after(dve.tensor_copy(conv_p[:, :, :], bank[6][:, 0:68].rearrange('p (c k) -> p c k', c=2)))
                    order.after(dve.tensor_scalar(conv_p[:, :, 0:31], conv_p[:, :, 0:31], 0.5, None, ALU.mult))
                    order.after(dve.tensor_scalar(conv_p[:, :, 32:34], conv_p[:, :, 32:34], 0.5, None, ALU.mult))
                    dve.wait_ge(half_out, 2 * WHERE['conv_a', 1] + 2)
                    for c in range(2):
                        body = conv_h[:, c, CONV_K - 1:]
                        order.after(dve.scalar_tensor_tensor(body, conv_gate[:, c, :], 1.0, body, ALU.add, ALU.mult))
                elif what == 'tap':
                    k = item[1]
                    for c in range(2):
                        if k == 0:
                            ins = dve.tensor_scalar(conv_y[:, c, :], conv_h[:, c, 0:S], conv_p[:, c, 0:1],
                                                    conv_p[:, c, 31:32], ALU.mult, ALU.add)
                        else:
                            dve.wait_ge(taps_done, 2 * k - 1 + c)
                            ins = dve.scalar_tensor_tensor(conv_y[:, c, :], conv_h[:, c, k:k + S], conv_p[:, c, k:k + 1],
                                                           conv_y[:, c, :], ALU.mult, ALU.add)
                        ins.then_inc(taps_done, 1)
                elif what == 'conv_mean':
                    dve.wait_ge(conv_mean_done, 1)
                    for h in range(2):
                        cols = slice(h * HALF, (h + 1) * HALF)
                        order.after(dve.tensor_tensor(conv_y[:, :, cols], conv_y[:, :, cols],
                                                      bcast(bank[2 + h][:, :], 1, 2), ALU.subtract))
                    dve.tensor_tensor(conv_gate, conv_y, conv_y, ALU.mult).then_inc(conv_sq, 1)
                elif what == 'conv_var':
                    dve.wait_ge(conv_sd, 1)
                    order.after(dve.reciprocal(conv_r, conv_r))
                    order.after(dve.tensor_tensor(conv_y, conv_y, bcast(conv_r, 1, 2), ALU.mult))
                    for c in range(2):
                        ins = dve.tensor_scalar(conv_y[:, c, :], conv_y[:, c, :], conv_p[:, c, 32:33],
                                                conv_p[:, c, 33:34], ALU.mult, ALU.add)
                    ins.then_inc(conv_norm, 1)
                elif what == 'conv_out':
                    dve.wait_ge(conv_th, 1)
                    dve.wait_ge(conv_norm, 1)
                    dve.scalar_tensor_tensor(conv_y, conv_gate, 1.0, conv_y, ALU.add, ALU.mult).then_inc(conv_fin, 1)
                elif what == 'ret_a':
                    pair, n = item[1:]
                    i = NT * pair + n
                    s, R, K = i % 2, RET[pair], bank[3 + 3 * (i % 2)]
                    dve.wait_ge(ret_a_done, i + 1)
                    if i >= 2:
                        dve.wait_ge(ret_b_done, i - 1)
                    for e, src in enumerate((K[:, P:2 * P], bank[4 + 3 * s][:, 3 * P:4 * P])):
                        dve.tensor_tensor(inner[:, s, e, :], src,
                                          const('decay')[:, (2 * pair + e) * P:(2 * pair + e + 1) * P], ALU.mult)
                    dve.tensor_tensor(k_z[:, s, :].rearrange('p (e c) -> p e c', e=2),
                                      K[:, 0:P].rearrange('p (e c) -> p e c', e=2),
                                      bcast(const('zeta')[:, 2 * pair:2 * pair + 2], 2, 64), ALU.mult)
                    dve.tensor_tensor(q_xi[:, s, :], R['q'][:, n * P:(n + 1) * P],
                                      const('xi')[:, pair * P:(pair + 1) * P], ALU.mult).then_inc(ret_mid, 1)
                elif what == 'ret_b':
                    pair, n = item[1:]
                    i = NT * pair + n
                    R, O = RET[pair], bank[4 + 3 * (i % 2)]
                    dve.wait_ge(ret_b_done, i + 1)
                    kv = O[:, 2 * P:3 * P]
                    if n == NT - 1:
                        dve.memset(state[:, :, :], 0.0)
                    else:
                        for e in range(2):
                            rows = slice(64 * e, 64 * e + 64)
                            dve.scalar_tensor_tensor(state[rows, e, :], state[rows, e, :],
                                                     const('chunk_decay')[rows, pair:pair + 1], kv[rows, :],
                                                     ALU.mult, ALU.add)
                    for e in range(2):
                        dve.bn_stats(o_stats[:, e * NT + n, :], O[:, e * P:(e + 1) * P])
                    dve.tensor_copy(R['v'][:, :, n * P:(n + 1) * P],
                                    O[:, 0:2 * P].rearrange('p (e c) -> p e c', e=2)).then_inc(ret_state, 1)
                elif what == 'ret_norm':
                    pair = item[1]
                    R = RET[pair]
                    dve.wait_ge(ret_state, NT * (pair + 1))
                    for j in range(16):
                        ins = dve.bn_aggr(o_mv[:, j, :], o_stats[:, j, :])
                    ins.then_inc(ret_mv, 1)
                    if pair == 0:
                        dve.wait_ge(gn_in, 32)
                        order.after(dve.tensor_scalar(reg_s[:, 2048:3072], reg_s[:, 2048:3072], 0.5, None, ALU.mult))
                    dve.wait_ge(ret_sd, pair + 1)
                    order.after(dve.reciprocal(o_rstd[:, :], o_rstd[:, :]))
                    for e in range(2):
                        for n in range(NT):
                            j, blk = e * NT + n, R['v'][:, e, n * P:(n + 1) * P]
                            ins = dve.tensor_scalar(blk, blk, o_mv[:, j, 0:1], o_rstd[:, j:j + 1], ALU.subtract,
                                                    ALU.mult)
                    order.after(ins)
                    per = lambda ap: ap.rearrange('p (n c) -> p n c', c=P)
                    for table, op in ((gn_g, ALU.mult), (gn_b, ALU.add)):
                        for e in range(2):
                            o = per(R['v'][:, e, :])
                            ins = dve.tensor_tensor(o, o, bcast(table[:, 2 * pair + e, :], 1, NT), op)
                        order.after(ins)
                    dve.wait_ge(ret_th, pair + 1)
                    order.after(dve.scalar_tensor_tensor(R['g'], R['th'], 1.0, R['g'], ALU.add, ALU.mult))
                    dve.tensor_tensor(R['v'], R['v'], R['g'], ALU.mult).then_inc(ret_fin, 1)
                elif what == 'sel_table':
                    n = item[1]
                    order.after(dve.tensor_tensor(
                        dist_n[:, 0:(n + 1) * P].rearrange('p (b l) -> p b l', l=SLC),
                        const('dist_sel')[:, 896 - P * n:1024].rearrange('p (b l) -> p b l', l=SLC),
                        bcast(sel_pen[:, n, 0:2 * n + 2], 2, SLC), ALU.add))
                elif what == 'max':
                    un = UNITS[item[1]]
                    kind, u, n, h, s, L = un['kind'], un['u'], un['n'], un['h'], un['u'] % 3, un['nb'] * P
                    if u == 0:
                        order.after(dve.tensor_scalar(sink8[:, :], sink8[:, :], 8.0, None, ALU.mult))
                    table = {'swa': const('dist_swa'), 'win': const('dist_win'), 'sel': dist_n[:, 0:L]}[kind]
                    table = table[:, table.shape[1] - L:]
                    slope = (SLOPE_SWA if kind == 'swa' else SLOPE_NSA)[h]
                    dve.wait_ge(score_done, u + 1)
                    if u >= 3:
                        dve.wait_ge(fill_done, UNITS[u - 3]['last_fill'] + 1)
                    for at in range(0, L, HALF):
                        w = min(HALF, L - at)
                        ins = dve.scalar_tensor_tensor(soft[:, s, at:at + w], table[:, at:at + w], -8.0 * slope,
                                                       bank[2 + 2 * (u % 2) + at // HALF][:, 0:w], ALU.mult, ALU.add)
                    order.after(ins)
                    order.after(dve.reduce_max(m_raw[:, s:s + 1], soft[:, s, 0:L], AX.X))
                    if kind == 'swa':
                        dve.tensor_scalar(m_neg[:, s:s + 1], m_raw[:, s:s + 1], sink8[:, h:h + 1], -0.125, ALU.max,
                                          ALU.mult).then_inc(max_done, 1)
                    else:
                        dve.tensor_scalar(m_neg[:, s:s + 1], m_raw[:, s:s + 1], -0.125, None, ALU.mult
                                          ).then_inc(max_done, 1)
                elif what == 'norm':
                    un = UNITS[item[1]]
                    kind, u, n, h, s, L = un['kind'], un['u'], un['n'], un['h'], un['u'] % 3, un['nb'] * P
                    dve.wait_ge(exp_done, u + 1)
                    if kind == 'swa':
                        order.after(dve.tensor_scalar(den[:, s:s + 1], den[:, s:s + 1], e_sink[:, s:s + 1], 1e-30,
                                                      ALU.add, ALU.max))
                    else:
                        order.after(dve.tensor_scalar(den[:, s:s + 1], den[:, s:s + 1], 1e-30, None, ALU.max))
                    order.after(dve.reciprocal(rden[:, s:s + 1], den[:, s:s + 1]))
                    if kind == 'swa':
                        dve.tensor_scalar(soft[:, s, 0:L], soft[:, s, 0:L], rden[:, s:s + 1], None, ALU.mult
                                          ).then_inc(soft_done, 1)
                    else:
                        col = 4 * (2 if kind == 'win' else 1) + h
                        dve.tensor_scalar(soft[:, s, 0:L], soft[:, s, 0:L], rden[:, s:s + 1], gate_n[:, n, col:col + 1],
                                          ALU.mult, ALU.mult).then_inc(soft_done, 1)
                elif what == 'fill' and item[2] == 'pe':
                    dve.wait_ge(fill_out, item[1] + 1)
                    src = kcvc.rearrange('p (i l) -> p l i', l=CMP_STRIDE)
                    for part in range(2):
                        rows = slice(CMP_STRIDE * part, CMP_STRIDE * (part + 1))
                        dve.tensor_tensor(z_cmp[:, rows, 0:NCMP], src[:, :, part:part + NCMP],
                                          bcast(pe_t[:, rows], 2, NCMP), ALU.add).then_inc(z_ready, 1)
                elif what == 'cmp_score':
                    n = item[1]
                    t = cs[:, n % 2, :, :]
                    if n == 0:
                        order.after(dve.memset(c_all[:, :], 0.0))
                    dve.wait_ge(cscore_done, n + 1)
                    if n >= 2:
                        dve.wait_ge(fill_done, CMP_FILL + n - 1)
                    for h in range(4):
                        B = bank[2 + 2 * (n % 2) + h % 2]
                        ins = dve.scalar_tensor_tensor(cs[:, n % 2, h, :], const('dist_cmp')[:, n * NCMP:(n + 1) * NCMP],
                                                       -8.0 * SLOPE_NSA[h], B[:, h * 64:h * 64 + NCMP], ALU.mult, ALU.add)
                    order.after(ins)
                    order.after(dve.reduce_max(c_max[:, :], t, AX.X))
                    dve.tensor_tensor(t, t, bcast(c_max[:, :], 2, NCMP), ALU.subtract).then_inc(cmax_done, 1)
                    dve.wait_ge(cexp_done, n + 1)
                    order.after(dve.tensor_tensor(t, t, bcast(const('mask_cmp')[:, n * NCMP:(n + 1) * NCMP], 1, 4), ALU.mult))
                    order.after(dve.reduce_sum(c_sum[:, :], t, AX.X))
                    order.after(dve.tensor_scalar(c_sum[:, :], c_sum[:, :], 1e-30, None, ALU.max))
                    order.after(dve.reciprocal(c_sum[:, :], c_sum[:, :]))
                    order.after(dve.tensor_tensor(t, t, bcast(c_sum[:, :], 2, NCMP), ALU.mult))
                    order.after(dve.reduce_sum(c_all[:, 1:64], t.rearrange('p h c -> p c h'), AX.X))
                    order.after(dve.reduce_sum(imp[:, :], c_all[:, 1:65].rearrange('p (j c) -> p j c', c=4), AX.X))
                    order.after(dve.tensor_tensor(imp[:, :], imp[:, :],
                                                  c_all[:, 0:64].rearrange('p (j c) -> p j c', c=4)[:, :, 0], ALU.add))
                    order.after(dve.tensor_tensor(imp[:, :], imp[:, :], const('imp_keep')[:, n * NSLC:(n + 1) * NSLC],
                                                  ALU.mult))
                    order.after(dve.tensor_tensor(imp[:, :], imp[:, :], const('imp_set')[:, n * NSLC:(n + 1) * NSLC],
                                                  ALU.add))
                    order.after(dve.max(imp_top[:, :], imp[:, :]))
                    order.after(dve.match_replace(imp_cut[:, :], imp_top[:, :], imp[:, :], NEG))
                    order.after(dve.tensor_scalar(sel_pen[:, n, :], imp_cut[:, :], NEG, BIG, ALU.not_equal, ALU.mult))
                    dve.tensor_tensor(t, t, bcast(gate_n[:, n, 0:4], 2, NCMP), ALU.mult).then_inc(csoft_done, 1)


CMP_FILL = next(item[1] for item in SCHEDULE if item[0] == 'fill' and item[2] == 'cmp')


EARLY_LOADS = 16 * 5
SPLIT = [(0, 2), (2, 4), (4, 8), (8, 10)]


def merge(nc, d, yt, gates, merged, w_out, y_done, half_merged, wo_in, piece_in, sem):
    with ExitStack() as ctx:
        def sb(name, shape, dt=F32):
            return ctx.enter_context(nc.sbuf_tensor(name, shape, dt))
        y_hi, y_lo = sb('y_hi', [P, 10, S], F32R), sb('y_lo', [P, 10, S], F32R)
        p_hi, p_lo, p_raw = sb('p_hi', [P, 2, 10, P], F32R), sb('p_lo', [P, 2, 10, P], F32R), sb('p_raw', [P, 2, 10, P])
        y_raw = lambda a, b, cols: w_out[:, a:b, cols] if b <= KD else merged[:, a - 2:b - 2, cols]
        g_sb = sb('g_sb', [P, 2, 4, HALF])
        term = sb('term', [P, 2, HALF])
        bank = [ctx.enter_context(nc.psum_tensor(f'b_bank{i}', [P, HALF], F32)) for i in range(8)]
        p_hi_ready, p_lo_ready, y_hi_ready, y_lo_ready, b_order = (
            sem(n) for n in ('p_hi_ready', 'p_lo_ready', 'y_hi_ready', 'y_lo_ready', 'b_order'))
        p_in, g_in = ([sem(f'{n}{i}') for i in range(2)] for n in ('p_in', 'g_in'))
        PIECES = [(a, b, slice(h * HALF, (h + 1) * HALF)) for h in range(2) for a, b in SPLIT]
        block = ctx.enter_context(nc.Block())

        @block.sync
        def _(sp):
            def weights(j):
                cols = slice(j * P, (j + 1) * P)
                if j >= 2:
                    sp.wait_ge(p_lo_ready, j - 1)
                for (a, b), name in zip(SPLIT, ('p_conv', 'p_swa', 'p_ret', 'p_nsa')):
                    sp.dma_start(p_raw[:, j % 2, a:b, :], d[name][0, :, cols].rearrange('(c p) n -> p c n', p=P)
                                 ).then_inc(p_in[j % 2], 16)

            def gate(j, h):
                if j:
                    sp.wait_ge(half_merged, 2 * j + h - 1)
                sp.dma_start(g_sb[:, h, :, :], gates[j, :, :, h * HALF:(h + 1) * HALF].rearrange('b p s -> p b s')
                             ).then_inc(g_in[h], 16)
            weights(0)
            for h in range(2):
                for i, (a, b, cols) in enumerate(PIECES):
                    if i // 4 == h:
                        sp.dma_start(y_raw(a, b, cols), yt[a:b, :, cols].rearrange('c p s -> p c s')
                                     ).then_inc(piece_in[i], 16)
                if h == 0:
                    weights(1)
                gate(0, h)
            for j in range(1, KD):
                gate(j, 0)
                if j + 1 < KD:
                    weights(j + 1)
                gate(j, 1)
                if 2 <= j < 6:
                    k = 2 * (j - 2)
                    sp.wait_ge(y_lo_ready, 8)
                    sp.dma_start(w_out[:, k:k + 2, :], d['w_out'][0, k * P:(k + 2) * P, :].rearrange('(k p) n -> p k n', p=P)
                                 ).then_inc(wo_in, 16)

        @block.tensor
        def _(pe):
            for j in range(KD):
                pe.wait_ge(p_hi_ready, j + 1)
                pe.wait_ge(p_lo_ready, j + 1)
                for h in range(2):
                    cols = slice(h * HALF, (h + 1) * HALF)
                    if j:
                        pe.wait_ge(half_merged, 2 * j + h - 1)
                    for b, (lo, hi) in enumerate(SPLIT):
                        if j == 0:
                            pe.wait_ge(y_lo_ready, 4 * h + b + 1)
                        for c in range(lo, hi):
                            for i, (w, y) in enumerate(((p_hi, y_hi), (p_hi, y_lo), (p_lo, y_hi))):
                                ins = pe.matmul(bank[4 * h + b][:, :], w[:, j % 2, c, :], y[:, c, cols],
                                                start=c == lo and i == 0, stop=c == hi - 1 and i == 2)
                        ins.then_inc(y_done, 1)

        @block.scalar
        def _(act):
            def p_high(j):
                act.wait_ge(p_in[j % 2], 64 * (j // 2 + 1))
                if j >= 2:
                    act.wait_ge(y_done, 8 * (j - 1))
                act.activation(p_hi[:, j % 2, :, :], p_raw[:, j % 2, :, :], ACT.Copy).then_inc(p_hi_ready, 1)
            p_high(0)
            for i, (a, b, cols) in enumerate(PIECES):
                act.wait_ge(piece_in[i], 16)
                act.activation(y_hi[:, a:b, cols], y_raw(a, b, cols), ACT.Copy).then_inc(y_hi_ready, 1)
            for j in range(1, KD):
                p_high(j)

        @block.gpsimd
        def _(pool):
            for j in range(1, KD):
                pool.wait_ge(p_hi_ready, j + 1)
                pool.tensor_tensor(p_lo[:, j % 2, :, :], p_raw[:, j % 2, :, :], p_hi[:, j % 2, :, :].bitcast(F32),
                                   ALU.subtract).then_inc(p_lo_ready, 1)

        @block.vector
        def _(dve):
            order = Order(dve, b_order)
            dve.wait_ge(p_hi_ready, 1)
            dve.tensor_tensor(p_lo[:, 0, :, :], p_raw[:, 0, :, :], p_hi[:, 0, :, :].bitcast(F32), ALU.subtract
                              ).then_inc(p_lo_ready, 1)
            for i, (a, b, cols) in enumerate(PIECES):
                dve.wait_ge(y_hi_ready, i + 1)
                dve.tensor_tensor(y_lo[:, a:b, cols], y_raw(a, b, cols), y_hi[:, a:b, cols].bitcast(F32), ALU.subtract
                                  ).then_inc(y_lo_ready, 1)
            for j in range(KD):
                for h in range(2):
                    dve.wait_ge(g_in[h], 16 * (j + 1))
                    cols = slice(h * HALF, (h + 1) * HALF)
                    total = merged[:, j, cols]
                    for b in range(4):
                        dve.wait_ge(y_done, 8 * j + 4 * h + b + 1)
                        out = total if b == 0 else term[:, b % 2, :]
                        order.after(dve.scalar_tensor_tensor(out, g_sb[:, h, b, :], 1.0, bank[4 * h + b][:, :],
                                                             ALU.add, ALU.mult))
                        if b:
                            ins = dve.tensor_tensor(total, total, out, ALU.add)
                            if b < 3:
                                order.after(ins)
                    ins.then_inc(half_merged, 1)


def project(nc, d, merged, w_out, half_merged, wo_in, consts_moe, early, x1d, x1_n, x1_t, logits, sem):
    cst, rb, sh, e_in, s_gu_done, bank = early[:6]
    with ExitStack() as ctx:
        def sb(name, shape, dt=F32):
            return ctx.enter_context(nc.sbuf_tensor(name, shape, dt))
        late = sb('late', [P, 4 * S])
        s_gu = sh[:, 0:4096].rearrange('p (k f) -> p k f', k=KD)
        s_d = sh[:, 4096:6144].rearrange('p (k n) -> p k n', k=2)
        x_row, g1, b1 = late[:, 0:2 * D].rearrange('p (r d) -> p r d', r=2), late[:, 2 * D:3 * D], late[:, 3 * D:4 * D]
        r_nat, r_t = sb('r_nat', [E, D]), sb('r_t', [P, KD, E])
        stats, mv, sd = sb('ln_stats', [P, 2, 2, 6]), sb('ln_mv', [P, 2, 2]), sb('ln_sd', [P, 2])
        ident, eps = sb('b_ident', [P, P]), sb('b_eps', [P, 1])

        ln_in, id_in = sem('ln_in'), sem('id_in')
        x_in = [sem('xr_in0'), sem('xr_in1')]
        r_tr, r_ready, c_order, eps_set = sem('r_tr'), sem('r_ready'), sem('c_order'), sem('b_eps_set')
        mix_done, xa_ready, mv_done, sd_done, pre_read, x1_done = (sem('mix_done'), sem('xa_ready'), sem('mv_done'),
                                                                   sem('sd_done'), sem('pre_read'), sem('x1_done'))
        x1_tr, x1_t_out, router_done, x1_stored = sem('x1_tr'), sem('x1_t_out'), sem('router_done'), sem('x1_stored')
        block = ctx.enter_context(nc.Block())

        @block.sync
        def _(sp):
            sp.dma_start(ident[:, :], d['ident']).then_inc(id_in, 16)
            sp.dma_start(r_nat[:, :], d['router_w'][0]).then_inc(id_in, 16)
            sp.dma_start(g1, d['ln1_g'].broadcast_to([P, D])).then_inc(ln_in, 16)
            sp.dma_start(b1, d['ln1_b'].broadcast_to([P, D])).then_inc(ln_in, 16)
            for t in range(2):
                sp.dma_start(x_row[:, t % 2, :], d['x'][0, t * P:(t + 1) * P, :]).then_inc(x_in[t % 2], 16)
            sp.dma_start(cst[:, :], consts_moe).then_inc(e_in, 16)
            sp.dma_start(rb[:, :], d['router_b'].broadcast_to([P, E])).then_inc(e_in, 16)
            for i, name in enumerate(('sh_wg', 'sh_wu')):
                sp.dma_start(s_gu[:, :, i * FE:(i + 1) * FE], d[name][0].rearrange('(k p) f -> p k f', p=P)
                             ).then_inc(e_in, 16)
            sp.dma_start(s_d[:, :, :], d['sh_wd'][0].rearrange('(k p) n -> p k n', p=P)).then_inc(e_in, 16)
            for t in range(2, NT):
                sp.wait_ge(pre_read, t - 1)
                sp.dma_start(x_row[:, t % 2, :], d['x'][0, t * P:(t + 1) * P, :]).then_inc(x_in[t % 2], 16)
                sp.wait_ge(x1_done, t - 1)
                sp.dma_start(x1d[(t - 2) * P:(t - 1) * P, :], x1_n[:, t - 2, :]).then_inc(x1_stored, 16)
            for t in (NT - 2, NT - 1):
                sp.wait_ge(x1_done, t + 1)
                sp.dma_start(x1d[t * P:(t + 1) * P, :], x1_n[:, t, :]).then_inc(x1_stored, 16)
            sp.wait_ge(x1_stored, 16 * NT)

        @block.tensor
        def _(pe):
            def rows_out(t):
                if t >= 2:
                    pe.wait_ge(pre_read, t - 1)
                for h in range(2):
                    for k in range(KD):
                        ins = pe.matmul(bank[2 * (t % 2) + h][:, :], merged[:, k, t * P:(t + 1) * P],
                                        w_out[:, k, h * HALF:(h + 1) * HALF], start=k == 0, stop=k == KD - 1)
                ins.then_inc(mix_done, 1)
            pe.wait_ge(half_merged, 2 * KD)
            pe.wait_ge(wo_in, 64)
            rows_out(0)
            pe.wait_ge(id_in, 32)
            for k in range(KD):
                ins = pe.transpose(bank[7][:, k * E:(k + 1) * E], r_nat[:, k * P:(k + 1) * P], ident[0:E, 0:E])
            ins.then_inc(r_tr, 1)

            def router(t):
                pe.wait_ge(r_ready, 1)
                pe.wait_ge(x1_t_out, t + 1)
                for k in range(KD):
                    ins = pe.matmul(bank[6][:, t * E:(t + 1) * E], x1_t[:, k, t * P:(t + 1) * P], r_t[:, k, :],
                                    start=k == 0, stop=k == KD - 1)
                return ins
            for t in range(NT):
                if t + 1 < NT:
                    rows_out(t + 1)
                if t:
                    router(t - 1)
                if t == NT - 1:
                    pe.wait_ge(pre_read, NT - 1)
                    pe.wait_ge(e_in, EARLY_LOADS)
                    for i in range(2):
                        for k in range(KD):
                            ins = pe.matmul(bank[i][:, :], x1_t[:, k, i * P:(i + 1) * P], s_gu[:, k, :],
                                            start=k == 0, stop=k == KD - 1)
                        ins.then_inc(s_gu_done, 1)
                pe.wait_ge(x1_done, t + 1)
                if t:
                    pe.wait_ge(x1_t_out, t)
                for k in range(KD):
                    ins = pe.transpose(bank[4 + k // 4][:, (k % 4) * P:(k % 4 + 1) * P], x1_n[:, t, k * P:(k + 1) * P],
                                       ident[:, :])
                ins.then_inc(x1_tr, 1)
            ins = router(NT - 1)
            ins.then_inc(router_done, 1)

        @block.scalar
        def _(act):
            act.wait_ge(r_tr, 1)
            act.activation(r_t[:, :, :], bank[7][:, :].rearrange('p (k e) -> p k e', e=E), ACT.Copy).then_inc(r_ready, 1)

            act.wait_ge(eps_set, 1)

            def scaled(t):
                act.wait_ge(x_in[t % 2], 16 * (t // 2 + 1))
                act.activation(x_row[:, t % 2, :], x_row[:, t % 2, :], ACT.Copy, scale=ALPHA).then_inc(xa_ready, 1)
            scaled(0)
            for t in range(NT):
                if t + 1 < NT:
                    scaled(t + 1)
                act.wait_ge(mv_done, t + 1)
                act.activation(sd[:, t % 2:t % 2 + 1], mv[:, t % 2, 1:2], ACT.Sqrt, bias=eps[:, 0:1]).then_inc(sd_done, 1)
                act.wait_ge(x1_tr, t + 1)
                for h in range(2):
                    ins = act.activation(x1_t[:, 4 * h:4 * h + 4, t * P:(t + 1) * P],
                                         bank[4 + h][:, :].rearrange('p (k c) -> p k c', k=4), ACT.Copy)
                ins.then_inc(x1_t_out, 1)
            act.wait_ge(router_done, 1)
            act.activation(logits[:, :, :], bank[6][:, :].rearrange('p (n e) -> p n e', e=E), ACT.Sigmoid
                           ).then_inc(r_ready, 1)
            act.wait_ge(r_ready, 2)

        @block.vector
        def _(dve):
            order = Order(dve, c_order)
            dve.memset(eps[:, :], EPS).then_inc(eps_set, 1)
            dve.wait_ge(half_merged, 2 * KD)
            dve.wait_ge(ln_in, 32)
            for t in range(NT):
                s, row = t % 2, x1_n[:, t, :]
                dve.wait_ge(mix_done, t + 1)
                dve.wait_ge(xa_ready, t + 1)
                for h in range(2):
                    cols = slice(h * HALF, (h + 1) * HALF)
                    ins = dve.scalar_tensor_tensor(x1_n[:, t, cols], bank[2 * s + h][:, :], 0.5, x_row[:, s, cols],
                                                   ALU.mult, ALU.add)
                ins.then_inc(pre_read, 1)
                dve.wait_ge(pre_read, t + 1)
                for h in range(2):
                    ins = dve.bn_stats(stats[:, s, h, :], x1_n[:, t, h * HALF:(h + 1) * HALF])
                order.after(ins)
                dve.bn_aggr(mv[:, s, :], stats[:, s, :, :]).then_inc(mv_done, 1)
                dve.wait_ge(sd_done, t + 1)
                order.after(dve.reciprocal(sd[:, s:s + 1], sd[:, s:s + 1]))
                order.after(dve.tensor_scalar(row, row, mv[:, s, 0:1], sd[:, s:s + 1], ALU.subtract, ALU.mult))
                order.after(dve.tensor_tensor(row, row, g1, ALU.mult))
                dve.tensor_tensor(row, row, b1, ALU.add).then_inc(x1_done, 1)


def experts(nc, d, c_at, early, work, w_gu, x1d, acc, x1_n, x1_t, scores, scratch, out, sem):
    with ExitStack() as ctx:
        def sb(name, shape, dt=F32):
            return ctx.enter_context(nc.sbuf_tensor(name, shape, dt))
        cst, rb, sh, e_in, s_gu_done, bank, acc_row_in = early
        s_gu = sh[:, 0:4096].rearrange('p (k f) -> p k f', k=KD)
        s_d = sh[:, 4096:6144].rearrange('p (k n) -> p k n', k=2)

        def const(name):
            at, width = c_at[name]
            return cst[:, at:at + width]
        ident = const('ident')
        w_gu = w_gu.rearrange('p (s m k f) -> p s m k f', s=2, m=2, k=KD)
        w_d = sb('w_d', [P, 2, 2, D])
        area = work
        w4 = lambda i: area[:, 2048 * i:2048 * (i + 1)].rearrange('p (s c) -> p s c', s=2)
        x_g, y_out = w4(0), w4(2)
        x_gt = area[:, 2048:4096].rearrange('p (s k c) -> p s k c', s=2, c=P)
        one_hot = sb('one_hot', [P, 2, NT, P], BF16)
        r3 = lambda i, w=E: area[:, 512 * i:512 * i + NT * w].rearrange('p (n e) -> p n e', n=NT)
        r4 = lambda i: area[:, 512 * i:512 * (i + 1)].rearrange('p (n g h) -> p n g h', n=NT, g=NG)
        biased, t8, t_gt, t_ge = r3(0), r4(1), r4(2), r4(3)
        cand, cut = r3(4, E + 2), r3(6, E + 2)
        mask, run = r3(8), r3(9)
        gate_w, cmp8 = r3(10), r4(11)
        gs, keep = sb('gs', [P, NT, NG]), sb('keep', [P, NT, NG])
        top = sb('top', [P, NT, 8])
        g_sum = sb('g_sum', [P, NT])
        pos = sb('pos', [P, NT, E])
        info = sb('info', [P, NT, E, 6], BF16)
        n_blk, end_blk, le = sb('n_blk', [P, E]), sb('end_blk', [P, E]), sb('le', [P, E])
        ek = sb('ek', [P, 4])
        table = sb('table', [1, 2 * MAXB + 1], I32)
        hidden, silu, u_sb, hid_t = sb('hidden', [P, 2, FE]), sb('silu', [P, 2, FE]), sb('u_sb', [P, 2, FE]), sb('hid_t', [P, 2, P])
        found, idx_f = sb('found', [P, 2, 6]), sb('idx_f', [P, 1])
        row_gate = sb('row_gate', [P, 4])
        idx_kept, idx, idx_out = sb('idx_kept', [P, 2], I32), sb('idx', [P, 2], I32), sb('idx_out', [P, 2], I32)
        s_row, s_acc = area[:, 6144:8192].rearrange('p (s d) -> p s d', s=2), scratch[:, 2 * NT * D:2 * NT * D + 2 * D].rearrange('p (s d) -> p s d', s=2)
        zero = s_row[:, 0, :]
        g2, b2 = s_gu[:, 0:2, :].rearrange('p a b -> p (a b)'), s_gu[:, 2:4, :].rearrange('p a b -> p (a b)')
        stats, mv, sd, eps = sb('ln2_stats', [P, 2, 2, 6]), sb('ln2_mv', [P, 2, 2]), sb('ln2_sd', [P, 2]), sb('e_eps', [P, 1])
        rows2 = x1_t[:, :, :]

        zero_set = sem('zero_set')
        d_order, mask_done, pos_done, ek_done, tab_done, tab_ready, route_ready = (
            sem('d_order'), sem('mask_done'), sem('pos_done'), sem('ek_done'), sem('tab_done'), sem('tab_ready'),
            sem('route_ready'))
        s_silu, s_h, s_ht, s_ht_out, s_down, s_y, s_acc_ready = (
            sem(n) for n in ('s_silu', 's_h', 's_ht', 's_ht_out', 's_down', 's_y', 's_acc_ready'))
        acc_in = [sem('acc_in0'), sem('acc_in1')]
        w_gu_in, w_d_in, gathered = ([sem(f'{n}{i}') for i in range(2)] for n in ('w_gu_in', 'w_d_in', 'gathered'))
        oh_ready, idx_done, idx_ready, xt_done, xgt_ready, gu_done, sg_ready, h_ready, ht_done, ht_ready, down_done, \
            y_act, y_dve, scattered, gathers, so_ready = (
                sem(n) for n in ('oh_ready', 'idx_done', 'idx_ready', 'xt_done', 'xgt_ready', 'gu_done', 'sg_ready',
                                 'h_ready', 'ht_done', 'ht_ready', 'down_done', 'y_act', 'y_dve', 'scattered', 'gathers', 'so_ready'))
        scale, shift = sb('ln2_scale', [P, NT]), sb('ln2_shift', [P, NT])
        scale_done, normed, gained = sem('scale_done'), sem('normed'), sem('gained')
        ln_in2, eps_set2, mv_done2, sd_done2, row_done, out_stored, f_order = (
            sem(n) for n in ('ln_in2', 'eps_set2', 'mv_done2', 'sd_done2', 'row_done', 'out_stored', 'f_order'))
        block = ctx.enter_context(nc.Block())
        CREDIT = ((gu_done, 2), (h_ready, 2), (ht_done, 2), (down_done, 2), (y_act, 1), (y_dve, 1), (xt_done, 1),
                  (ht_ready, 1))

        def trips(eng):
            eng.wait_ge(tab_ready, 1)
            return eng.value_load(table[0:1, 2 * MAXB:2 * MAXB + 1], min_val=1, max_val=MAXB // 2 - 4)

        def expert_of(eng, b):
            return eng.value_load(table[0:1, bass.ds(b, 1)], min_val=0, max_val=E - 1)

        @block.sync
        def _(sp):
            n = trips(sp)

            def load_up(blk, s):
                e = expert_of(sp, blk)
                sp.wait_ge(gu_done, blk + 1)
                for m, name in enumerate(('moe_wg', 'moe_wu')):
                    sp.dma_start(w_gu[:, s, m, :, :].rearrange('p k f -> p (k f)'),
                                 d[name][0, bass.ds(e, 1)].rearrange('a (p k) f -> p (a k f)', k=KD)
                                 ).then_inc(w_gu_in[s], 16)

            def load_down(blk, s):
                e = expert_of(sp, blk)
                sp.wait_ge(down_done, blk + 1)
                sp.dma_start(w_d[:, s, :, :].rearrange('p k f -> p (k f)'),
                             d['moe_wd'][0, bass.ds(e, 1)].rearrange('a (p k) f -> p (a k f)', k=2)
                             ).then_inc(w_d_in[s], 16)
            load_up(0, 0)
            with sp.Fori(0, n) as i:
                for s in range(2):
                    load_up(2 * i + s + 1, 1 - s)
                    load_down(2 * i + s, s)
            load_up(2 * n + 1, 1)
            for s in range(2):
                load_down(2 * n + s, s)
            sp.dma_start(g2, d['ln2_g'].broadcast_to([P, D])).then_inc(ln_in2, 16)
            sp.dma_start(b2, d['ln2_b'].broadcast_to([P, D])).then_inc(ln_in2, 16)
            sp.wait_ge(scattered, 32 * n + 64)
            for t in range(NT):
                sp.dma_start(rows2[:, t, :], acc[t * P:(t + 1) * P, :]).then_inc(acc_row_in[t], 16)
            for t in range(NT):
                sp.wait_ge(row_done, t + 1)
                sp.dma_start(out[0, t * P:(t + 1) * P, :], rows2[:, t, :]).then_inc(out_stored, 16)
            sp.wait_ge(out_stored, 16 * NT)

        @block.gpsimd
        def _(pool):

            def gather(s, blk):
                pool.wait_ge(idx_ready, blk + 1)
                if not isinstance(blk, int) or blk >= 2:
                    pool.wait_ge(xt_done, blk)
                pool.sem_inc(gathers, 1)
                pool.indirect_dma_start(out=x_g[:, s, :], out_offset=None, in_=x1d[:, :],
                                        in_offset=bass.IndirectOffsetOnAxis(ap=idx[:, s:s + 1], axis=0)
                                        ).then_inc(gathered[s], 16)


            def shared_hidden(t):
                s = t % 2
                pool.wait_ge(s_silu, t + 1)
                if t >= 2:
                    pool.wait_ge(s_ht, t - 1)
                pool.tensor_tensor(hidden[:, s, :], silu[:, s, :], u_sb[:, s, :], ALU.mult).then_inc(s_h, 1)
            shared_hidden(0)
            pool.memset(zero, 0.0).then_inc(zero_set, 1)
            pool.wait_ge(zero_set, 1)
            pool.dma_start(acc[S:S + P, :], zero).then_inc(scattered, 16)
            pool.dma_start(x1d[S:S + P, :], zero).then_inc(scattered, 16)
            pool.wait_ge(scattered, 32)
            for t in range(NT):
                s = t % 2
                if t + 1 < NT:
                    shared_hidden(t + 1)
                pool.wait_ge(s_y, t + 1)
                pool.tensor_tensor(s_acc[:, s, :], s_acc[:, s, :], s_row[:, s, :], ALU.add).then_inc(s_acc_ready, 1)
                pool.wait_ge(s_acc_ready, t + 1)
                pool.dma_start(acc[t * P:(t + 1) * P, :], s_acc[:, s, :]).then_inc(acc_in[s], 16)
                if t in (5, 6):
                    gather(t - 5, t - 5)
            for s in range(2):
                pool.wait_ge(acc_in[s], 16 * NT // 2)
            n = trips(pool)

            def body(b, s, ahead=True):
                if ahead:
                    gather(1 - s, b + 3)
                pool.wait_ge(y_act, b + 2)
                pool.wait_ge(y_dve, b + 2)
                pool.wait_ge(so_ready, b + 1)
                pool.wait_ge(scattered, 16 * b + 32)
                pool.sem_inc(gathers, 1)
                pool.indirect_dma_start(out=acc[:, :], out_offset=bass.IndirectOffsetOnAxis(ap=idx_out[:, s:s + 1], axis=0),
                                        in_=y_out[:, s, :], in_offset=None, compute_op=ALU.add
                                        ).then_inc(scattered, 16)
            gather(0, 2)
            with pool.Fori(0, n) as i:
                for s in range(2):
                    body(2 * i + s, s)
            for s in range(2):
                body(2 * n + s, s, ahead=False)
            pool.wait_ge(gathered[0], 16 * n + 32)
            pool.wait_ge(gathered[1], 16 * n + 16)
            pool.wait_ge(scattered, 32 * n + 64)
            pool.wait_ge(ln_in2, 32)
            for t in range(NT):
                pool.wait_ge(gained, t + 1)
                pool.tensor_tensor(rows2[:, t, :], rows2[:, t, :], b2, ALU.add).then_inc(row_done, 1)

        @block.tensor
        def _(pe):
            pe.wait_ge(e_in, EARLY_LOADS)
            for sm, v in CREDIT:
                pe.sem_inc(sm, v)

            def shared_up(t):
                s = t % 2
                if t >= 2:
                    pe.wait_ge(s_silu, t - 1)
                for k in range(KD):
                    ins = pe.matmul(bank[s][:, :], x1_t[:, k, t * P:(t + 1) * P], s_gu[:, k, :], start=k == 0, stop=k == KD - 1)
                ins.then_inc(s_gu_done, 1)

            def shared_turn(t):
                pe.wait_ge(s_h, t + 1)
                if t:
                    pe.wait_ge(s_ht_out, t)
                for j in range(2):
                    ins = pe.transpose(bank[4][:, j * P:(j + 1) * P], hidden[:, t % 2, j * P:(j + 1) * P], ident)
                ins.then_inc(s_ht, 1)

            def shared_down(t):
                if t:
                    pe.wait_ge(s_y, t)
                pe.wait_ge(s_ht_out, t + 1)
                for h in range(2):
                    for j in range(2):
                        ins = pe.matmul(bank[2 + h][:, :], hid_t[:, j, :], s_d[:, j, h * HALF:(h + 1) * HALF],
                                        start=j == 0, stop=j == 1)
                ins.then_inc(s_down, 1)

            def turn(blk, s, count):
                pe.wait_ge(gathered[s], count)
                if not isinstance(blk, int) or blk >= 1:
                    pe.wait_ge(xgt_ready, blk)
                for k in range(KD):
                    ins = pe.transpose(bank[4 + k // 4][:, (k % 4) * P:(k % 4 + 1) * P],
                                       x_g[:, s, :].rearrange('p (c k) -> p k c', k=KD)[:, k, :], ident)
                ins.then_inc(xt_done, 1)

            def up(blk, s, count):
                pe.wait_ge(w_gu_in[s], count)
                pe.wait_ge(xgt_ready, blk + 1)
                pe.wait_ge(h_ready, blk + 1)
                for k in range(KD):
                    ins = pe.matmul(bank[s][:, :].rearrange('p (m f) -> p m f', m=2), x_gt[:, s, k, :],
                                    w_gu[:, s, :, k, :], start=k == 0, stop=k == KD - 1)
                ins.then_inc(gu_done, 1)

            def find(blk, s):
                e = expert_of(pe, blk)
                if isinstance(blk, int):
                    pe.wait_ge(route_ready, 1)
                pe.wait_ge(oh_ready, blk + 1)
                if not isinstance(blk, int) or blk >= 1:
                    pe.wait_ge(idx_ready, blk)
                for t in range(NT):
                    ins = pe.matmul(bank[7][:, 8 * s:8 * s + 6], one_hot[:, s, t, :],
                                    info[:, t, bass.ds(e, 1), :].rearrange('p a b -> p (a b)'), start=t == 0, stop=t == NT - 1)
                ins.then_inc(idx_done, 1)

            for t in range(NT):
                shared_turn(t)
                if 2 <= t + 1 < NT:
                    shared_up(t + 1)
                if t == NT - 1:
                    pe.wait_ge(s_ht_out, NT)
                    turn(0, 0, 16)
                    find(2, 0)
                    pe.wait_ge(s_silu, NT - 1)
                    up(0, 0, 32)
                shared_down(t)
                if t == 1:
                    pe.wait_ge(mask_done, 1)
                    for n in range(NT):
                        o = bank[6][:, n * E:(n + 1) * E]
                        pe.matmul(o, const('before'), mask[:, n, :], start=True, stop=n == 0)
                        if n:
                            pe.matmul(o, const('ones'), run[:, n - 1, :], start=False, stop=True)
                    pe.matmul(bank[7][:, 0:E], const('ones'), run[:, NT - 1, :], start=True, stop=True).then_inc(pos_done, 1)
                if t == 2:
                    pe.wait_ge(ek_done, 1)
                    for i in range(2):
                        pe.matmul(bank[5][0:1, i * MAXB:(i + 1) * MAXB], ek[:, i:i + 1], ident, start=True, stop=True)
                    pe.matmul(bank[5][0:1, 2 * MAXB:2 * MAXB + 1], ek[:, 2:3], const('ones')[:, 0:1], start=True,
                              stop=True).then_inc(tab_done, 1)
                if t == 4:
                    n = trips(pe)
                    find(0, 0)
                    find(1, 1)
            pe.wait_ge(s_y, NT)

            def body(b, s, i, ahead1=True, ahead=True):
                pe.wait_ge(h_ready, b + 3)
                pe.wait_ge(ht_ready, b + 1)
                for j in range(2):
                    ins = pe.transpose(bank[6][:, j * P:(j + 1) * P],
                                       hidden[:, s, :].rearrange('p (c k) -> p k c', k=2)[:, j, :], ident)
                ins.then_inc(ht_done, 1)
                if ahead:
                    find(b + 3, 1 - s)
                if ahead1:
                    up(b + 1, 1 - s, 32 * i + 32 * (s + 1))
                if ahead:
                    turn(b + 2, s, 16 * i + 32)
                pe.wait_ge(w_d_in[s], 16 * i + 16)
                pe.wait_ge(ht_ready, b + 2)
                pe.wait_ge(y_act, b + 1)
                pe.wait_ge(y_dve, b + 1)
                for h in range(2):
                    for j in range(2):
                        ins = pe.matmul(bank[2 + h][:, :], hid_t[:, j, :], w_d[:, s, j, h * HALF:(h + 1) * HALF],
                                        start=j == 0, stop=j == 1)
                ins.then_inc(down_done, 1)
            turn(1, 1, 16)
            with pe.Fori(0, n) as i:
                for s in range(2):
                    body(2 * i + s, s, i)
            for s in range(2):
                body(2 * n + s, s, n, ahead1=s == 0, ahead=False)

        @block.scalar
        def _(act):
            def turned(blk, s):
                act.wait_ge(xt_done, blk + 2)
                act.wait_ge(gu_done, blk + 1)
                for h in range(2):
                    ins = act.activation(x_gt[:, s, 4 * h:4 * h + 4, :],
                                         bank[4 + h][:, :].rearrange('p (k c) -> p k c', k=4), ACT.Copy)
                ins.then_inc(xgt_ready, 1)

            def gated(blk, s):
                act.wait_ge(gu_done, blk + 3)
                act.wait_ge(h_ready, blk + 1)
                act.activation(silu[:, s, :], bank[s][:, 0:FE], ACT.Silu).then_inc(sg_ready, 1)

            def shared_gated(t):
                s = t % 2
                act.wait_ge(s_gu_done, t + 1)
                if t >= 2:
                    act.wait_ge(s_h, t - 1)
                act.activation(silu[:, s, :], bank[s][:, 0:FE], ACT.Silu)
                act.activation(u_sb[:, s, :], bank[s][:, FE:2 * FE], ACT.Copy).then_inc(s_silu, 1)
            shared_gated(0)
            for t in range(NT):
                s = t % 2
                act.wait_ge(s_ht, t + 1)
                if t:
                    act.wait_ge(s_down, t)
                act.activation(hid_t[:, :, :], bank[4][:, 0:2 * P].rearrange('p (j c) -> p j c', j=2), ACT.Copy
                               ).then_inc(s_ht_out, 1)
                if t + 1 < NT:
                    shared_gated(t + 1)
                else:
                    turned(0, 0)
                    gated(0, 0)
                if t == 0:
                    act.wait_ge(scattered, 32)
                if t >= 2:
                    act.wait_ge(acc_in[s], 16 * (t // 2))
                act.activation(s_row[:, s, :], x1_n[:, t, :], ACT.Copy, scale=ALPHA)
                act.wait_ge(s_down, t + 1)
                for h in range(2):
                    ins = act.activation(s_acc[:, s, h * HALF:(h + 1) * HALF], bank[2 + h][:, :], ACT.Copy)
                ins.then_inc(s_y, 1)
            n = trips(act)

            def body(b, s, ahead1=True, ahead=True):
                act.wait_ge(ht_done, b + 3)
                act.wait_ge(down_done, b + 2)
                act.activation(hid_t[:, :, :], bank[6][:, 0:2 * P].rearrange('p (j c) -> p j c', j=2), ACT.Copy
                               ).then_inc(ht_ready, 1)
                if ahead1:
                    gated(b + 1, 1 - s)
                if ahead:
                    turned(b + 2, s)
                act.wait_ge(down_done, b + 3)
                act.wait_ge(scattered, 16 * b + 16)
                act.activation(y_out[:, s, 0:HALF], bank[2][:, :], ACT.Copy).then_inc(y_act, 1)
            turned(1, 1)
            with act.Fori(0, n) as i:
                for s in range(2):
                    body(2 * i + s, s)
            for s in range(2):
                body(2 * n + s, s, ahead1=s == 0, ahead=False)
            act.wait_ge(eps_set2, 1)
            for t in range(NT + 1):
                if t < NT:
                    act.wait_ge(mv_done2, t + 1)
                    act.activation(sd[:, t % 2:t % 2 + 1], mv[:, t % 2, 1:2], ACT.Sqrt, bias=eps[:, 0:1]
                                   ).then_inc(sd_done2, 1)
                if t:
                    act.wait_ge(scale_done, t)
                    act.activation(rows2[:, t - 1, :], rows2[:, t - 1, :], ACT.Identity, scale=scale[:, t - 1:t],
                                   bias=shift[:, t - 1:t]).then_inc(normed, 1)

        @block.vector
        def _(dve):
            order = Order(dve, d_order)
            X = order.after
            dve.memset(eps[:, :], EPS).then_inc(eps_set2, 1)
            dve.wait_ge(e_in, EARLY_LOADS)
            X(dve.tensor_tensor(biased, scores[:, :, :], bcast(rb[:, :], 1, NT), ALU.add))
            for n in range(NT):
                for g in range(NG):
                    ins = dve.max(t8[:, n, g, :], biased[:, n, g * EG:(g + 1) * EG])
            X(ins)
            X(dve.tensor_tensor(gs[:, :, :], t8[:, :, :, 0], t8[:, :, :, 1], ALU.add))
            other, own = bcast(gs[:, :, :], 2, NG), bcast(gs[:, :, :], 3, NG)
            X(dve.tensor_tensor(t_gt, other, own, ALU.is_gt))
            X(dve.tensor_tensor(t_ge, other, own, ALU.is_ge))
            X(dve.tensor_tensor(t_ge, t_ge, t_gt, ALU.subtract))
            X(dve.tensor_tensor(t_ge.rearrange('p n g h -> p n (g h)'), t_ge.rearrange('p n g h -> p n (g h)'),
                                bcast(const('lower'), 1, NT), ALU.mult))
            X(dve.tensor_tensor(t_gt, t_gt, t_ge, ALU.add))
            X(dve.reduce_sum(keep[:, :, :], t_gt, AX.X))
            X(dve.tensor_scalar(keep[:, :, :], keep[:, :, :], float(TOPG), None, ALU.is_lt))
            for n in range(NT):
                ins = dve.tensor_tensor(cand[:, n, 0:E].rearrange('p (g h) -> p g h', g=NG),
                                        biased[:, n, :].rearrange('p (g h) -> p g h', g=NG), bcast(keep[:, n, :], 2, EG),
                                        ALU.mult)
            dve.memset(cand[:, :, E:E + 2], 1e30)
            X(dve.tensor_scalar(gs[:, :, :], keep[:, :, :], 1e30, -1e30, ALU.mult, ALU.add))
            for n in range(NT):
                ins = dve.tensor_tensor(cand[:, n, 0:E].rearrange('p (g h) -> p g h', g=NG),
                                        cand[:, n, 0:E].rearrange('p (g h) -> p g h', g=NG), bcast(gs[:, n, :], 2, EG),
                                        ALU.add)
            X(ins)
            for n in range(NT):
                ins = dve.max(top[:, n, :], cand[:, n, 0:E])
            X(ins)
            X(dve.memset(top[:, :, TOPK:8], 1e30))
            for n in range(NT):
                ins = dve.match_replace(cut[:, n, :], top[:, n, :], cand[:, n, :], -3e38)
            X(ins)
            X(dve.tensor_scalar(mask, cut[:, :, 0:E], -3e38, None, ALU.is_equal))
            X(dve.tensor_copy(run[:, 0, :], mask[:, 0, :]))
            for n in range(1, NT):
                ins = dve.tensor_tensor(run[:, n, :], run[:, n - 1, :], mask[:, n, :], ALU.add)
                if n < NT - 1:
                    X(ins)
            ins.then_inc(mask_done, 1)
            X(dve.tensor_tensor(gate_w, scores[:, :, :], mask, ALU.mult))
            X(dve.reduce_sum(g_sum[:, :], gate_w, AX.X))
            X(dve.reciprocal(g_sum[:, :], g_sum[:, :]))
            X(dve.tensor_tensor(gate_w, gate_w, bcast(g_sum[:, :], 2, E), ALU.mult))
            X(dve.tensor_scalar(gate_w, gate_w, ROUTE, None, ALU.mult))
            for part in (3, 4, 5):
                X(dve.tensor_copy(info[:, :, :, part], gate_w))
                if part < 5:
                    X(dve.tensor_tensor(gate_w, gate_w, info[:, :, :, part], ALU.subtract))
            dve.tensor_copy(info[:, :, :, 0], bcast(const('tile_tok'), 2, E))
            dve.tensor_copy(info[:, :, :, 1], bcast(const('row').broadcast_to([P, NT]), 2, E))
            dve.memset(info[:, :, :, 2], 1.0)
            dve.wait_ge(pos_done, 1)
            X(dve.tensor_scalar(pos[:, :, :], bank[6][:, :].rearrange('p (n e) -> p n e', n=NT), 4096.0, None, ALU.add))
            X(dve.tensor_tensor(pos[:, :, :], pos[:, :, :], mask, ALU.mult))
            dve.tensor_scalar(pos[:, :, :], pos[:, :, :], -4096.0, None, ALU.add)
            c8 = cmp8.rearrange('p n g h -> p (n g) h')
            X(dve.tensor_copy(le[:, :], bank[7][:, 0:E]))
            X(dve.tensor_tensor(c8, bcast(le[:, :], 2, 8), bcast(const('steps'), 1, E), ALU.is_gt))
            X(dve.reduce_sum(n_blk[:, :], c8, AX.X))
            X(dve.memset(end_blk[:, :], 1.0))
            X(dve.tensor_tensor_scan(le[:, :], end_blk[:, :], n_blk[:, :], 0.0, ALU.mult, ALU.add))
            X(dve.tensor_scalar(end_blk[:, :], le[:, :], const('row'), None, ALU.is_le))
            X(dve.reduce_sum(ek[:, 0:1], end_blk[:, :], AX.X))
            X(dve.tensor_tensor(end_blk[:, :], end_blk[:, :], n_blk[:, :], ALU.mult))
            X(dve.reduce_sum(ek[:, 1:2], end_blk[:, :], AX.X))
            X(dve.tensor_scalar(ek[:, 3:4], ek[:, 0:1], float(E), 8.0, ALU.is_ge, ALU.mult))
            X(dve.tensor_tensor(ek[:, 1:2], const('row'), ek[:, 1:2], ALU.subtract))
            X(dve.tensor_scalar(ek[:, 1:2], ek[:, 1:2], ek[:, 3:4], 8.0, ALU.max, ALU.min))
            X(dve.tensor_scalar(ek[:, 1:2], ek[:, 1:2], float(P), None, ALU.mult))
            X(dve.tensor_scalar(ek[:, 2:3], ek[:, 3:4], 8.0, const('even'), ALU.is_lt, ALU.mult))
            dve.tensor_scalar(ek[:, 0:1], ek[:, 0:1], float(E - 1), None, ALU.min).then_inc(ek_done, 1)
            dve.wait_ge(tab_done, 1)
            dve.tensor_copy(table[:, :], bank[5][0:1, 0:2 * MAXB + 1]).then_inc(tab_ready, 1)
            n = trips(dve)
            dve.nop().then_inc(route_ready, 1)

            def one_hots(blk, s):
                e = expert_of(dve, blk)
                first = dve.value_load(table[0:1, bass.ds(blk + MAXB, 1)], min_val=0, max_val=NT * P)
                ranks = const('rank')[:, bass.ds(first, P)]
                if not isinstance(blk, int) or blk >= 2:
                    dve.wait_ge(idx_done, blk - 1)
                dve.tensor_tensor(one_hot[:, s, :, :], bcast(ranks, 1, NT),
                                  pos[:, :, bass.ds(e, 1)].broadcast_to([P, NT, P]), ALU.is_equal).then_inc(oh_ready, 1)

            def keep_rows(s):
                dve.tensor_copy(row_gate[:, 2 + s:3 + s], row_gate[:, s:s + 1])
                return dve.tensor_copy(idx_kept[:, s:s + 1], idx[:, s:s + 1])

            def rows(blk, s):
                dve.wait_ge(idx_done, blk + 1)
                if not isinstance(blk, int) or blk >= 2:
                    dve.wait_ge(xt_done, blk)
                    keep_rows(s)
                wait_f(dve.tensor_copy(found[:, s, :], bank[7][:, 8 * s:8 * s + 6]), blk, 1)
                wait_f(dve.scalar_tensor_tensor(idx_f[:, :], found[:, s, 2:3], const('neg_row'), found[:, s, 0:1],
                                                ALU.mult, ALU.add), blk, 2)
                dve.reduce_sum(row_gate[:, s:s + 1], found[:, s, 3:6], AX.X)
                dve.tensor_scalar(idx[:, s:s + 1], idx_f[:, :], found[:, s, 1:2], const('row_dummy'), ALU.add, ALU.add
                                  ).then_inc(idx_ready, 1)

            def wait_f(ins, blk, k):
                ins.then_inc(f_order, 1)
                dve.wait_ge(f_order, 2 * blk + k)

            def hide(blk, s):
                dve.wait_ge(sg_ready, blk + 1)
                dve.wait_ge(ht_done, blk + 1)
                dve.wait_ge(idx_ready, blk + 3)
                dve.scalar_tensor_tensor(hidden[:, s, :], bank[s][:, FE:2 * FE], row_gate[:, 2 + s:3 + s], silu[:, s, :],
                                         ALU.mult, ALU.mult).then_inc(h_ready, 1)
                dve.wait_ge(scattered, 16 * blk + 16)
                dve.tensor_copy(idx_out[:, s:s + 1], idx_kept[:, s:s + 1]).then_inc(so_ready, 1)

            def body(b, s, ahead1=True, ahead=True):
                if ahead:
                    rows(b + 3, 1 - s)
                elif ahead1:
                    keep_rows(1 - s).then_inc(idx_ready, 1)
                if ahead1:
                    hide(b + 1, 1 - s)
                if ahead:
                    one_hots(b + 4, s)
                dve.wait_ge(down_done, b + 3)
                dve.wait_ge(scattered, 16 * b + 16)
                dve.tensor_copy(y_out[:, s, HALF:D], bank[3][:, :]).then_inc(y_dve, 1)
            one_hots(0, 0)
            one_hots(1, 1)
            rows(0, 0)
            rows(1, 1)
            one_hots(2, 0)
            rows(2, 0)
            hide(0, 0)
            one_hots(3, 1)
            with dve.Fori(0, n) as i:
                for s in range(2):
                    body(2 * i + s, s)
            for s in range(2):
                body(2 * n + s, s, ahead1=s == 0, ahead=False)
            dve.wait_ge(ln_in2, 32)

            def scales(t):
                s = t % 2
                dve.wait_ge(sd_done2, t + 1)
                X(dve.reciprocal(sd[:, s:s + 1], sd[:, s:s + 1]))
                dve.scalar_tensor_tensor(shift[:, t:t + 1], mv[:, s, 0:1], -1.0, sd[:, s:s + 1], ALU.mult, ALU.mult)
                dve.tensor_copy(scale[:, t:t + 1], sd[:, s:s + 1]).then_inc(scale_done, 1)

            def gain(t):
                dve.wait_ge(normed, t + 1)
                dve.tensor_tensor(rows2[:, t, :], rows2[:, t, :], g2, ALU.mult).then_inc(gained, 1)
            for t in range(NT):
                s = t % 2
                dve.wait_ge(acc_row_in[t], 32)
                for h in range(2):
                    ins = dve.bn_stats(stats[:, s, h, :], rows2[:, t, h * HALF:(h + 1) * HALF])
                X(ins)
                dve.bn_aggr(mv[:, s, :], stats[:, s, :, :]).then_inc(mv_done2, 1)
                if t:
                    scales(t - 1)
                if t >= 2:
                    gain(t - 2)
            scales(NT - 1)
            gain(NT - 2)
            gain(NT - 1)


def program(nc, d, consts, c_at, consts_moe, e_at, out):
    yt = nc.dram_tensor('yt', (10, P, S), F32, kind='Internal').ap()
    gates = nc.dram_tensor('gates', (KD, 4, P, S), F32, kind='Internal').ap()
    x1d = nc.dram_tensor('x1d', (S + P, D), F32, kind='Internal').ap()
    acc = nc.dram_tensor('acc', (S + P, D), F32, kind='Internal').ap()
    with ExitStack() as ctx:
        def sem(name):
            return ctx.enter_context(nc.semaphore(name))
        d = dict(d, ident=consts_moe[:, e_at['ident'][0]:e_at['ident'][0] + P])
        mixers(nc, d, consts, c_at, yt, gates, sem)
        work = [ctx.enter_context(nc.sbuf_tensor(f'work{i}', [P, KD * S], F32))[:, :] for i in range(2)]
        merged, w_out = (w.rearrange('p (k s) -> p k s', k=KD) for w in work)
        y_done, half_merged, wo_in, piece_in = sem('y_done'), sem('half_merged'), sem('wo_in'), [sem(f'piece_in{i}') for i in range(8)]
        merge(nc, d, yt, gates, merged, w_out, y_done, half_merged, wo_in, piece_in, sem)
        x1 = ctx.enter_context(nc.sbuf_tensor('x1', [P, 2 * KD * S + 2048], F32))
        x1_n = x1[:, 0:NT * D].rearrange('p (n d) -> p n d', d=D)
        x1_t = x1[:, NT * D:2 * NT * D].rearrange('p (k s) -> p k s', s=S)
        scores = ctx.enter_context(nc.sbuf_tensor('scores', [P, NT, E], F32))
        early = [ctx.enter_context(nc.sbuf_tensor(name, shape, F32)) for name, shape in (
            ('e_const', [P, consts_moe.shape[1]]), ('rb', [P, E]), ('sh', [P, 6144]))]
        early += [sem('early_in'), sem('s_gu_done'),
                  [ctx.enter_context(nc.psum_tensor(f'e_bank{i}', [P, HALF], F32)) for i in range(8)], piece_in]
        project(nc, d, merged, w_out, half_merged, wo_in, consts_moe, early, x1d, x1_n, x1_t, scores, sem)
        experts(nc, d, e_at, early, work[0], work[1], x1d, acc, x1_n, x1_t, scores, x1, out, sem)


def kernel(**inputs):
    import concourse.bacc as bacc
    from concourse.bass_utils import run_bass_kernel_spmd

    nc = bacc.Bacc('TRN2', target_bir_lowering=False, num_devices=1)
    (c_tab, c_at), (e_tab, e_at) = packed(constants()), packed(constants_moe())
    arrays = {f'in_{k}': np.ascontiguousarray(inputs[k]) for k in IN_NAMES}
    arrays['in_tables'], arrays['in_tables_moe'] = c_tab, e_tab
    aps = {k: nc.dram_tensor(k, v.shape, mybir.dt.from_np(v.dtype), kind='ExternalInput').ap() for k, v in arrays.items()}
    out = nc.dram_tensor('out_0', (1, S, D), F32, kind='ExternalOutput').ap()
    program(nc, {k: aps[f'in_{k}'] for k in IN_NAMES}, aps['in_tables'], c_at, aps['in_tables_moe'], e_at, out)
    got = run_bass_kernel_spmd(nc, [arrays], core_ids=[0])
    return got.results[0]['out_0']
```
